# Optimizing a Trainium2 kernel written in Bass

```python
import functools
import jax, jax.numpy as jnp
from jax import lax
import numpy as np

D_MODEL = 1024
BATCH = 1
SEQ = 1024
DEPTH = 2
DEC_BATCH = 1
DEC_SEQ = 64
PAST_LEN = 256

CHUNK = 64
QBLOCK = 128
ROPE_THETA = 500000.0
EPS = 1e-6
HEAD_DIM = 64
ROT_DIM = HEAD_DIM // 4
A_HEADS = 8
A_KV_HEADS = 2
IDX_HEADS = 8
IDX_DIM = 32
IDX_ROT = IDX_DIM // 4
TOPK_MAX = 256
B_HEADS = 8
Q_RANK = 256
KV_RANK = 128
B_NOPE = 64
B_ROPE = 32
B_VDIM = 64
C_HEADS = 8
D_HEADS = 8
D_FF = 2816
CONV_W = 3

N_EVEN = (DEPTH + 1) // 2
N_ODD = DEPTH // 2
EVEN_SPLIT = [A_HEADS * HEAD_DIM, A_KV_HEADS * HEAD_DIM, A_KV_HEADS * HEAD_DIM,
              IDX_HEADS * IDX_DIM, IDX_DIM, IDX_HEADS, Q_RANK, KV_RANK, B_ROPE]
ODD_SPLIT = [C_HEADS * HEAD_DIM] * 3 + [C_HEADS] + [D_HEADS * HEAD_DIM] * 3
EVEN_IN = sum(EVEN_SPLIT)
ODD_IN = sum(ODD_SPLIT)
EVEN_MIX = A_HEADS * HEAD_DIM + B_HEADS * B_VDIM
ODD_MIX = (C_HEADS + D_HEADS) * HEAD_DIM

kernel_name = 'hybrid_dsa_mla_fox_stickbreak_convffn_step'

def rmsnorm(x, g):
    xf = x.astype(jnp.float32)
    y = xf * lax.rsqrt(jnp.mean(xf * xf, axis=-1, keepdims=True) + EPS)
    return (y * g.astype(jnp.float32)).astype(x.dtype)

def rope(x, pos, n_rot):
    half = n_rot // 2
    inv = ROPE_THETA ** (-jnp.arange(half, dtype=jnp.float32) * 2.0 / n_rot)
    ang = pos.astype(jnp.float32)[:, None] * inv[None, :]
    shape = (ang.shape[0],) + (1,) * (x.ndim - 3) + (half,)
    cos = jnp.cos(ang).reshape(shape).astype(x.dtype)
    sin = jnp.sin(ang).reshape(shape).astype(x.dtype)
    x1 = x[..., :half]
    x2 = x[..., half:n_rot]
    return jnp.concatenate([x1 * cos - x2 * sin, x1 * sin + x2 * cos, x[..., n_rot:]], axis=-1)

def chunk_mask(q_pos, k_pos):
    return (k_pos[None, :] // CHUNK) <= (q_pos[:, None] // CHUNK)

def run_queries(fn, q_arrays, q_pos, blocked):
    if not blocked:
        return fn(*q_arrays, q_pos)
    n_blk = q_pos.shape[0] // QBLOCK

    def split(a):
        return jnp.moveaxis(a.reshape((a.shape[0], n_blk, QBLOCK) + a.shape[2:]), 1, 0)

    blocks = tuple(split(a) for a in q_arrays)
    out = lax.map(lambda args: fn(*args[0], args[1]), (blocks, q_pos.reshape(n_blk, QBLOCK)))
    out = jnp.moveaxis(out, 0, 1)
    return out.reshape((out.shape[0], n_blk * QBLOCK) + out.shape[3:])

def dsa_core(k, v, ki, k_pos, topk, q, qi, wi, q_pos):
    sc = jnp.einsum('bqhd,bsd->bqhs', qi, ki).astype(jnp.float32)
    idx_score = jnp.einsum('bqhs,bqh->bqs', jax.nn.relu(sc), wi.astype(jnp.float32))
    idx_score = jnp.where(chunk_mask(q_pos, k_pos)[None], idx_score, -jnp.inf)
    _, sel = lax.top_k(idx_score, topk)
    valid = (k_pos[sel] // CHUNK) <= (q_pos // CHUNK)[None, :, None]
    gather = jax.vmap(lambda a, i: a[i])
    kg = gather(k, sel)
    vg = gather(v, sel)
    b_, q_ = q.shape[0], q.shape[1]
    qg = q.reshape(b_, q_, A_KV_HEADS, A_HEADS // A_KV_HEADS, HEAD_DIM)
    logits = jnp.einsum('bqgrd,bqkgd->bqgrk', qg, kg).astype(jnp.float32) * HEAD_DIM ** -0.5
    logits = jnp.where(valid[:, :, None, None, :], logits, -jnp.inf)
    p = jax.nn.softmax(logits, axis=-1).astype(v.dtype)
    out = jnp.einsum('bqgrk,bqkgd->bqgrd', p, vg)
    return out.reshape(b_, q_, A_HEADS * HEAD_DIM)

def mla_core(k_nope, k_rope, v, k_pos, q_nope, q_rope, q_pos):
    logits = (jnp.einsum('bqhd,bshd->bhqs', q_nope, k_nope)
              + jnp.einsum('bqhd,bsd->bhqs', q_rope, k_rope)).astype(jnp.float32)
    logits = logits * (B_NOPE + B_ROPE) ** -0.5
    logits = jnp.where(chunk_mask(q_pos, k_pos)[None, None], logits, -jnp.inf)
    p = jax.nn.softmax(logits, axis=-1).astype(v.dtype)
    out = jnp.einsum('bhqs,bshd->bqhd', p, v)
    return out.reshape(out.shape[0], out.shape[1], B_HEADS * B_VDIM)

def fox_core(k, v, ck, k_pos, q, cq, q_pos):
    logits = jnp.einsum('bqhd,bshd->bhqs', q, k).astype(jnp.float32) * HEAD_DIM ** -0.5
    logits = logits + jnp.transpose(cq, (0, 2, 1))[..., None] - jnp.transpose(ck, (0, 2, 1))[:, :, None, :]
    mask = k_pos[None, :] <= q_pos[:, None]
    logits = jnp.where(mask[None, None], logits, -jnp.inf)
    p = jax.nn.softmax(logits, axis=-1).astype(v.dtype)
    out = jnp.einsum('bhqs,bshd->bqhd', p, v)
    return out.reshape(out.shape[0], out.shape[1], C_HEADS * HEAD_DIM)

def sb_core(k, v, k_pos, q, q_pos):
    z = jnp.einsum('bqhd,bshd->bhqs', q, k).astype(jnp.float32) * HEAD_DIM ** -0.5
    mask = (k_pos[None, :] < q_pos[:, None])[None, None]
    log_beta = jax.nn.log_sigmoid(z)
    log_1m = jnp.where(mask, jax.nn.log_sigmoid(-z), 0.0)
    after = lax.cumsum(log_1m, axis=3, reverse=True) - log_1m
    a = jnp.where(mask, jnp.exp(log_beta + after), 0.0).astype(v.dtype)
    out = jnp.einsum('bhqs,bshd->bqhd', a, v)
    return out.reshape(out.shape[0], out.shape[1], D_HEADS * HEAD_DIM)

def even_mixer(h, q_pos, past, w_in, g_bq, g_bkv, w_uq, w_ukv, w_o):
    bsz, s_len, _ = h.shape
    cuts = np.cumsum(EVEN_SPLIT)[:-1].tolist()
    qa, ka, va, qi, ki, wi, cq, ckv, kr = jnp.split(h @ w_in, cuts, axis=-1)
    qa = rope(qa.reshape(bsz, s_len, A_HEADS, HEAD_DIM), q_pos, ROT_DIM)
    ka = rope(ka.reshape(bsz, s_len, A_KV_HEADS, HEAD_DIM), q_pos, ROT_DIM)
    va = va.reshape(bsz, s_len, A_KV_HEADS, HEAD_DIM)
    qi = rope(qi.reshape(bsz, s_len, IDX_HEADS, IDX_DIM), q_pos, IDX_ROT) * IDX_DIM ** -0.5
    ki = rope(ki, q_pos, IDX_ROT)
    wi = wi * IDX_HEADS ** -0.5
    qb = (rmsnorm(cq, g_bq) @ w_uq).reshape(bsz, s_len, B_HEADS, B_NOPE + B_ROPE)
    qn = qb[..., :B_NOPE]
    qr = rope(qb[..., B_NOPE:], q_pos, B_ROPE)
    lat = rmsnorm(ckv, g_bkv)
    kr = rope(kr, q_pos, B_ROPE)
    new_rows = (ka, va, ki, lat, kr)
    if past is None:
        keys = new_rows
        k_pos = q_pos
    else:
        keys = tuple(jnp.concatenate([p_, n_], axis=1) for p_, n_ in zip(past, new_rows))
        k_pos = jnp.arange(keys[0].shape[1], dtype=jnp.int32)
    k_a, v_a, k_i, lat_all, kr_all = keys
    n_keys = k_a.shape[1]
    kv = (lat_all @ w_ukv).reshape(bsz, n_keys, B_HEADS, B_NOPE + B_VDIM)
    kn, vb = kv[..., :B_NOPE], kv[..., B_NOPE:]
    topk = min(TOPK_MAX, n_keys // 4)
    blocked = past is None
    out_a = run_queries(functools.partial(dsa_core, k_a, v_a, k_i, k_pos, topk), (qa, qi, wi), q_pos, blocked)
    out_b = run_queries(functools.partial(mla_core, kn, kr_all, vb, k_pos), (qn, qr), q_pos, blocked)
    return jnp.concatenate([out_a, out_b], axis=-1) @ w_o, new_rows

def odd_mixer(h, q_pos, past, w_in, b_f, w_o):
    bsz, s_len, _ = h.shape
    cuts = np.cumsum(ODD_SPLIT)[:-1].tolist()
    qc, kc, vc, fc, qd, kd, vd = jnp.split(h @ w_in, cuts, axis=-1)
    heads = lambda a, n: a.reshape(bsz, s_len, n, HEAD_DIM)
    qc, kc, vc = heads(qc, C_HEADS), heads(kc, C_HEADS), heads(vc, C_HEADS)
    qd, kd, vd = heads(qd, D_HEADS), heads(kd, D_HEADS), heads(vd, D_HEADS)
    logf = jax.nn.log_sigmoid((fc + b_f).astype(jnp.float32))
    new_rows = (kc, vc, logf, kd, vd)
    if past is None:
        keys = new_rows
        k_pos = q_pos
    else:
        keys = tuple(jnp.concatenate([p_, n_], axis=1) for p_, n_ in zip(past, new_rows))
        k_pos = jnp.arange(keys[0].shape[1], dtype=jnp.int32)
    k_c, v_c, logf_all, k_d, v_d = keys
    c_all = jnp.cumsum(logf_all.astype(jnp.float32), axis=1)
    c_q = c_all[:, c_all.shape[1] - s_len:]
    blocked = past is None
    out_c = run_queries(functools.partial(fox_core, k_c, v_c, c_all, k_pos), (qc, c_q), q_pos, blocked)
    out_d = run_queries(functools.partial(sb_core, k_d, v_d, k_pos), (qd,), q_pos, blocked)
    return jnp.concatenate([out_c, out_d], axis=-1) @ w_o, new_rows

def conv_ffn(h, buf, w_up, w_conv, b_conv, w_down):
    gate, up = jnp.split(h @ w_up, 2, axis=-1)
    s_len = h.shape[1]
    if buf is None:
        buf = jnp.zeros((h.shape[0], CONV_W - 1, D_FF), gate.dtype)
    ext = jnp.concatenate([buf.astype(gate.dtype), gate], axis=1)
    gc = b_conv + ext[:, 0:s_len] * w_conv[0]
    for i in range(1, CONV_W):
        gc = gc + ext[:, i:i + s_len] * w_conv[i]
    y = (jax.nn.silu(gc) * up) @ w_down
    return y, ext[:, ext.shape[1] - (CONV_W - 1):]

def trunk(x, q_pos, caches, params):
    (g_mix, g_ffn, g_final, w_in_even, g_b_q, g_b_kv, w_b_uq, w_b_ukv, w_o_even,
     w_in_odd, b_forget, w_o_odd, w_up, w_conv, b_conv, w_down) = params
    even_rows = [[] for _ in range(5)]
    odd_rows = [[] for _ in range(5)]
    conv_rows = []
    for l in range(DEPTH):
        h = rmsnorm(x, g_mix[l])
        j = l // 2
        if l % 2 == 0:
            past = None if caches is None else tuple(c[j] for c in caches[0:5])
            y, rows = even_mixer(h, q_pos, past, w_in_even[j], g_b_q[j], g_b_kv[j], w_b_uq[j], w_b_ukv[j], w_o_even[j])
            for lst, r in zip(even_rows, rows):
                lst.append(r)
        else:
            past = None if caches is None else tuple(c[j] for c in caches[5:10])
            y, rows = odd_mixer(h, q_pos, past, w_in_odd[j], b_forget[j], w_o_odd[j])
            for lst, r in zip(odd_rows, rows):
                lst.append(r)
        x = x + y
        buf = None if caches is None else caches[10][l]
        y, new_buf = conv_ffn(rmsnorm(x, g_ffn[l]), buf, w_up[l], w_conv[l], b_conv[l], w_down[l])
        conv_rows.append(new_buf)
        x = x + y
    out = rmsnorm(x, g_final)
    states = [jnp.stack(r, axis=0) for r in even_rows + odd_rows] + [jnp.stack(conv_rows, axis=0)]
    return out, states

def setup_inputs(seed: int = 0) -> dict:
    key = jax.random.key(seed)
    ks = iter(jax.random.split(key, 40))

    def nrm(shape, scale=1.0):
        return jax.random.normal(next(ks), shape, jnp.float32) * scale

    db, pl = DEC_BATCH, PAST_LEN
    return {
        'x_prompt': nrm((BATCH, SEQ, D_MODEL)),
        'x_sample': nrm((DEC_BATCH, DEC_SEQ, D_MODEL)),
        'cache_a_k': nrm((N_EVEN, db, pl, A_KV_HEADS, HEAD_DIM)),
        'cache_a_v': nrm((N_EVEN, db, pl, A_KV_HEADS, HEAD_DIM)),
        'cache_a_idx_k': nrm((N_EVEN, db, pl, IDX_DIM)),
        'cache_b_latent': nrm((N_EVEN, db, pl, KV_RANK)),
        'cache_b_rope': nrm((N_EVEN, db, pl, B_ROPE)),
        'cache_c_k': nrm((N_ODD, db, pl, C_HEADS, HEAD_DIM)),
        'cache_c_v': nrm((N_ODD, db, pl, C_HEADS, HEAD_DIM)),
        'cache_c_logf': jax.nn.log_sigmoid(nrm((N_ODD, db, pl, C_HEADS))),
        'cache_d_k': nrm((N_ODD, db, pl, D_HEADS, HEAD_DIM)),
        'cache_d_v': nrm((N_ODD, db, pl, D_HEADS, HEAD_DIM)),
        'state_ffn_conv': nrm((DEPTH, db, CONV_W - 1, D_FF)),
        'g_mix': 1.0 + nrm((DEPTH, D_MODEL), 0.01),
        'g_ffn': 1.0 + nrm((DEPTH, D_MODEL), 0.01),
        'g_final': 1.0 + nrm((D_MODEL,), 0.01),
        'w_in_even': nrm((N_EVEN, D_MODEL, EVEN_IN), D_MODEL ** -0.5),
        'g_b_q': 1.0 + nrm((N_EVEN, Q_RANK), 0.01),
        'g_b_kv': 1.0 + nrm((N_EVEN, KV_RANK), 0.01),
        'w_b_uq': nrm((N_EVEN, Q_RANK, B_HEADS * (B_NOPE + B_ROPE)), Q_RANK ** -0.5),
        'w_b_ukv': nrm((N_EVEN, KV_RANK, B_HEADS * (B_NOPE + B_VDIM)), KV_RANK ** -0.5),
        'w_o_even': nrm((N_EVEN, EVEN_MIX, D_MODEL), EVEN_MIX ** -0.5),
        'w_in_odd': nrm((N_ODD, D_MODEL, ODD_IN), D_MODEL ** -0.5),
        'b_forget': nrm((N_ODD, C_HEADS), 0.1),
        'w_o_odd': nrm((N_ODD, ODD_MIX, D_MODEL), ODD_MIX ** -0.5),
        'w_up': nrm((DEPTH, D_MODEL, 2 * D_FF), D_MODEL ** -0.5),
        'w_conv': nrm((DEPTH, CONV_W, D_FF), CONV_W ** -0.5),
        'b_conv': nrm((DEPTH, D_FF), 0.01),
        'w_down': nrm((DEPTH, D_FF, D_MODEL), D_FF ** -0.5),
    }

def reference(x_prompt, x_sample, cache_a_k, cache_a_v, cache_a_idx_k, cache_b_latent, cache_b_rope,
              cache_c_k, cache_c_v, cache_c_logf, cache_d_k, cache_d_v, state_ffn_conv,
              g_mix, g_ffn, g_final, w_in_even, g_b_q, g_b_kv, w_b_uq, w_b_ukv, w_o_even,
              w_in_odd, b_forget, w_o_odd, w_up, w_conv, b_conv, w_down):
    params = (g_mix, g_ffn, g_final, w_in_even, g_b_q, g_b_kv, w_b_uq, w_b_ukv, w_o_even,
              w_in_odd, b_forget, w_o_odd, w_up, w_conv, b_conv, w_down)
    caches = (cache_a_k, cache_a_v, cache_a_idx_k, cache_b_latent, cache_b_rope,
              cache_c_k, cache_c_v, cache_c_logf, cache_d_k, cache_d_v, state_ffn_conv)
    past_len = cache_a_k.shape[2]
    pos_prompt = jnp.arange(x_prompt.shape[1], dtype=jnp.int32)
    pos_sample = past_len + jnp.arange(x_sample.shape[1], dtype=jnp.int32)
    y_prompt, p_states = trunk(x_prompt, pos_prompt, None, params)
    (p_a_k, p_a_v, p_a_idx_k, p_b_latent, p_b_rope,
     p_c_k, p_c_v, p_c_logf, p_d_k, p_d_v, p_conv) = p_states
    y_sample, s_states = trunk(x_sample, pos_sample, caches, params)
    (s_a_k, s_a_v, s_a_idx_k, s_b_latent, s_b_rope,
     s_c_k, s_c_v, s_c_logf, s_d_k, s_d_v, s_conv) = s_states
    return (y_prompt, y_sample,
            p_a_k, p_a_v, p_a_idx_k, p_b_latent, p_b_rope, p_c_k, p_c_v, p_c_logf, p_d_k, p_d_v, p_conv,
            s_a_k, s_a_v, s_a_idx_k, s_b_latent, s_b_rope, s_c_k, s_c_v, s_c_logf, s_d_k, s_d_v, s_conv)


_drawn_inputs = setup_inputs


def setup_inputs(seed=0):
    import zlib

    import numpy as np

    out = dict(_drawn_inputs(seed))
    spreads = {}
    factors = {'cache_c_logf': 39.496,
     'g_mix': 2.993,
     'g_ffn': 4.795,
     'g_final': 32.647,
     'g_b_q': 8.0,
     'g_b_kv': 5.949,
     'b_conv': 7.971,
     'cache_c_k': 8.0,
     'cache_c_v': 8.0,
     'cache_d_k': 7.626,
     'cache_d_v': 6.272}
    for name, (base, spread) in spreads.items():
        noise = np.random.default_rng([zlib.crc32(name.encode()), seed]).standard_normal(out[name].shape)
        drawn = base * np.exp(spread * noise) if base else spread * noise
        out[name] = __import__('jax').numpy.asarray(drawn.astype(out[name].dtype))
    for name, factor in factors.items():
        out[name] = (out[name] * factor).astype(out[name].dtype)
    return out
```

```python
from contextlib import ExitStack

import concourse.bass as bass
from concourse import mybir

F32 = mybir.dt.float32
F32R = mybir.dt.float32r
BF16 = mybir.dt.bfloat16
ALU = mybir.AluOpType
ACT = mybir.ActivationFunctionType
AX_X = mybir.AxisListType.X
ds = bass.ds

P = 128
D = 1024
KD = D // P
SEQ, DEC, PAST = 1024, 64, 256
NT = SEQ // P
TOK = SEQ + DEC
KEYS = SEQ + PAST + DEC
OWN = SEQ + PAST
KT = NT + PAST // P + 1
EPS = 1e-6
HD = 64
A_IN, C_IN, D_IN = 1480, 1544, 1536
TOPK_P, TOPK_S = 256, 80
QR, KVR = 256, 128
FF = 2816
NF = FF // P
NEG = -1.0e30
GONE = -3.4e38
ROPE_COLS = 2 * (8 + 4 + 16)
RA, RI, RB = 0, 16, 24


FROM = 1


class Phase:

    def __init__(self, nc, name):
        self.nc, self.name, self.ctx, self.sems = nc, name, ExitStack(), []

    def __enter__(self):
        self.ctx.__enter__()
        return self

    def __exit__(self, *a):
        return self.ctx.__exit__(*a)

    def sb(self, name, shape, dt=F32):
        return self.ctx.enter_context(self.nc.sbuf_tensor(f"{self.name}_{name}", shape, dt))

    def ps(self, name, shape=(P, 512), dt=F32):
        return self.ctx.enter_context(self.nc.psum_tensor(f"{self.name}_{name}", list(shape), dt))

    def sem(self, name):
        s = self.ctx.enter_context(self.nc.semaphore(f"{self.name}_{name}"))
        self.sems.append(s)
        return s

    def block(self):
        def reset(eng, share):
            for s in self.sems[share::4]:
                eng.sem_clear(s)
                eng.sem_inc(s, FROM)

        with self.nc.Block() as start:
            @start.sync
            def _(sp):
                reset(sp, 0)

            @start.tensor
            def _(pe):
                reset(pe, 1)

            @start.vector
            def _(dve):
                reset(dve, 2)

            @start.scalar
            def _(act):
                reset(act, 3)
        return self.ctx.enter_context(self.nc.Block())


def bc(ap, n):
    return ap.unsqueeze(2).to_broadcast([ap.shape[0], ap.shape[1], n])


def one(ap, i):
    if isinstance(i, int):
        return ap[:, i]
    return ap[:, ds(i, 1)].rearrange("p a n -> p (a n)")


def rows(ap, i, n):
    return ap[i:i + n] if isinstance(i, int) else ap[ds(i, n)]


def key_tile(t):
    return (P * (t + 1), 0) if t < NT else (PAST + DEC, SEQ)


class Norm:

    def __init__(self, ph, nc, consts, x_loaded, x, g_dram, sbp=None):
        self.nc, self.x, self.x_loaded = nc, x, x_loaded
        self.ident = consts["ident"]
        self.g_dram = g_dram
        self.junk = ph.sb("junk", [P, D], BF16)
        self.hn = ph.sb("hn", [P, D])
        self.hf = ph.sb("hf", [P, KD, P])
        self.gT = ph.sb("gT", [P, KD])
        self.stat = ph.sb("stat", [P, 4])
        self.tp = [ph.ps("ht0"), ph.ps("ht1")]
        self.g_in = ph.sem("g_in")
        self.ssq = ph.sem("ssq")
        self.ms = ph.sem("ms")
        self.rt = ph.sem("rt")
        self.rinv = ph.sem("rinv")
        self.hn_ready = ph.sem("hn_ready")
        self.ht_ready = ph.sem("ht_ready")
        self.hf_ready = ph.sem("hf_ready")
        self.hi_ready = ph.sem("hi_ready")
        self.lo_ready = ph.sem("lo_ready")

    def load_g(self, sp):
        sp.dma_start(self.gT[:], self.g_dram.rearrange("(k p) -> p k", p=P),
                     allow_slow_non_contiguous=True).then_inc(self.g_in, 16)

    def act_square(self, act, i, x_sem, x_val):
        act.wait_ge(x_sem, FROM + x_val)
        act.wait_ge(self.hn_ready, FROM + i)
        self.nc.scalar.activation(self.junk[:], self.x, ACT.Square, accum_out=self.stat[:, 0:1]).then_inc(self.ssq, 1)

    def act_sqrt(self, act, i):
        act.wait_ge(self.ms, FROM + i + 1)
        self.nc.scalar.activation(self.stat[:, 2:3], self.stat[:, 1:2], ACT.Sqrt).then_inc(self.rt, 1)

    def dve_norm(self, dve, i):
        v = self.nc.vector
        dve.wait_ge(self.ssq, FROM + i + 1)
        v.tensor_scalar(self.stat[:, 1:2], self.stat[:, 0:1], 1.0 / D, EPS, ALU.mult, ALU.add).then_inc(self.ms, 1)
        dve.wait_ge(self.rt, FROM + i + 1)
        v.reciprocal(self.stat[:, 3:4], self.stat[:, 2:3]).then_inc(self.rinv, 1)
        dve.wait_ge(self.rinv, FROM + i + 1)
        dve.wait_ge(self.ht_ready, FROM + i * 2)
        v.tensor_scalar(self.hn[:], self.x, self.stat[:, 3:4], None, ALU.mult).then_inc(self.hn_ready, 1)

    def pe_transposes(self, pe, i):
        pe.wait_ge(self.hn_ready, FROM + i + 1)
        pe.wait_ge(self.hf_ready, FROM + i * 2)
        for b in range(2):
            for k in range(4):
                last = self.nc.tensor.transpose(self.tp[b][:, k * P:(k + 1) * P],
                                                self.hn[:, (4 * b + k) * P:(4 * b + k + 1) * P], self.ident[:])
            last.then_inc(self.ht_ready, 1)

    def dve_scale_g(self, dve, i):
        dve.wait_ge(self.hi_ready, FROM + i * 2)
        dve.wait_ge(self.lo_ready, FROM + i * 2)
        if isinstance(i, int) and i == 0:
            dve.wait_ge(self.g_in, FROM + 16)
        for b in range(2):
            dve.wait_ge(self.ht_ready, FROM + i * 2 + b + 1)
            self.nc.vector.tensor_tensor(self.hf[:, 4 * b:4 * b + 4, :],
                                         self.tp[b][:].rearrange("p (k t) -> p k t", k=4),
                                         bc(self.gT[:, 4 * b:4 * b + 4], P), ALU.mult).then_inc(self.hf_ready, 1)

    def act_hi(self, act, i, hi, n=P):
        for b in range(2):
            act.wait_ge(self.hf_ready, FROM + i * 2 + b + 1)
            self.nc.scalar.activation(hi[b], self.hf[:, 4 * b:4 * b + 4, 0:n], ACT.Copy).then_inc(self.hi_ready, 1)

    def dve_lo(self, dve, i, hi, lo, n=P):
        for b in range(2):
            dve.wait_ge(self.hf_ready, FROM + i * 2 + b + 1)
            dve.wait_ge(self.hi_ready, FROM + i * 2 + b + 1)
            self.nc.vector.tensor_tensor(lo[b], self.hf[:, 4 * b:4 * b + 4, 0:n], hi[b].bitcast(F32),
                                         ALU.subtract).then_inc(self.lo_ready, 1)


def three_passes(nc, out, lhs, rhs, first, last):
    (lh, ll), (rh, rl) = lhs, rhs
    nc.tensor.matmul(out, lh, rh, start=first, stop=False)
    nc.tensor.matmul(out, lh, rl, start=False, stop=False)
    return nc.tensor.matmul(out, ll, rh, start=False, stop=last)


def projection(nc, dram, consts, kind, x_src, g_dram, w_dram, dst, out):
    even, fox = kind == "even", kind == "c"
    width = w_dram.shape[1]
    ng = 4 if fox else 3
    gw = [494, 494, 492] if even else [386] * 4 if fox else [512] * 3
    go = [sum(gw[:g]) for g in range(ng)]
    ident = consts["ident"]
    with Phase(nc, f"proj_{kind}") as ph:
        sb, sem = ph.sb, ph.sem
        whi = sb("whi", [P, KD, width], F32R)
        wlo = sb("wlo", [P, KD, width], F32R)
        wraw = sb("wraw", [P, 2, width])
        x = sb("x", [P, D])
        hhi = sb("hhi", [P, KD, P], F32R)
        hlo = sb("hlo", [P, KD, P], F32R)
        proj = sb("proj", [P, width])
        trig = sb("trig", [P, TILES, ROPE_COLS]) if even else None
        norm = Norm(ph, nc, consts, None, x[:], g_dram)
        mm = [ph.ps(f"mm{g}") for g in range(ng)]
        tq = [ph.ps(f"tq{g}") for g in range(6 - ng)]
        w_in = [sem("w_in0"), sem("w_in1")]
        w_hi, w_lo = sem("w_hi"), sem("w_lo")
        x_in, trig_in = sem("x_in"), sem("trig_in")
        mm_ready, proj_act = sem("mm_ready"), sem("proj_act")
        tq_ready, tq_act, qb_tp = sem("tq_ready"), sem("tq_act"), sem("qb_tp")
        stored, cache_in, cache_tp, cache_cp = sem("stored"), sem("cache_in"), sem("cache_tp"), sem("cache_cp")
        post, dve_step, passed = sem("post"), sem("dve_step"), sem("passed")
        dve_rope, stage_step, rr_done = sem("dve_rope"), sem("stage_step"), sem("rr_done")
        if even:
            rot = sb("rot", [P, 4, 10 * 16])
            stage = sb("stage", [P, P + 96])
            gq = sb("gq", [P, QR])
            gkv = sb("gkv", [P, KVR])
            lat = sb("lat", [P, KVR])
            cqn = norm.hf[:, 4:6, :].rearrange("p k t -> p (k t)")
            cqT = sb("cqT", [P, 2, P])
            wuq = sb("wuq", [P, 2, 768])
            qb = sb("qb", [P, 8, 96])
            qbT = sb("qbT", [96, 8, P])
            nst = sb("nst", [P, 8])
            sq_done, ms_done, rt_done = sem("sq_done"), sem("ms_done"), sem("rt_done")
            cqT_ready, qb_mm, qb_cp, qbT_ready, gq_in, qbT_stored = (
                sem("cqT_ready"), sem("qb_mm"), sem("qb_cp"), sem("qbT_ready"), sem("gq_in"),
                sem("qbT_stored"))
        rows4 = norm.hn[:].rearrange("p (b c n) -> p b c n", b=2, c=4)
        if even:
            ck, ci, cl, cr = rows4[:, :, 0], rows4[:, :, 1], rows4[:, :, 2], rows4[:, :, 3, 0:96]

        nstore = 5 if even else 2

        def keycol(i, tail):
            return OWN if tail else i * P

        def tiles(eng):
            with eng.Fori(0, NT) as i:
                yield i, False
            yield NT, True

        block = ph.block()

        @block.sync
        def _(sp):
            for k in range(KD):
                if k >= 2:
                    sp.wait_ge(w_lo, FROM + k - 1)
                sp.dma_start(wraw[:, k % 2, :], w_dram[k * P:(k + 1) * P, :]).then_inc(w_in[k % 2], 16)
            norm.load_g(sp)
            if even:
                sp.dma_start(gq[:], dram["g_b_q"][0:1, :].to_broadcast([P, QR])).then_inc(gq_in, 16)
                sp.dma_start(gkv[:], dram["g_b_kv"][0:1, :].to_broadcast([P, KVR])).then_inc(gq_in, 16)
                sp.dma_start(wuq[:], dram["w_b_uq"][0].rearrange("(k p) n -> p k n", p=P)).then_inc(gq_in, 16)
                for b in range(2):
                    r = slice(b * P, (b + 1) * P)
                    sp.dma_start(ck[:, b], dram["cache_a_k"][0, 0, r].rearrange("t g d -> t (g d)")).then_inc(cache_in, 16)
                    sp.dma_start(dst["v"][:, NT + b, :], dram["cache_a_v"][0, 0, r].rearrange("t g d -> t (g d)")).then_inc(cache_in, 16)
                    for c in range(4):
                        sp.dma_start(ci[:, b, c * 32:c * 32 + 32], dram["cache_a_idx_k"][0, 0, r]).then_inc(cache_in, 16)
                    sp.dma_start(cl[:, b, :], dram["cache_b_latent"][0, 0, r]).then_inc(cache_in, 16)
                    sp.dma_start(cr[:, b, 64:96], dram["cache_b_rope"][0, 0, r]).then_inc(cache_in, 16)
            else:
                for b in range(2):
                    r = slice(b * P, (b + 1) * P)
                    sp.dma_start(rows4[:, b].rearrange("p a n -> p (a n)"),
                                 dram[f"cache_{kind}_k"][0, 0, r].rearrange("t g d -> t (g d)")).then_inc(cache_in, 16)
                    sp.dma_start(dst["v"][:, NT + b, :],
                                 dram[f"cache_{kind}_v"][0, 0, r].rearrange("t g d -> t (g d)")).then_inc(cache_in, 16)
            if even:
                sp.dma_start(trig[:], dram["trig"].rearrange("t p n -> p t n")).then_inc(trig_in, 16)

            def load(i, tail):
                sp.wait_ge(norm.hn_ready, FROM + i)
                if tail:
                    sp.dma_start(x[0:DEC, :], x_src[1]).then_inc(x_in, 16)
                else:
                    sp.dma_start(x[:], rows(x_src[0], i * P, P)).then_inc(x_in, 16)

            def store(i, tail):
                n, pre, r0 = (DEC, "s", 0) if tail else (P, "p", i * P)

                def put(name, src):
                    sp.dma_start(rows(out[f"{pre}_{name}"], r0, n), src).then_inc(stored, 16)

                if not even:
                    sp.wait_ge(proj_act, FROM + ng * i + ng)
                    put(f"{kind}_k", proj[0:n, 512:1024])
                    put(f"{kind}_v", proj[0:n, 1024:1536])
                    return
                sp.wait_ge(post, FROM + i + 1)
                put("a_k", proj[0:n, 512:640])
                put("a_v", proj[0:n, 640:768])
                put("a_idx_k", proj[0:n, 1024:1056])
                put("b_latent", lat[0:n, :])
                put("b_rope", proj[0:n, 1448:1480])
                sp.wait_ge(qbT_ready, FROM + 2 * i + 2)
                sp.sem_inc(passed, 1)
                q0 = ds(i * P, P) if not tail else slice(SEQ, TOK)
                sp.dma_start(dram["qbT"][:, :, q0].rearrange("h d t -> d h t"), qbT[:, :, 0:n]).then_inc(qbT_stored, 16)

            load(0, False)
            with sp.Fori(0, NT - 1) as i:
                load(i + 1, False)
                store(i, False)
            load(NT, True)
            store(NT - 1, False)
            store(NT, True)
            sp.wait_ge(stored, FROM + (NT + 1) * 16 * nstore)
            if even:
                sp.wait_ge(qbT_stored, FROM + (NT + 1) * 16)

        @block.scalar
        def _(act):
            s = nc.scalar
            for k in range(KD):
                act.wait_ge(w_in[k % 2], FROM + 16 * (k // 2 + 1))
                s.activation(whi[:, k, :], wraw[:, k % 2, :], ACT.Copy).then_inc(w_hi, 1)
            if even:
                for b in range(2):
                    act.wait_ge(cache_tp, FROM + b + 1)
                    c0 = SEQ + b * P
                    s.activation(dst["kaT"][:, c0:c0 + P], mm[b][:, 0:P], ACT.Copy)
                    s.activation(dst["kiT"][:, c0:c0 + P], mm[b][:, P:2 * P], ACT.Copy)
                    s.activation(dst["latT"][:, c0:c0 + P], mm[b][:, 2 * P:3 * P], ACT.Copy)
                    s.activation(dst["krT"][64:96, c0:c0 + P], mm[b][64:96, 3 * P:4 * P], ACT.Copy).then_inc(cache_cp, 1)
            else:
                for b in range(2):
                    act.wait_ge(cache_tp, FROM + b + 1)
                    c0 = SEQ + b * P
                    s.activation(dst["kT"][:, :, c0:c0 + P], mm[b][:].rearrange("p (c t) -> p c t", c=4),
                                 ACT.Copy).then_inc(cache_cp, 1)
            for i, tail in tiles(act):
                n = DEC if tail else P
                kc = keycol(i, tail)
                norm.act_square(act, i, x_in, i * 16 + 16)
                norm.act_sqrt(act, i)
                act.wait_ge(mm_ready, FROM + ng * i)
                norm.act_hi(act, i, [hhi[:, 0:4, :], hhi[:, 4:8, :]])
                act.wait_ge(stored, FROM + i * 16 * nstore)
                act.wait_ge(tq_ready, FROM + (3 if even else 2) * i)
                for g in range(ng):
                    act.wait_ge(mm_ready, FROM + ng * i + g + 1)
                    s.activation(proj[:, go[g]:go[g] + gw[g]], mm[g][:, 0:gw[g]], ACT.Copy).then_inc(proj_act, 1)
                vt = KT - 1 if tail else i
                vs = slice(640, 768) if even else slice(1024, 1536)
                act.wait_ge(proj_act, FROM + ng * i + ng)
                if even:
                    act.wait_ge(dve_step, FROM + i * 1)
                    s.activation(norm.junk[:, 0:QR], proj[:, 1064:1320], ACT.Square, accum_out=nst[:, 0:1]).then_inc(sq_done, 1)
                    s.activation(norm.junk[:, QR:QR + KVR], proj[:, 1320:1448], ACT.Square, accum_out=nst[:, 1:2]).then_inc(sq_done, 1)
                    act.wait_ge(ms_done, FROM + i + 1)
                    s.activation(nst[:, 4:6], nst[:, 2:4], ACT.Sqrt).then_inc(rt_done, 1)
                    s.activation(one(dst["v"], vt), proj[:, vs], ACT.Copy)
                    s.activation(one(dst["wi"], i), proj[:, 1056:1064], ACT.Copy, scale=8 ** -0.5)
                    q = ds(i * P, n) if not tail else slice(SEQ, TOK)
                    kk = ds(kc, n) if not tail else slice(kc, kc + n)
                    act.wait_ge(tq_ready, FROM + 3 * i + 1)
                    s.activation(dst["qaT"][:, :, q], tq[0][:].rearrange("p (c t) -> p c t", c=4)[:, :, 0:n], ACT.Copy,
                                 scale=HD ** -0.5).then_inc(tq_act, 1)
                    act.wait_ge(tq_ready, FROM + 3 * i + 2)
                    s.activation(dst["kaT"][:, kk], tq[1][:, 0:n], ACT.Copy)
                    s.activation(dst["kiT"][:, kk], tq[1][:, P:P + n], ACT.Copy)
                    s.activation(dst["latT"][:, kk], tq[1][:, 2 * P:2 * P + n], ACT.Copy)
                    s.activation(dst["krT"][64:96, kk], tq[1][64:96, 3 * P:3 * P + n], ACT.Copy).then_inc(tq_act, 1)
                    for g in range(2):
                        act.wait_ge(qb_mm, FROM + 2 * i + g + 1)
                        s.activation(qb[:, 4 * g:4 * g + 4, :].rearrange("p h d -> p (h d)"), tq[g][:, 0:384],
                                     ACT.Copy).then_inc(qb_cp, 1)
                    for g in range(2):
                        act.wait_ge(qb_tp, FROM + 2 * i + g + 1)
                        if g == 0:
                            act.wait_ge(qbT_stored, FROM + i * 16)
                        s.activation(qbT[:, 4 * g:4 * g + 4, :], tq[g][0:96, :].rearrange("p (h t) -> p h t", h=4),
                                     ACT.Copy, scale=96 ** -0.5).then_inc(qbT_ready, 1)
                else:
                    s.activation(one(dst["v"], vt), proj[:, vs], ACT.Copy)
                    q = ds(i * P, n) if not tail else slice(SEQ, TOK)
                    kk = ds(kc, n) if not tail else slice(kc, kc + n)
                    if fox:
                        s.activation(one(dst["fc"], vt), proj[:, 1536:1544], ACT.Copy)
                    act.wait_ge(tq_ready, FROM + 2 * i + 1)
                    s.activation(dst["qT"][:, :, q], tq[0][:].rearrange("p (c t) -> p c t", c=4)[:, :, 0:n], ACT.Copy,
                                 scale=HD ** -0.5).then_inc(tq_act, 1)
                    act.wait_ge(tq_ready, FROM + 2 * i + 2)
                    s.activation(dst["kT"][:, :, kk], tq[1][:].rearrange("p (c t) -> p c t", c=4)[:, :, 0:n],
                                 ACT.Copy).then_inc(tq_act, 1)

        def rope(v, dve, i, src, tab, nh, hd, off, half, cnt):
            x1, x2 = src[:, :, off:off + half], src[:, :, off + half:off + 2 * half]
            tr = one(trig, i)
            cos = tr[:, tab:tab + half].unsqueeze(1).to_broadcast([P, nh, half])
            sin = tr[:, tab + half:tab + 2 * half].unsqueeze(1).to_broadcast([P, nh, half])
            r = [rot[:, j, 0:nh * half].rearrange("p (h d) -> p h d", h=nh) for j in range(4)]
            v.tensor_tensor(r[0], x1, cos, ALU.mult).then_inc(dve_rope, 1)
            v.tensor_tensor(r[1], x2, sin, ALU.mult).then_inc(dve_rope, 1)
            v.tensor_tensor(r[2], x1, sin, ALU.mult).then_inc(dve_rope, 1)
            v.tensor_tensor(r[3], x2, cos, ALU.mult).then_inc(dve_rope, 1)
            dve.wait_ge(dve_rope, FROM + cnt + 4)
            v.tensor_tensor(x1, r[0], r[1], ALU.subtract).then_inc(dve_rope, 1)
            v.tensor_tensor(x2, r[2], r[3], ALU.add).then_inc(dve_rope, 1)
            dve.wait_ge(dve_rope, FROM + cnt + 6)
            return cnt + 6

        @block.vector
        def _(dve):
            v = nc.vector
            for k in range(KD):
                dve.wait_ge(w_hi, FROM + k + 1)
                v.tensor_tensor(wlo[:, k, :], wraw[:, k % 2, :], whi[:, k, :].bitcast(F32), ALU.subtract).then_inc(w_lo, 1)
            if even:
                v.memset(stage[:], 0.0).then_inc(stage_step, 1)
                v.memset(cr[:, :, 0:64], 0.0).then_inc(stage_step, 1)
                dve.wait_ge(gq_in, FROM + 48)
            if fox:
                v.memset(dst["fc"][:, NT:KT - 1, :], 0.0)
            dve.wait_ge(norm.g_in, FROM + 16)
            dve.wait_ge(cache_tp, FROM + 2)
            for i, tail in tiles(dve):
                norm.dve_norm(dve, i)
                norm.dve_scale_g(dve, i)
                dve.wait_ge(mm_ready, FROM + ng * i)
                norm.dve_lo(dve, i, [hhi[:, 0:4, :], hhi[:, 4:8, :]], [hlo[:, 0:4, :], hlo[:, 4:8, :]])
                dve.wait_ge(proj_act, FROM + ng * i + ng)
                if not even:
                    continue
                c = 24 * i
                dve.wait_ge(trig_in, FROM + 16)
                c = rope(v, dve, i, proj[:, 0:640].rearrange("p (h d) -> p h d", d=64), RA, 10, 64, 0, 8, c)
                c = rope(v, dve, i, proj[:, 768:1056].rearrange("p (h d) -> p h d", d=32), RI, 9, 32, 0, 4, c)
                c = rope(v, dve, i, proj[:, 1448:1480].rearrange("p (h d) -> p h d", d=32), RB, 1, 32, 0, 16, c)
                dve.wait_ge(sq_done, FROM + 2 * i + 2)
                v.tensor_scalar(nst[:, 2:3], nst[:, 0:1], 1.0 / QR, EPS, ALU.mult, ALU.add)
                v.tensor_scalar(nst[:, 3:4], nst[:, 1:2], 1.0 / KVR, EPS, ALU.mult, ALU.add).then_inc(ms_done, 1)
                dve.wait_ge(rt_done, FROM + i + 1)
                v.reciprocal(nst[:, 6:8], nst[:, 4:6]).then_inc(rr_done, 1)
                dve.wait_ge(rr_done, FROM + i + 1)
                v.scalar_tensor_tensor(cqn, proj[:, 1064:1320], nst[:, 6:7], gq[:], ALU.mult, ALU.mult)
                v.scalar_tensor_tensor(lat[:], proj[:, 1320:1448], nst[:, 7:8], gkv[:], ALU.mult, ALU.mult).then_inc(dve_step, 1)
                v.tensor_copy(stage[:, 0:P].rearrange("p (c d) -> p c d", c=4),
                              proj[:, 1024:1056].unsqueeze(1).to_broadcast([P, 4, 32]))
                v.tensor_copy(norm.hf[:, 0:4, :].rearrange("p c (g d) -> p c g d", g=2),
                              proj[:, 0:512].rearrange("p (g c d) -> p c g d", g=2, d=HD))
                v.tensor_copy(stage[:, P + 64:P + 96], proj[:, 1448:1480]).then_inc(post, 1)
                dve.wait_ge(tq_ready, FROM + 3 * i + 3)
                n = DEC if tail else P
                q = ds(i * P, n) if not tail else slice(SEQ, TOK)
                v.tensor_copy(cqT[:], tq[2][:, 2 * P:4 * P].rearrange("p (c t) -> p c t", c=2)).then_inc(cqT_ready, 1)
                v.tensor_scalar(dst["qiT"][:, :, q], tq[2][:, 0:2 * P].rearrange("p (c t) -> p c t", c=2)[:, :, 0:n],
                                32 ** -0.5, None, ALU.mult).then_inc(cqT_ready, 1)
                dve.wait_ge(qb_cp, FROM + 2 * i + 2)
                rope(v, dve, i, qb[:], RB, 8, 96, 64, 16, c)

        @block.tensor
        def _(pe):
            t = nc.tensor
            pe.wait_ge(cache_in, FROM + 16 * (16 if even else 4))
            if even:
                pe.wait_ge(stage_step, FROM + 2)
                for b in range(2):
                    t.transpose(mm[b][:, 0:P], ck[:, b], ident[:])
                    t.transpose(mm[b][:, P:2 * P], ci[:, b], ident[:])
                    t.transpose(mm[b][:, 2 * P:3 * P], cl[:, b, :], ident[:])
                    t.transpose(mm[b][0:96, 3 * P:4 * P], cr[:, b, :], ident[:]).then_inc(cache_tp, 1)
            else:
                for b in range(2):
                    for c in range(4):
                        last = t.transpose(mm[b][:, c * P:(c + 1) * P], rows4[:, b, c, :], ident[:])
                    last.then_inc(cache_tp, 1)
            pe.wait_ge(cache_cp, FROM + 2)
            pe.wait_ge(w_lo, FROM + KD)
            for i, tail in tiles(pe):
                norm.pe_transposes(pe, i)
                pe.wait_ge(norm.lo_ready, FROM + 2 * i + 2)
                pe.wait_ge(proj_act, FROM + ng * i)
                for g in range(ng):
                    cols = slice(go[g], go[g] + gw[g])
                    for k in range(KD):
                        last = three_passes(nc, mm[g][:, 0:gw[g]], (hhi[:, k, :], hlo[:, k, :]),
                                            (whi[:, k, cols], wlo[:, k, cols]), k == 0, k == KD - 1)
                    last.then_inc(mm_ready, 1)
                if even:
                    pe.wait_ge(post, FROM + i + 1)
                else:
                    pe.wait_ge(proj_act, FROM + ng * i + ng)
                if even:
                    pe.wait_ge(qbT_ready, FROM + 2 * i)
                    for c in range(4):
                        last = t.transpose(tq[0][:, c * P:(c + 1) * P], norm.hf[:, c, :], ident[:])
                    last.then_inc(tq_ready, 1)
                    t.transpose(tq[1][:, 0:P], proj[:, 512:640], ident[:])
                    t.transpose(tq[1][:, P:2 * P], stage[:, 0:P], ident[:])
                    t.transpose(tq[1][:, 2 * P:3 * P], lat[:], ident[:])
                    t.transpose(tq[1][0:96, 3 * P:4 * P], stage[:, P:P + 96], ident[:]).then_inc(tq_ready, 1)
                    pe.wait_ge(cqT_ready, FROM + 2 * i)
                    for c in range(2):
                        t.transpose(tq[2][:, c * P:(c + 1) * P], proj[:, 768 + c * P:768 + (c + 1) * P], ident[:])
                    for c in range(2):
                        last = t.transpose(tq[2][:, (2 + c) * P:(3 + c) * P], cqn[:, c * P:(c + 1) * P], ident[:])
                    last.then_inc(tq_ready, 1)
                    pe.wait_ge(cqT_ready, FROM + 2 * i + 1)
                    for g in range(2):
                        pe.wait_ge(tq_act, FROM + 2 * i + g + 1)
                        for c in range(2):
                            last = t.matmul(tq[g][:, 0:384], cqT[:, c, :], wuq[:, c, 384 * g:384 * (g + 1)],
                                            start=(c == 0), stop=(c == 1))
                        last.then_inc(qb_mm, 1)
                    pe.wait_ge(dve_rope, FROM + 24 * i + 24)
                    for g in range(2):
                        for h in range(4):
                            last = t.transpose(tq[g][0:96, h * P:(h + 1) * P], qb[:, 4 * g + h, :], ident[:])
                        last.then_inc(qb_tp, 1)
                else:
                    pe.wait_ge(tq_act, FROM + 2 * i)
                    for g in range(2):
                        for c in range(4):
                            last = t.transpose(tq[g][:, c * P:(c + 1) * P],
                                               proj[:, 512 * g + c * P:512 * g + (c + 1) * P], ident[:])
                        last.then_inc(tq_ready, 1)


TILES = NT + 1
UNITS = 2 * TILES
UNIT = [(t, h) for t in range(TILES) for h in range(2)]


def queries(t):
    return DEC if t == NT else P


def blocks(t, g):
    w = key_tile(t)[0]
    return [(b, min(P, w - b * P)) for b in range(4 * g, min(4 * g + 4, (w + P - 1) // P))]


WIDE = [u for u, (t, h) in enumerate(UNIT) if blocks(t, 1)]
O_USES = [[t for t in range(TILES) if t % 2 == s] for s in range(2)]


def group_count(p, u, g):
    return p * UNITS + u if g == 0 else p * len(WIDE) + WIDE.index(u)


def o_count(p, t):
    return p * len(O_USES[t % 2]) + O_USES[t % 2].index(t)


def attention(nc, dram, consts, kind, src, chunk0):
    ident, ident_bf = consts["ident"], consts["ident_bf"]
    stick, mla, fox, dsa = kind == "d", kind == "b", kind == "c", kind == "a"
    mask = None if dsa else consts[{"b": "mask_chunk", "c": "mask_causal", "d": "mask_strict"}[kind]]
    with Phase(nc, f"att_{kind}") as ph:
        sb, sem = ph.sb, ph.sem
        q = sb("q", [96, 2, TOK]) if mla else sb("q", [P, TOK])
        if dsa:
            k, v = src["kaT"], src["v"]
        elif mla:
            k, v = [src["krT"], sb("k1", [96, KEYS])], sb("v", [P, KT, P])
            wkv = sb("wkv", [P, 2 * P])
        else:
            k, v = sb("k", [P, KEYS]), sb("v", [P, KT, P])
        if fox:
            fk = sb("fk", [P, 2, KEYS])
        prob = [sb(f"prob{s}", [P, SEQ]) for s in range(2)]
        if stick:
            ez = sb("ez", [P, SEQ])
            sp = sb("sp", [P, SEQ])
        pt = [sb(f"pt{s}", [P, 8, P]) for s in range(2)]
        ot = [sb(f"ot{s}", [P, P]) for s in range(2)]
        nm = sb("nm", [P, 2])
        rs = sb("rs", [P, 2])
        rr = sb("rr", [P, 2])
        S = [ph.ps(f"s{s}", (P, SEQ)) for s in range(2)]
        TP = [ph.ps(f"tp{g}") for g in range(2)]
        O = [ph.ps(f"o{g}") for g in range(2)]
        staged, passed = sem("staged"), sem("passed")
        s_ready, prob_ready, pv_done = sem("s_ready"), sem("prob_ready"), sem("pv_done")
        max_done, exp_done, rcp_done = sem("max_done"), sem("exp_done"), sem("rcp_done")
        tp_ready = [sem(f"tp_ready{g}") for g in range(2)]
        pt_ready = [sem(f"pt_ready{g}") for g in range(2)]
        o_out = [sem(f"o_out{s}") for s in range(2)]
        ot_stored = [sem(f"ot_stored{s}") for s in range(2)]
        if mla:
            w_in, kv_ready, kv_out = sem("w_in"), sem("kv_ready"), sem("kv_out")
        if stick:
            abs_done, ez_done, ln_done, sp_done, scan_done, arg_done = (
                sem("abs_done"), sem("ez_done"), sem("ln_done"), sem("sp_done"), sem("scan_done"), sem("arg_done"))
        block = ph.block()

        @block.sync
        def _(eng):
            with eng.Fori(0, 4) as p:
                if mla:
                    eng.wait_ge(pv_done, FROM + p * UNITS)
                    eng.dma_start(q[:], dram["qbT"][ds(2 * p, 2)].rearrange("h d t -> d h t")).then_inc(w_in, 16)
                    eng.dma_start(wkv[:], dram["w_b_ukv"][0, :, ds(p * 2 * P, 2 * P)]).then_inc(w_in, 16)
                for t in range(TILES):
                    s, n = t % 2, queries(t)
                    eng.wait_ge(o_out[s], FROM + o_count(p, t) + 1)
                    eng.dma_start(dram["att"][ds(p + chunk0, 1), :, t * P:t * P + n].rearrange("a p n -> (a p) n"),
                                  ot[s][:, 0:n]).then_inc(ot_stored[s], 16)
            for s in range(2):
                eng.wait_ge(ot_stored[s], FROM + 16 * 4 * len(O_USES[s]))

        @block.gpsimd
        def _(pool):
            g = nc.gpsimd
            if mla:
                g.tensor_copy(k[1][64:96, :], src["krT"][64:96, :]).then_inc(staged, 1)
                return
            with pool.Fori(0, 4) as p:
                pool.wait_ge(pv_done, FROM + p * UNITS)
                g.tensor_copy(q[:], one(src["qaT"] if dsa else src["qT"], p)).then_inc(staged, 1)
                if not dsa:
                    g.tensor_copy(k[:], one(src["kT"], p)).then_inc(staged, 1)
                    g.tensor_copy(v[:, 0:KT - 1], src["v"][:, 0:KT - 1, ds(p * P, P)]).then_inc(staged, 1)
                    g.tensor_copy(v[0:DEC, KT - 1], src["v"][0:DEC, KT - 1, ds(p * P, P)]).then_inc(staged, 1)

        staged_pair = (0 if mla else 1 if dsa else 4) + (2 if fox else 0)

        @block.tensor
        def _(pe):
            tt = nc.tensor

            def scores(u):
                t, h = UNIT[u]
                n, s = queries(t), u % 2
                w, k0 = key_tile(t)
                hp = slice(h * HD, (h + 1) * HD)
                for c0 in range(0, w, 512):
                    cw = min(512, w - c0)
                    o = S[s][0:n, c0:c0 + cw]
                    if mla:
                        parts = [(o, q[:, h, t * P:t * P + n], k[h][:, k0 + c0:k0 + c0 + cw])]
                    else:
                        parts = [(o, q[hp, t * P:t * P + n], k[hp, k0 + c0:k0 + c0 + cw])]
                    if fox:
                        parts.append((o, src["fq"][:, t * P:t * P + n], fk[:, h, k0 + c0:k0 + c0 + cw]))
                    if dsa:
                        b0 = src["bias_at"][t] + c0
                        parts.append((o, ident_bf[:, 0:n], src["bias"][:, b0:b0 + cw]))
                    elif c0 + cw == w and not (mla and t == NT):
                        parts.append((S[s][0:n, w - n:w], ident_bf[:, 0:n], mask[:, 0:n]))
                    for j, (o, a, b) in enumerate(parts):
                        last = tt.matmul(o, a, b, start=(j == 0), stop=(j == len(parts) - 1))
                last.then_inc(s_ready, 1)

            def products(p, u):
                t, h = UNIT[u]
                n, s = queries(t), u % 2
                w = key_tile(t)[0]
                groups = [g for g in range(2) if blocks(t, g)]
                pe.wait_ge(prob_ready, FROM + p * UNITS + u + 1)
                for g in groups:
                    pe.wait_ge(pt_ready[g], FROM + group_count(p, u, g))
                    if n < P:
                        pe.sem_inc(passed, 1)
                    for b, r in blocks(t, g):
                        last = tt.transpose(TP[g][0:r, (b % 4) * P:(b % 4) * P + n],
                                            prob[s][0:n, b * P:b * P + r], ident[0:n, 0:n])
                    last.then_inc(tp_ready[g], 1)
                if h == 0:
                    pe.wait_ge(o_out[t % 2], FROM + o_count(p, t))
                for g in groups:
                    pe.wait_ge(pt_ready[g], FROM + group_count(p, u, g) + 1)
                    for b, r in blocks(t, g):
                        last = tt.matmul(O[t % 2][h * HD:(h + 1) * HD, 0:n],
                                         v[0:r, b if t < NT else NT + b, h * HD:(h + 1) * HD],
                                         pt[s][0:r, b, 0:n], start=(b == 0), stop=(b * P + r == w))
                last.then_inc(pv_done, 1)

            def expand(p):
                pe.wait_ge(w_in, FROM + 32 * p + 32)
                wv = wkv[:].rearrange("p (h x) -> p h x", h=2)[:, :, HD:P]
                for j in range(9):
                    if j >= 2:
                        pe.wait_ge(kv_out, FROM + 9 * p + j - 1)
                    if j < 6:
                        h, c = j // 3, j % 3
                        last = tt.matmul(S[j % 2][0:HD, 0:448], wkv[:, h * P:h * P + HD],
                                         src["latT"][:, c * 448:(c + 1) * 448], start=True, stop=True)
                    else:
                        for b in range(4 * (j - 6), min(4 * (j - 5), KT)):
                            r = DEC if b == KT - 1 else P
                            last = tt.matmul(S[j % 2][0:r, (b % 4) * P:(b % 4 + 1) * P],
                                             src["latT"][:, b * P:b * P + r], wv, start=True, stop=True)
                    last.then_inc(kv_ready, 1)
                pe.wait_ge(kv_out, FROM + 9 * p + 9)

            if mla:
                pe.wait_ge(staged, FROM + 1)
            with pe.Fori(0, 4) as p:
                if mla:
                    expand(p)
                else:
                    pe.wait_ge(staged, FROM + staged_pair * p + staged_pair)
                scores(0)
                for u in range(UNITS):
                    if u + 1 < UNITS:
                        scores(u + 1)
                    products(p, u)

        def copy_group(eng, p, u, g):
            t, h = UNIT[u]
            bl = blocks(t, g)
            if not bl:
                return
            n, s = queries(t), u % 2
            eng.wait_ge(tp_ready[g], FROM + group_count(p, u, g) + 1)
            full = [b for b, r in bl if r == P]
            jobs = [(full[0], full[-1] + 1, P)] if full else []
            jobs += [(b, b + 1, r) for b, r in bl if r != P]
            for b0, b1, r in jobs:
                i = TP[g][:].rearrange("p (b t) -> p b t", b=4)[0:r, b0 - 4 * g:b1 - 4 * g, 0:n]
                o = pt[s][0:r, b0:b1, 0:n]
                last = nc.scalar.activation(o, i, ACT.Copy) if g == 0 else nc.vector.tensor_copy(o, i)
            last.then_inc(pt_ready[g], 1)

        @block.scalar
        def _(act):
            s_ = nc.scalar

            def soft(p, u):
                t, h = UNIT[u]
                n, s, w = queries(t), u % 2, key_tile(t)[0]
                m = p * UNITS + u
                if stick:
                    act.wait_ge(s_ready, FROM + m + 1)
                    act.wait_ge(sp_done, FROM + m)
                    s_.activation(ez[0:n, 0:w], S[s][0:n, 0:w], ACT.Abs).then_inc(abs_done, 1)
                    act.wait_ge(abs_done, FROM + m + 1)
                    s_.activation(ez[0:n, 0:w], ez[0:n, 0:w], ACT.Exp, scale=-1.0).then_inc(ez_done, 1)
                    act.wait_ge(ez_done, FROM + m + 1)
                    s_.activation(ez[0:n, 0:w], ez[0:n, 0:w], ACT.Ln, bias=1.0).then_inc(ln_done, 1)
                    act.wait_ge(arg_done, FROM + m + 1)
                    s_.activation(prob[s][0:n, 0:w], prob[s][0:n, 0:w], ACT.Exp).then_inc(prob_ready, 1)
                else:
                    act.wait_ge(max_done, FROM + m + 1)
                    s_.activation(prob[s][0:n, 0:w], S[s][0:n, 0:w], ACT.Exp, bias=nm[0:n, s:s + 1],
                                  accum_out=rs[0:n, s:s + 1]).then_inc(exp_done, 1)

            def output(p, u):
                t, h = UNIT[u]
                if h == 0:
                    return
                act.wait_ge(pv_done, FROM + p * UNITS + u + 1)
                act.wait_ge(ot_stored[t % 2], FROM + 16 * o_count(p, t))
                s_.activation(ot[t % 2][:, 0:queries(t)], O[t % 2][:, 0:queries(t)], ACT.Copy).then_inc(o_out[t % 2], 1)

            with act.Fori(0, 4) as p:
                if mla:
                    for j in range(9):
                        act.wait_ge(kv_ready, FROM + 9 * p + j + 1)
                        if j < 6:
                            c = slice((j % 3) * 448, (j % 3 + 1) * 448)
                            s_.activation(k[j // 3][0:HD, c], S[j % 2][0:HD, 0:448], ACT.Copy).then_inc(kv_out, 1)
                        else:
                            b0 = 4 * (j - 6)
                            b1 = min(b0 + 4, KT - 1)
                            last = s_.activation(v[:, b0:b1, :].rearrange("p b d -> p (b d)"),
                                                 S[j % 2][:, 0:(b1 - b0) * P], ACT.Copy)
                            if j == 8:
                                last = s_.activation(v[0:DEC, KT - 1, :], S[j % 2][0:DEC, (b1 - b0) * P:(b1 - b0 + 1) * P],
                                                     ACT.Copy)
                            last.then_inc(kv_out, 1)
                soft(p, 0)
                for u in range(UNITS):
                    copy_group(act, p, u, 0)
                    if u + 1 < UNITS:
                        soft(p, u + 1)
                    output(p, u)

        @block.vector
        def _(dve):
            v_ = nc.vector

            def top(p, u):
                t, h = UNIT[u]
                n, s, w = queries(t), u % 2, key_tile(t)[0]
                m = p * UNITS + u
                if not stick:
                    dve.wait_ge(s_ready, FROM + m + 1)
                    v_.tensor_reduce(nm[0:n, s:s + 1], S[s][0:n, 0:w], AX_X, ALU.max, negate=True).then_inc(max_done, 1)

            def finish(p, u):
                t, h = UNIT[u]
                n, s, w = queries(t), u % 2, key_tile(t)[0]
                m = p * UNITS + u
                if stick:
                    dve.wait_ge(ln_done, FROM + m + 1)
                    v_.scalar_tensor_tensor(sp[0:n, 0:w], S[s][0:n, 0:w], 0.0, ez[0:n, 0:w], ALU.max, ALU.add).then_inc(sp_done, 1)
                    dve.wait_ge(sp_done, FROM + m + 1)
                    v_.tensor_tensor_scan(prob[s][0:n, 0:w][:, ::-1], sp[0:n, 0:w][:, ::-1], sp[0:n, 0:w][:, ::-1],
                                          0.0, ALU.add, ALU.bypass).then_inc(scan_done, 1)
                    dve.wait_ge(scan_done, FROM + m + 1)
                    v_.tensor_tensor(prob[s][0:n, 0:w], S[s][0:n, 0:w], prob[s][0:n, 0:w], ALU.subtract).then_inc(arg_done, 1)
                else:
                    dve.wait_ge(exp_done, FROM + m + 1)
                    v_.reciprocal(rr[0:n, s:s + 1], rs[0:n, s:s + 1]).then_inc(rcp_done, 1)
                    dve.wait_ge(rcp_done, FROM + m + 1)
                    v_.tensor_scalar(prob[s][0:n, 0:w], prob[s][0:n, 0:w], rr[0:n, s:s + 1], None, ALU.mult).then_inc(prob_ready, 1)

            with dve.Fori(0, 4) as p:
                if fox:
                    dve.wait_ge(pv_done, FROM + p * UNITS)
                    for h in range(2):
                        v_.tensor_scalar(fk[:, h, :], src["fk_all"][:], src["onehot"][:, ds(2 * p + h, 1)], None,
                                         ALU.mult).then_inc(staged, 1)
                top(p, 0)
                finish(p, 0)
                for u in range(UNITS):
                    if u + 1 < UNITS:
                        top(p, u + 1)
                    copy_group(dve, p, u, 1)
                    if u + 1 < UNITS:
                        finish(p, u + 1)


def index_scores(nc, dram, consts, src):
    with Phase(nc, "index") as ph:
        sb, sem = ph.sb, ph.sem
        work = [sb(f"work{s}", [P, SEQ]) for s in range(2)]
        relu = [sb(f"relu{s}", [P, SEQ]) for s in range(2)]
        best = sb("best", [P, 8])
        S = [ph.ps(f"s{s}", (P, SEQ)) for s in range(2)]
        s_ready, relu_done, acc_done, step, passed = sem("s_ready"), sem("relu_done"), sem("acc_done"), sem("step"), sem("passed")
        block = ph.block()
        H = 8
        qiT, kiT, wi, bias, at = src["qiT"], src["kiT"], src["wi"], src["bias"], src["bias_at"]

        @block.tensor
        def _(pe):
            for t in range(TILES):
                w, k0 = key_tile(t)
                n = queries(t)
                for h in range(H):
                    u = t * H + h
                    if u >= 2:
                        pe.wait_ge(relu_done, FROM + u - 1)
                    hp = slice(32 * (h % 4), 32 * (h % 4) + 32)
                    for c0 in range(0, w, 512):
                        cw = min(512, w - c0)
                        last = nc.tensor.matmul(S[u % 2][0:n, c0:c0 + cw], qiT[hp, h // 4, t * P:t * P + n],
                                                kiT[hp, k0 + c0:k0 + c0 + cw], start=True, stop=True)
                    last.then_inc(s_ready, 1)

        @block.scalar
        def _(act):
            for t in range(TILES):
                w, n = key_tile(t)[0], queries(t)
                for h in range(H):
                    u = t * H + h
                    act.wait_ge(s_ready, FROM + u + 1)
                    if u >= 2:
                        act.wait_ge(acc_done, FROM + u - 1)
                    nc.scalar.activation(relu[u % 2][0:n, 0:w], S[u % 2][0:n, 0:w], ACT.Relu).then_inc(relu_done, 1)

        @block.vector
        def _(dve):
            v = nc.vector
            steps = 0
            v.memset(bias[DEC:P, at[NT]:at[NT] + key_tile(NT)[0]], 0.0)
            for t in range(TILES):
                w, n = key_tile(t)[0], queries(t)
                wk = work[t % 2][0:n, 0:w]
                for h in range(H):
                    u = t * H + h
                    dve.wait_ge(relu_done, FROM + u + 1)
                    if h == 0:
                        v.tensor_scalar(wk, relu[u % 2][0:n, 0:w], wi[0:n, t, h:h + 1], None, ALU.mult).then_inc(acc_done, 1)
                    else:
                        dve.wait_ge(acc_done, FROM + u)
                        v.scalar_tensor_tensor(wk, relu[u % 2][0:n, 0:w], wi[0:n, t, h:h + 1], wk, ALU.mult, ALU.add).then_inc(acc_done, 1)
                dve.wait_ge(acc_done, FROM + (t + 1) * H)
                b = bias[0:n, at[t]:at[t] + w]
                if t < NT:
                    v.memset(work[t % 2][0:P // 2, w - P // 2:w], -3.0e38).then_inc(step, 1)
                    steps += 1
                    dve.wait_ge(step, FROM + steps)
                topk = TOPK_P if t < NT else TOPK_S
                if w <= topk:
                    v.tensor_scalar(b, wk, -2.9e38, NEG, ALU.is_lt, ALU.mult).then_inc(step, 1)
                    steps += 1
                    continue
                with dve.Fori(0, topk // 8) as j:
                    dve.wait_ge(step, FROM + steps + 2 * j)
                    dve.sem_inc(passed, 1)
                    v.max(best[0:n, :], wk).then_inc(step, 1)
                    dve.wait_ge(step, FROM + steps + 2 * j + 1)
                    dve.sem_inc(passed, 1)
                    v.match_replace(wk, best[0:n, :], wk, GONE).then_inc(step, 1)
                steps += 2 * (topk // 8)
                dve.wait_ge(step, FROM + steps)
                v.tensor_scalar(b, wk, -3.2e38, NEG, ALU.is_gt, ALU.mult).then_inc(step, 1)
                steps += 1


def forget(nc, dram, consts, fc, dst, out):
    with Phase(nc, "forget") as ph:
        sb, sem = ph.sb, ph.sem
        bf = sb("bf", [P, 8])
        u = sb("u", [P, KT, 8])
        e = sb("e", [P, KT, 8])
        lf = sb("lf", [P, KT, 40])
        lfT = sb("lfT", [40, KEYS])
        cum = sb("cum", [40, KEYS])
        tp = [ph.ps(f"tp{b}") for b in range(3)]
        b_in, c_in, dstep, astep, tp_ready, tp_out, stored = (sem("b_in"), sem("c_in"), sem("dstep"), sem("astep"),
                                                              sem("tp_ready"), sem("tp_out"), sem("stored"))
        ident = consts["ident"]
        block = ph.block()

        @block.sync
        def _(sp):
            sp.dma_start(bf[:], dram["b_forget"][0:1, :].to_broadcast([P, 8])).then_inc(b_in, 16)
            sp.wait_ge(dstep, FROM + 8)
            for b in range(2):
                for c in (0, 32):
                    sp.dma_start(lf[:, NT + b, c:c + 8], dram["cache_c_logf"][0, 0, b * P:(b + 1) * P]).then_inc(c_in, 16)
            sp.dma_start(out["p_c_logf"].rearrange("(t p) h -> p t h", p=P), lf[:, 0:NT, 0:8]).then_inc(stored, 16)
            sp.dma_start(out["s_c_logf"], lf[0:DEC, KT - 1, 0:8]).then_inc(stored, 16)
            sp.wait_ge(stored, FROM + 32)

        @block.vector
        def _(dve):
            v = nc.vector
            v.memset(lf[:], 0.0).then_inc(dstep, 1)
            v.memset(dst["fk_all"][:], 0.0).then_inc(dstep, 1)
            v.memset(dst["fq"][:], 0.0).then_inc(dstep, 1)
            dve.wait_ge(b_in, FROM + 16)
            v.tensor_tensor(u[:], fc[:], bf[:].unsqueeze(1).to_broadcast([P, KT, 8]), ALU.add).then_inc(dstep, 1)
            dve.wait_ge(dstep, FROM + 4)
            dve.wait_ge(astep, FROM + 3)
            v.scalar_tensor_tensor(u[:], u[:], 0.0, e[:], ALU.min, ALU.subtract).then_inc(dstep, 1)
            dve.wait_ge(dstep, FROM + 5)
            v.tensor_copy(lf[:, 0:NT, 0:8], u[:, 0:NT]).then_inc(dstep, 1)
            v.tensor_copy(lf[0:DEC, KT - 1, 0:8], u[0:DEC, KT - 1]).then_inc(dstep, 1)
            v.tensor_copy(lf[:, 0:NT, 32:40], u[:, 0:NT])
            v.tensor_copy(lf[0:DEC, KT - 1, 32:40], u[0:DEC, KT - 1]).then_inc(dstep, 1)
            dve.wait_ge(tp_out, FROM + 3)
            for c0, c1 in ((0, SEQ), (SEQ, KEYS)):
                for r in (slice(0, 8), slice(32, 40)):
                    a = lfT[r, c0:c1]
                    v.tensor_tensor_scan(cum[r, c0:c1], a, a, 0.0, ALU.add, ALU.bypass).then_inc(dstep, 1)
            dve.wait_ge(dstep, FROM + 12)
            v.tensor_scalar(dst["fk_all"][0:8, :], cum[0:8, :], -1.0, None, ALU.mult)
            v.memset(dst["fk_all"][32:40, :], 1.0)
            v.memset(dst["fq"][0:8, :], 1.0)
            v.tensor_copy(dst["fq"][32:40, 0:SEQ], cum[32:40, 0:SEQ])
            v.tensor_copy(dst["fq"][32:40, SEQ:TOK], cum[32:40, OWN:KEYS]).then_inc(dstep, 1)
            v.tensor_copy(dst["onehot"][:, :], ident[:, 0:8]).then_inc(dstep, 1)
            dve.wait_ge(dstep, FROM + 14)
            v.tensor_copy(dst["onehot"][32:40, :], ident[32:40, 32:40]).then_inc(dstep, 1)

        @block.scalar
        def _(act):
            s = nc.scalar
            act.wait_ge(dstep, FROM + 4)
            s.activation(e[:], u[:], ACT.Abs).then_inc(astep, 1)
            act.wait_ge(astep, FROM + 1)
            s.activation(e[:], e[:], ACT.Exp, scale=-1.0).then_inc(astep, 1)
            act.wait_ge(astep, FROM + 2)
            s.activation(e[:], e[:], ACT.Ln, bias=1.0).then_inc(astep, 1)
            for b in range(3):
                act.wait_ge(tp_ready, FROM + b + 1)
                c0, c1 = b * 512, min(b * 512 + 512, KEYS)
                s.activation(lfT[:, c0:c1], tp[b][0:40, 0:c1 - c0], ACT.Copy).then_inc(tp_out, 1)

        @block.tensor
        def _(pe):
            pe.wait_ge(c_in, FROM + 64)
            for b in range(3):
                for i in range(4 * b, min(4 * b + 4, KT)):
                    r = DEC if i == KT - 1 else P
                    last = nc.tensor.transpose(tp[b][0:40, (i % 4) * P:(i % 4) * P + r], lf[0:r, i, :], ident[0:r, 0:r])
                last.then_inc(tp_ready, 1)


def output_projection(nc, dram, consts, layer, even, w_dram, x_src, xres, hT):
    with Phase(nc, f"out_{layer}") as ph:
        sb, sem = ph.sb, ph.sem
        whi = sb("whi", [P, KD, D], F32R)
        wlo = sb("wlo", [P, KD, D], F32R)
        wraw = sb("wraw", [P, 2, D])
        a = sb("a", [P, KD, P])
        ahi = sb("ahi", [P, KD, P], F32R)
        alo = sb("alo", [P, KD, P], F32R)
        x = sb("x", [P, D])
        norm = Norm(ph, nc, consts, None, x[:], dram["g_ffn"][layer])
        mm = [ph.ps(f"mm{g}") for g in range(2)]
        w_in = [sem("w_in0"), sem("w_in1")]
        w_hi, w_lo, a_in, x_in = sem("w_hi"), sem("w_lo"), sem("a_in"), sem("x_in")
        a_hi, a_lo, mm_ready, added, kept, padded = (sem("a_hi"), sem("a_lo"), sem("mm_ready"), sem("added"),
                                                     sem("kept"), sem("padded"))
        block = ph.block()

        def tiles(eng):
            with eng.Fori(0, NT) as i:
                yield i, False
            yield NT, True

        @block.sync
        def _(sp):
            for k in range(KD):
                if k >= 2:
                    sp.wait_ge(w_lo, FROM + k - 1)
                if even and k < 4:
                    for h in range(2):
                        r0 = (k + 4 * h) * HD
                        sp.dma_start(wraw[h * HD:(h + 1) * HD, k % 2, :], w_dram[r0:r0 + HD, :]).then_inc(w_in[k % 2], 16)
                else:
                    sp.dma_start(wraw[0:HD, k % 2, :], w_dram[k * P:k * P + HD, :]).then_inc(w_in[k % 2], 16)
                    sp.dma_start(wraw[HD:P, k % 2, :], w_dram[k * P + HD:(k + 1) * P, :]).then_inc(w_in[k % 2], 16)
            norm.load_g(sp)
            for i, tail in tiles(sp):
                n = DEC if tail else P
                sp.wait_ge(a_lo, FROM + i)
                if tail:
                    sp.dma_start(a[:, :, 0:n], dram["att"][:, :, SEQ:TOK].rearrange("c p t -> p c t")).then_inc(a_in, 16)
                else:
                    sp.dma_start(a[:], dram["att"][:, :, ds(i * P, P)].rearrange("c p t -> p c t")).then_inc(a_in, 16)
                sp.wait_ge(norm.hn_ready, FROM + i)
                sp.wait_ge(kept, FROM + i)
                if tail:
                    sp.dma_start(x[0:n, :], x_src[1]).then_inc(x_in, 16)
                else:
                    sp.dma_start(x[:], rows(x_src[0], i * P, P)).then_inc(x_in, 16)

        @block.scalar
        def _(act):
            s = nc.scalar
            for k in range(KD):
                act.wait_ge(w_in[k % 2], FROM + 32 * (k // 2 + 1))
                s.activation(whi[:, k, :], wraw[:, k % 2, :], ACT.Copy).then_inc(w_hi, 1)
            for i, tail in tiles(act):
                n = DEC if tail else P
                act.wait_ge(a_in, FROM + 16 * i + 16)
                act.wait_ge(mm_ready, FROM + 2 * i)
                s.activation(ahi[:], a[:], ACT.Copy).then_inc(a_hi, 1)
                norm.act_square(act, i, added, 2 * i + 2)
                s.activation(one(xres, i), x[:], ACT.Copy).then_inc(kept, 1)
                norm.act_sqrt(act, i)
                q = ds(i * P, n) if not tail else slice(SEQ, TOK)
                norm.act_hi(act, i, [hT[0][:, 0:4, q], hT[0][:, 4:8, q]], n)

        @block.vector
        def _(dve):
            v = nc.vector
            for k in range(KD):
                dve.wait_ge(w_hi, FROM + k + 1)
                v.tensor_tensor(wlo[:, k, :], wraw[:, k % 2, :], whi[:, k, :].bitcast(F32), ALU.subtract).then_inc(w_lo, 1)
            dve.wait_ge(norm.g_in, FROM + 16)
            for i, tail in tiles(dve):
                n = DEC if tail else P
                dve.wait_ge(a_hi, FROM + i + 1)
                dve.wait_ge(mm_ready, FROM + 2 * i)
                v.tensor_tensor(alo[:], a[:], ahi[:].bitcast(F32), ALU.subtract).then_inc(a_lo, 1)
                dve.wait_ge(x_in, FROM + 16 * i + 16)
                for g in range(2):
                    dve.wait_ge(mm_ready, FROM + 2 * i + g + 1)
                    v.tensor_tensor(x[:, g * 512:(g + 1) * 512], mm[g][:], x[:, g * 512:(g + 1) * 512], ALU.add).then_inc(added, 1)
                norm.dve_norm(dve, i)
                norm.dve_scale_g(dve, i)
                q = ds(i * P, n) if not tail else slice(SEQ, TOK)
                norm.dve_lo(dve, i, [hT[0][:, 0:4, q], hT[0][:, 4:8, q]], [hT[1][:, 0:4, q], hT[1][:, 4:8, q]], n)

        @block.tensor
        def _(pe):
            pe.wait_ge(w_lo, FROM + KD)
            for i, tail in tiles(pe):
                pe.wait_ge(a_lo, FROM + i + 1)
                pe.wait_ge(added, FROM + 2 * i)
                for g in range(2):
                    c = slice(g * 512, (g + 1) * 512)
                    for k in range(KD):
                        last = three_passes(nc, mm[g][:], (ahi[:, k, :], alo[:, k, :]), (whi[:, k, c], wlo[:, k, c]),
                                            k == 0, k == KD - 1)
                    last.then_inc(mm_ready, 1)
                norm.pe_transposes(pe, i)


def one_col(m):
    return slice(m, m + 1) if isinstance(m, int) else ds(m, 1)


TB = [(0, 384), (384, 384), (768, 320)]
CW = 2 + SEQ + 2 + DEC
NG = NF // 2


def conv_ffn(nc, dram, consts, layer, xres, hT, out, x_next):
    wup, wdn = dram["w_up"][layer], dram["w_down"][layer]
    last_layer = x_next is None
    with Phase(nc, f"ffn_{layer}") as ph:
        sb, sem = ph.sb, ph.sem
        uhi = [sb(f"uhi{c}", [P, 2, KD, P], F32R) for c in range(2)]
        ulo = [sb(f"ulo{c}", [P, 2, KD, P], F32R) for c in range(2)]
        dhi = sb("dhi", [P, 2, D], F32R)
        dlo = sb("dlo", [P, 2, D], F32R)
        uraw = sb("uraw", [P, 2, KD, P])
        draw = sb("draw", [P, 2, D])
        G = sb("G", [P, CW])
        cv = sb("cv", [P, 2, 384])
        ahi = sb("ahi", [P, 2, NT * P + P], F32R)
        alo = sb("alo", [P, 2, NT * P + P], F32R)
        rowbuf = cv[:].rearrange("p a n -> p (a n)")[:, 0:2 * P]
        ctap = sb("ctap", [P, 2, 4])
        tap = sb("tap", [P, 4 * NF])
        st = sb("st", [P, 2 * NF])
        tail = sb("tail", [P, 4, NF])
        up = [ph.ps(f"up{j}") for j in range(4)]
        dn = [ph.ps(f"dn{j}") for j in range(4)]
        uraw_in, u_hi, u_lo, draw_in, d_hi, d_lo = (sem("uraw_in"), sem("u_hi"), sem("u_lo"), sem("draw_in"),
                                                   sem("d_hi"), sem("d_lo"))
        tap_in, tap_tp, tap_ready, tail_ready, tail_tp, tail_out, state_out = (
            sem("tap_in"), sem("tap_tp"), sem("tap_ready"), sem("tail_ready"), sem("tail_tp"), sem("tail_out"), sem("state_out"))
        up_ready, g_out = sem("up_ready"), sem("g_out")
        c0_done, c1_done, c2_done, silu_done, a_done, ahi_done, alo_done = (
            sem("c0"), sem("c1"), sem("c2"), sem("silu"), sem("a_done"), sem("ahi_done"), sem("alo_done"))
        ctap_set = sem("ctap_set")
        dn_ready, dn_added, started, seam = sem("dn_ready"), sem("dn_added"), sem("started"), sem("seam")
        block = ph.block()
        wupv = wup.rearrange("(k p) (s f) -> p s k f", p=P, s=2)
        SEAM = 2 + SEQ

        def gcols(b):
            t0, n = TB[b]
            if t0 + n <= SEQ:
                return [(2 + t0, t0, n)]
            return [(2 + t0, t0, SEQ - t0), (SEAM + 2, SEQ, DEC)]

        @block.sync
        def _(sp):
            for j in range(3):
                sp.dma_start(rowbuf[j * NF:(j + 1) * NF, 0:P],
                             dram["w_conv"][layer, j].rearrange("(c p) -> c p", p=P)).then_inc(tap_in, 16)
            sp.dma_start(rowbuf[3 * NF:4 * NF, 0:P], dram["b_conv"][layer].rearrange("(c p) -> c p", p=P)).then_inc(tap_in, 16)
            for j in range(2):
                sp.dma_start(rowbuf[j * NF:(j + 1) * NF, P:2 * P],
                             dram["state_ffn_conv"][layer, 0, j].rearrange("(c p) -> c p", p=P)).then_inc(tap_in, 16)
            with sp.Fori(0, NG) as i:
                for c in range(2):
                    f = (2 * i + c) * P
                    sp.wait_ge(u_lo, FROM + 2 * i + c)
                    for s in range(2):
                        sp.dma_start(uraw[:, s], wupv[:, s, :, ds(f, P)]).then_inc(uraw_in, 16)
                    if c == 0:
                        sp.wait_ge(d_lo, FROM + i)
                        sp.dma_start(draw[:], wdn[ds(f, 2 * P), :].rearrange("(c p) n -> p c n", p=P)).then_inc(draw_in, 16)
            sp.wait_ge(tail_out, FROM + 1)
            for g, name in ((0, "p_conv"), (1, "s_conv")):
                for j in range(2):
                    r0 = (2 * g + j) * NF
                    sp.dma_start(out[name][layer, j].rearrange("(c p) -> c p", p=P), rowbuf[r0:r0 + NF, 0:P]).then_inc(state_out, 16)
            sp.wait_ge(state_out, FROM + 64)

        def upbank(c, b, s):
            return up[2 * ((3 * c + b) % 2) + s]

        def turns(eng):
            with eng.Fori(0, NG - 1) as i:
                yield i, True
            yield NG - 1, False

        @block.scalar
        def _(act):
            s = nc.scalar

            def split_up(m, c):
                act.wait_ge(uraw_in, FROM + 32 * m + 32)
                s.activation(uhi[c][:], uraw[:], ACT.Copy).then_inc(u_hi, 1)

            def split_down(i):
                act.wait_ge(draw_in, FROM + 16 * i + 16)
                act.wait_ge(dn_ready, FROM + 18 * i)
                s.activation(dhi[:], draw[:], ACT.Copy).then_inc(d_hi, 1)

            def chunk(i, c):
                for b in range(3):
                    m = 6 * i + 3 * c + b
                    n = TB[b][1]
                    if b == 0:
                        act.wait_ge(c2_done, FROM + m)
                        act.wait_ge(tail_ready, FROM + 2 * (2 * i + c))
                        act.wait_ge(seam, FROM + 2 * i + c + 1)
                    act.wait_ge(up_ready, FROM + m + 1)
                    for g0, t0, w in gcols(b):
                        j = t0 - TB[b][0]
                        s.activation(G[:, g0:g0 + w], upbank(c, b, 0)[:, j:j + w], ACT.Copy).then_inc(g_out, 1)
                    act.wait_ge(g_out, FROM + 8 * i + 4 * c + (b + 1 if b < 2 else 4))
                    act.wait_ge(silu_done, FROM + m)
                    for g0, t0, w in gcols(b):
                        j = t0 - TB[b][0]
                        last = s.activation(cv[:, 0, j:j + w], G[:, g0 - 2:g0 - 2 + w], ACT.Identity,
                                            scale=ctap[:, c, 0:1], bias=ctap[:, c, 3:4])
                    last.then_inc(c0_done, 1)
                    act.wait_ge(c2_done, FROM + m + 1)
                    act.wait_ge(alo_done, FROM + m)
                    s.activation(cv[:, 1, 0:n], cv[:, 0, 0:n], ACT.Silu).then_inc(silu_done, 1)
                    act.wait_ge(a_done, FROM + m + 1)
                    act.wait_ge(dn_ready, FROM + 18 * i)
                    t0 = TB[b][0]
                    s.activation(ahi[:, c, t0:t0 + n], cv[:, 1, 0:n], ACT.Copy).then_inc(ahi_done, 1)

            split_up(0, 0)
            split_up(1, 1)
            split_down(0)
            act.wait_ge(tap_ready, FROM + 2)
            for i, more in turns(act):
                for c in range(2):
                    chunk(i, c)
                    if more:
                        split_up(2 * i + 2 + c, c)
                if more:
                    split_down(i + 1)

        @block.vector
        def _(dve):
            v = nc.vector

            def split_up(m, c):
                dve.wait_ge(u_hi, FROM + m + 1)
                v.tensor_tensor(ulo[c][:].rearrange("p s k f -> p (s k f)"), uraw[:].rearrange("p s k f -> p (s k f)"),
                                uhi[c][:].rearrange("p s k f -> p (s k f)").bitcast(F32), ALU.subtract).then_inc(u_lo, 1)

            def split_down(i):
                dve.wait_ge(d_hi, FROM + i + 1)
                v.tensor_tensor(dlo[:], draw[:], dhi[:].bitcast(F32), ALU.subtract).then_inc(d_lo, 1)

            def chunk(i, c):
                dve.wait_ge(c2_done, FROM + 6 * i + 3 * c)
                m = 2 * i + c
                v.tensor_copy(ctap[:, c, :], tap[:].rearrange("p (j c) -> p j c", j=4)[:, :, one_col(m)]).then_inc(ctap_set, 1)
                dve.wait_ge(ctap_set, FROM + m + 1)
                v.tensor_copy(G[:, SEAM:SEAM + 2], st[:].rearrange("p (j c) -> p j c", j=2)[:, :, one_col(m)]).then_inc(seam, 1)
                for b in range(3):
                    m = 6 * i + 3 * c + b
                    t0, n0 = TB[b]
                    dve.wait_ge(c0_done, FROM + m + 1)
                    for tapno, done in ((1, c1_done), (2, c2_done)):
                        if tapno == 2:
                            dve.wait_ge(c1_done, FROM + m + 1)
                        for g0, t1, w in gcols(b):
                            j = t1 - t0
                            last = v.scalar_tensor_tensor(cv[:, 0, j:j + w], G[:, g0 - 2 + tapno:g0 - 2 + tapno + w],
                                                          ctap[:, c, tapno:tapno + 1], cv[:, 0, j:j + w], ALU.mult, ALU.add)
                        last.then_inc(done, 1)
                    if b == 2:
                        for g, col in ((0, SEAM - 2), (1, CW - 2)):
                            v.tensor_copy(tail[:, 2 * g:2 * g + 2, one_col(2 * i + c)], G[:, col:col + 2]).then_inc(tail_ready, 1)
                    dve.wait_ge(silu_done, FROM + m + 1)
                    v.tensor_tensor(cv[:, 1, 0:n0], upbank(c, b, 1)[:, 0:n0], cv[:, 1, 0:n0], ALU.mult).then_inc(a_done, 1)
                    dve.wait_ge(ahi_done, FROM + m + 1)
                    v.tensor_tensor(alo[:, c, t0:t0 + n0], cv[:, 1, 0:n0], ahi[:, c, t0:t0 + n0].bitcast(F32),
                                    ALU.subtract).then_inc(alo_done, 1)

            v.memset(G[:, 0:2], 0.0).then_inc(started, 1)
            v.memset(ahi[:, :, TOK:].bitcast(F32), 0.0).then_inc(started, 1)
            v.memset(alo[:, :, TOK:].bitcast(F32), 0.0).then_inc(started, 1)
            dve.wait_ge(started, FROM + 3)
            split_up(0, 0)
            split_up(1, 1)
            split_down(0)
            for b, (dst, n) in enumerate(((tap, 4 * NF), (st, 2 * NF))):
                dve.wait_ge(tap_tp, FROM + b + 1)
                v.tensor_copy(dst[:], dn[b][:, 0:n]).then_inc(tap_ready, 1)
            dve.wait_ge(tap_ready, FROM + 2)
            for i, more in turns(dve):
                for c in range(2):
                    chunk(i, c)
                    if more:
                        split_up(2 * i + 2 + c, c)
                for t in range(TILES):
                    for g in range(2):
                        j, n = 2 * t + g, queries(t)
                        dve.wait_ge(dn_ready, FROM + 18 * i + j + 1)
                        xs = xres[0:n, t, g * 512:(g + 1) * 512]
                        v.tensor_tensor(xs, dn[j % 4][0:n, :], xs, ALU.add).then_inc(dn_added, 1)
                if more:
                    split_down(i + 1)
            dve.wait_ge(tail_tp, FROM + 1)
            v.tensor_copy(rowbuf[0:4 * NF, 0:P], up[0][0:4 * NF, 0:P]).then_inc(tail_out, 1)

        @block.tensor
        def _(pe):
            pe.wait_ge(tap_in, FROM + 96)
            for b, n in enumerate((4 * NF, 2 * NF)):
                nc.tensor.transpose(dn[b][:, 0:n], rowbuf[0:n, b * P:(b + 1) * P], consts["ident"][0:n, 0:n]).then_inc(tap_tp, 1)
            pe.wait_ge(tap_ready, FROM + 2)
            with pe.Fori(0, NG) as i:
                for c in range(2):
                    pe.wait_ge(u_lo, FROM + 2 * i + c + 1)
                    for b, (t0, n) in enumerate(TB):
                        if 3 * c + b >= 2:
                            pe.wait_ge(a_done, FROM + 6 * i + 3 * c + b - 1)
                        for s in range(2):
                            for k in range(KD):
                                last = three_passes(nc, upbank(c, b, s)[:, 0:n],
                                                    (uhi[c][:, s, k, :], ulo[c][:, s, k, :]),
                                                    (hT[0][:, k, t0:t0 + n], hT[1][:, k, t0:t0 + n]), k == 0, k == KD - 1)
                        last.then_inc(up_ready, 1)
                pe.wait_ge(d_lo, FROM + i + 1)
                pe.wait_ge(started, FROM + 3)
                for t in range(TILES):
                    pe.wait_ge(alo_done, FROM + 6 * i + 3 + min(2, ((t + 1) * P - 1) // 384) + 1)
                    for g in range(2):
                        j = 2 * t + g
                        pe.wait_ge(dn_added, FROM + 18 * i + max(0, j - 3))
                        for c in range(2):
                            last = three_passes(nc, dn[j % 4][:], (ahi[:, c, t * P:(t + 1) * P], alo[:, c, t * P:(t + 1) * P]),
                                                (dhi[:, c, g * 512:(g + 1) * 512], dlo[:, c, g * 512:(g + 1) * 512]), c == 0, c == 1)
                        last.then_inc(dn_ready, 1)
            pe.wait_ge(tail_ready, FROM + 2 * NF)
            nc.tensor.transpose(up[0][0:4 * NF, 0:P], tail[:].rearrange("p j c -> p (j c)"), consts["ident"][:]).then_inc(tail_tp, 1)

    if not last_layer:
        with Phase(nc, f"keep_{layer}") as ph:
            done = ph.sem("done")
            block = ph.block()

            @block.sync
            def _(sp):
                sp.dma_start(x_next[0].rearrange("(t p) n -> p t n", p=P), xres[:, 0:NT, :]).then_inc(done, 16)
                sp.dma_start(x_next[1], xres[0:DEC, NT, :]).then_inc(done, 16)
                sp.wait_ge(done, FROM + 32)


def final_norm(nc, dram, xres, out):
    with Phase(nc, "final") as ph:
        sb, sem = ph.sb, ph.sem
        g = sb("g", [P, D])
        junk = sb("junk", [P, D])
        y = sb("y", [P, 2, D])
        st = sb("st", [P, 4, TILES])
        g_in, sq, step, rt, y_ready, stored = sem("g_in"), sem("sq"), sem("step"), sem("rt"), sem("y_ready"), [sem("stored0"), sem("stored1")]
        block = ph.block()

        @block.sync
        def _(sp):
            sp.dma_start(g[:], dram["g_final"].unsqueeze(0).to_broadcast([P, D])).then_inc(g_in, 16)
            for t in range(TILES):
                sp.wait_ge(y_ready, FROM + t + 1)
                n = queries(t)
                dst = out["y_sample"] if t == NT else out["y_prompt"][t * P:(t + 1) * P]
                sp.dma_start(dst, y[0:n, t % 2, :]).then_inc(stored[t % 2], 16)
            sp.wait_ge(stored[0], FROM + 16 * ((TILES + 1) // 2))
            sp.wait_ge(stored[1], FROM + 16 * (TILES // 2))

        @block.scalar
        def _(act):
            for t in range(TILES):
                n = queries(t)
                if t:
                    act.wait_ge(sq, FROM + t)
                nc.scalar.activation(junk[0:n, :], xres[0:n, t, :], ACT.Square, accum_out=st[0:n, 0, t:t + 1]).then_inc(sq, 1)
            act.wait_ge(step, FROM + 2)
            nc.scalar.activation(st[:, 2, :], st[:, 1, :], ACT.Sqrt).then_inc(rt, 1)

        @block.vector
        def _(dve):
            v = nc.vector
            v.memset(st[DEC:P, 0, NT:NT + 1], 1.0).then_inc(step, 1)
            dve.wait_ge(step, FROM + 1)
            dve.wait_ge(sq, FROM + TILES)
            v.tensor_scalar(st[:, 1, :], st[:, 0, :], 1.0 / D, EPS, ALU.mult, ALU.add).then_inc(step, 1)
            dve.wait_ge(rt, FROM + 1)
            v.reciprocal(st[:, 3, :], st[:, 2, :]).then_inc(step, 1)
            dve.wait_ge(step, FROM + 3)
            dve.wait_ge(g_in, FROM + 16)
            for t in range(TILES):
                n = queries(t)
                if t >= 2:
                    dve.wait_ge(stored[t % 2], FROM + 16 * (t // 2))
                v.scalar_tensor_tensor(y[0:n, t % 2, :], xres[0:n, t, :], st[0:n, 3, t:t + 1], g[0:n, :], ALU.mult,
                                       ALU.mult).then_inc(y_ready, 1)


def hybrid_step(nc, dram, out):
    with ExitStack() as ctx:
        def sb(name, shape, dt=F32):
            return ctx.enter_context(nc.sbuf_tensor(name, shape, dt))

        ident, ident_bf = sb("ident", [P, P]), sb("ident_bf", [P, P], BF16)
        masks = {n: sb(n, [P, P], BF16) for n in ("mask_chunk", "mask_causal", "mask_strict")}
        consts = {"ident": ident, "ident_bf": ident_bf, **masks}

        with Phase(nc, "start") as ph:
            raw = ph.sb("raw", [P, 3, P])
            got, done = ph.sem("got"), ph.sem("done")
            block = ph.block()

            @block.sync
            def _(sp):
                sp.dma_start(ident[:], dram["patterns"][0]).then_inc(got, 16)
                for j in range(3):
                    sp.dma_start(raw[:, j, :], dram["patterns"][1 + j]).then_inc(got, 16)

            @block.vector
            def _(dve):
                dve.wait_ge(got, FROM + 64)
                nc.vector.tensor_copy(ident_bf[:], ident[:])
                for j, m in enumerate(("mask_chunk", "mask_causal", "mask_strict")):
                    nc.vector.tensor_scalar(masks[m][:], raw[:, j, :], NEG, None, ALU.mult)

        x0 = (dram["x_prompt"][0], dram["x_sample"][0])
        with ExitStack() as even:
            def esb(name, shape, dt=F32):
                return even.enter_context(nc.sbuf_tensor(name, shape, dt))

            widths = [key_tile(t)[0] for t in range(TILES)]
            src = {"qaT": esb("qaT", [P, 4, TOK]), "kaT": esb("kaT", [P, KEYS]), "v": esb("va", [P, KT, P]),
                   "qiT": esb("qiT", [P, 2, TOK]), "kiT": esb("kiT", [P, KEYS]), "wi": esb("wi", [P, TILES, 8]),
                   "latT": esb("latT", [P, KEYS]), "krT": esb("krT", [96, KEYS]),
                   "bias_at": [sum(widths[:t]) for t in range(TILES)]}
            projection(nc, dram, consts, "even", x0, dram["g_mix"][0], dram["w_in_even"][0], src, out)
            src["bias"] = esb("bias", [P, sum(widths)], BF16)
            index_scores(nc, dram, consts, src)
            attention(nc, dram, consts, "a", src, 0)
            attention(nc, dram, consts, "b", src, 4)

        with ExitStack() as ff:
            xres = ff.enter_context(nc.sbuf_tensor("xres", [P, TILES, D], F32))
            hT = [ff.enter_context(nc.sbuf_tensor(f"hT{j}", [P, KD, TOK], F32R)) for j in range(2)]
            output_projection(nc, dram, consts, 0, True, dram["w_o_even"][0], x0, xres, hT)
            x1 = (dram["x1"][0:SEQ], dram["x1"][SEQ:TOK])
            conv_ffn(nc, dram, consts, 0, xres, hT, out, x1)

        for kind, c0, w, chunk0 in (("c", 0, C_IN, 0), ("d", C_IN, D_IN, 4)):
            with ExitStack() as odd:
                def osb(name, shape, dt=F32):
                    return odd.enter_context(nc.sbuf_tensor(f"{kind}_{name}", shape, dt))

                src = {"qT": osb("qT", [P, 4, TOK]), "kT": osb("kT", [P, 4, KEYS]), "v": osb("v", [P, KT, 512])}
                if kind == "c":
                    src["fc"] = osb("fc", [P, KT, 8])
                projection(nc, dram, consts, kind, x1, dram["g_mix"][1], dram["w_in_odd"][0][:, c0:c0 + w], src, out)
                if kind == "c":
                    src.update(fq=osb("fq", [P, TOK]), fk_all=osb("fk_all", [P, KEYS]), onehot=osb("onehot", [P, 8]))
                    forget(nc, dram, consts, src["fc"], src, out)
                attention(nc, dram, consts, kind, src, chunk0)

        with ExitStack() as ff:
            xres = ff.enter_context(nc.sbuf_tensor("xres_1", [P, TILES, D], F32))
            hT = [ff.enter_context(nc.sbuf_tensor(f"hT{j}_1", [P, KD, TOK], F32R)) for j in range(2)]
            output_projection(nc, dram, consts, 1, False, dram["w_o_odd"][0], x1, xres, hT)
            conv_ffn(nc, dram, consts, 1, xres, hT, out, None)
            final_norm(nc, dram, xres, out)


_INS = ["x_prompt", "x_sample", "cache_a_k", "cache_a_v", "cache_a_idx_k", "cache_b_latent", "cache_b_rope",
        "cache_c_k", "cache_c_v", "cache_c_logf", "cache_d_k", "cache_d_v", "state_ffn_conv",
        "g_mix", "g_ffn", "g_final", "w_in_even", "g_b_q", "g_b_kv", "w_b_uq", "w_b_ukv", "w_o_even",
        "w_in_odd", "b_forget", "w_o_odd", "w_up", "w_conv", "b_conv", "w_down"]
_OUTS = [("y_prompt", (1, SEQ, D), (SEQ, D)), ("y_sample", (1, DEC, D), (DEC, D))] + [
    (f"{g}_{name}", (1, 1, n) + shape, (n, flat)) if name != "conv" else (f"{g}_conv", (2, 1, 2, FF), (2, 2, FF))
    for g, n in (("p", SEQ), ("s", DEC))
    for name, shape, flat in (("a_k", (2, 64), 128), ("a_v", (2, 64), 128), ("a_idx_k", (32,), 32),
                              ("b_latent", (KVR,), KVR), ("b_rope", (32,), 32), ("c_k", (8, 64), 512),
                              ("c_v", (8, 64), 512), ("c_logf", (8,), 8), ("d_k", (8, 64), 512),
                              ("d_v", (8, 64), 512), ("conv", (), 0))]


def _constants():
    import numpy as np

    f = np.float32
    pos = np.concatenate([np.arange(SEQ), PAST + np.arange(DEC), np.zeros(P - DEC)]).astype(f)
    tabs = []
    for n_rot in (16, 8, 32):
        half = n_rot // 2
        inv = f(500000.0) ** (-np.arange(half, dtype=f) * f(2.0) / f(n_rot))
        ang = pos[:, None] * inv.astype(f)[None, :]
        tabs += [np.cos(ang), np.sin(ang)]
    trig = np.concatenate(tabs, axis=1).astype(f).reshape(TILES, P, ROPE_COLS)
    i = np.arange(P)
    hidden = [np.eye(P), (i[:, None] < P // 2) & (i[None, :] >= P // 2), i[None, :] > i[:, None], i[None, :] >= i[:, None]]
    return {"trig": trig, "patterns": np.stack(hidden).astype(f)}


def kernel(**inputs):
    import numpy as _np
    import concourse.bacc as _bacc
    from concourse import mybir as _mybir
    from concourse.bass_utils import run_bass_kernel_spmd as _run

    nc = _bacc.Bacc("TRN2", target_bir_lowering=False, num_devices=1)
    arrays, dram, out = {}, {}, {}
    for name, a in [(n, _np.ascontiguousarray(inputs[n])) for n in _INS] + list(_constants().items()):
        arrays[f"in_{name}_dram"] = a
        dram[name] = nc.dram_tensor(f"in_{name}_dram", a.shape, _mybir.dt.from_np(a.dtype), kind="ExternalInput").ap()
    for name, shape, flat in _OUTS:
        out[name] = nc.dram_tensor(f"out_{name}_dram", flat, F32, kind="ExternalOutput").ap()
    for name, shape in (("qbT", (8, 96, TOK)), ("att", (KD, P, TOK)), ("x1", (TOK, D))):
        dram[name] = nc.dram_tensor(f"scratch_{name}", shape, F32, kind="Internal").ap()
    hybrid_step(nc, dram, out)
    r = _run(nc, [arrays], core_ids=[0])
    return tuple(r.results[0][f"out_{name}_dram"].reshape(shape) for name, shape, flat in _OUTS)
```

```python
from contextlib import ExitStack

import concourse.bass as bass
from concourse import mybir

F32 = mybir.dt.float32
F32R = mybir.dt.float32r
BF16 = mybir.dt.bfloat16
ALU = mybir.AluOpType
ACT = mybir.ActivationFunctionType
AX_X = mybir.AxisListType.X
ds = bass.ds

P = 128
D = 1024
KD = D // P
SEQ, DEC, PAST = 1024, 64, 256
NT = SEQ // P
TOK = SEQ + DEC
KEYS = SEQ + PAST + DEC
OWN = SEQ + PAST
KT = NT + PAST // P + 1
EPS = 1e-6
HD = 64
A_IN, C_IN, D_IN = 1480, 1544, 1536
TOPK_P, TOPK_S = 256, 80
QR, KVR = 256, 128
FF = 2816
NF = FF // P
NEG = -1.0e30
GONE = -3.4e38
ROPE_COLS = 2 * (8 + 4 + 16)
RA, RI, RB = 0, 16, 24


FROM = 1


class Phase:

    def __init__(self, nc, name):
        self.nc, self.name, self.ctx, self.sems = nc, name, ExitStack(), []

    def __enter__(self):
        self.ctx.__enter__()
        return self

    def __exit__(self, *a):
        return self.ctx.__exit__(*a)

    def sb(self, name, shape, dt=F32):
        return self.ctx.enter_context(self.nc.sbuf_tensor(f"{self.name}_{name}", shape, dt))

    def ps(self, name, shape=(P, 512), dt=F32):
        return self.ctx.enter_context(self.nc.psum_tensor(f"{self.name}_{name}", list(shape), dt))

    def sem(self, name):
        s = self.ctx.enter_context(self.nc.semaphore(f"{self.name}_{name}"))
        self.sems.append(s)
        return s

    def block(self):
        def reset(eng, share):
            for s in self.sems[share::4]:
                eng.sem_clear(s)
                eng.sem_inc(s, FROM)

        with self.nc.Block() as start:
            @start.sync
            def _(sp):
                reset(sp, 0)

            @start.tensor
            def _(pe):
                reset(pe, 1)

            @start.vector
            def _(dve):
                reset(dve, 2)

            @start.scalar
            def _(act):
                reset(act, 3)
        return self.ctx.enter_context(self.nc.Block())


def bc(ap, n):
    return ap.unsqueeze(2).to_broadcast([ap.shape[0], ap.shape[1], n])


def one(ap, i):
    if isinstance(i, int):
        return ap[:, i]
    return ap[:, ds(i, 1)].rearrange("p a n -> p (a n)")


def rows(ap, i, n):
    return ap[i:i + n] if isinstance(i, int) else ap[ds(i, n)]


def key_tile(t):
    return (P * (t + 1), 0) if t < NT else (PAST + DEC, SEQ)


class Norm:

    def __init__(self, ph, nc, consts, x, g_dram):
        self.nc, self.x = nc, x
        self.ident = consts["ident"]
        self.g_dram = g_dram
        self.junk = ph.sb("junk", [P, D], BF16)
        self.hn = ph.sb("hn", [P, D])
        self.hf = ph.sb("hf", [P, KD, P])
        self.gT = ph.sb("gT", [P, KD])
        self.eps = consts["eps"]
        self.stat = ph.sb("stat", [P, 3])
        self.tp = [ph.ps("ht0"), ph.ps("ht1")]
        self.g_in = ph.sem("g_in")
        self.ssq = ph.sem("ssq")
        self.rt = ph.sem("rt")
        self.rinv = ph.sem("rinv")
        self.hn_ready = ph.sem("hn_ready")
        self.ht_ready = ph.sem("ht_ready")
        self.hf_ready = ph.sem("hf_ready")
        self.hi_ready = ph.sem("hi_ready")
        self.lo_ready = ph.sem("lo_ready")

    def load_g(self, sp):
        sp.dma_start(self.gT[:], self.g_dram.rearrange("(k p) -> p k", p=P),
                     allow_slow_non_contiguous=True).then_inc(self.g_in, 16)

    def act_square(self, act, i, x_sem, x_val):
        act.wait_ge(x_sem, FROM + x_val)
        act.wait_ge(self.hn_ready, FROM + i)
        self.nc.scalar.activation(self.junk[:], self.x, ACT.Square, scale=D ** -0.5,
                                  accum_out=self.stat[:, 0:1]).then_inc(self.ssq, 1)

    def act_root(self, act, i):
        act.wait_ge(self.ssq, FROM + i + 1)
        self.nc.scalar.activation(self.stat[:, 1:2], self.stat[:, 0:1], ACT.Sqrt, bias=self.eps[:]).then_inc(self.rt, 1)

    def dve_norm(self, dve, i):
        v = self.nc.vector
        dve.wait_ge(self.rt, FROM + i + 1)
        v.reciprocal(self.stat[:, 2:3], self.stat[:, 1:2]).then_inc(self.rinv, 1)
        dve.wait_ge(self.rinv, FROM + i + 1)
        dve.wait_ge(self.ht_ready, FROM + i * 2)
        v.tensor_scalar(self.hn[:], self.x, self.stat[:, 2:3], None, ALU.mult).then_inc(self.hn_ready, 1)

    def pe_transposes(self, pe, i):
        pe.wait_ge(self.hn_ready, FROM + i + 1)
        pe.wait_ge(self.hf_ready, FROM + i * 2)
        for b in range(2):
            for k in range(4):
                last = self.nc.tensor.transpose(self.tp[b][:, k * P:(k + 1) * P],
                                                self.hn[:, (4 * b + k) * P:(4 * b + k + 1) * P], self.ident[:])
            last.then_inc(self.ht_ready, 1)

    def dve_scale_g(self, dve, i):
        dve.wait_ge(self.hi_ready, FROM + i * 2)
        dve.wait_ge(self.lo_ready, FROM + i * 2)
        if isinstance(i, int) and i == 0:
            dve.wait_ge(self.g_in, FROM + 16)
        for b in range(2):
            dve.wait_ge(self.ht_ready, FROM + i * 2 + b + 1)
            self.nc.vector.tensor_tensor(self.hf[:, 4 * b:4 * b + 4, :],
                                         self.tp[b][:].rearrange("p (k t) -> p k t", k=4),
                                         bc(self.gT[:, 4 * b:4 * b + 4], P), ALU.mult).then_inc(self.hf_ready, 1)

    def act_hi(self, act, i, hi, n=P):
        for b in range(2):
            act.wait_ge(self.hf_ready, FROM + i * 2 + b + 1)
            self.nc.scalar.activation(hi[b], self.hf[:, 4 * b:4 * b + 4, 0:n], ACT.Copy).then_inc(self.hi_ready, 1)

    def dve_lo(self, dve, i, hi, lo, n=P):
        for b in range(2):
            dve.wait_ge(self.hf_ready, FROM + i * 2 + b + 1)
            dve.wait_ge(self.hi_ready, FROM + i * 2 + b + 1)
            self.nc.vector.tensor_tensor(lo[b], self.hf[:, 4 * b:4 * b + 4, 0:n], hi[b].bitcast(F32),
                                         ALU.subtract).then_inc(self.lo_ready, 1)


def three_passes(nc, out, lhs, rhs, first, last):
    (lh, ll), (rh, rl) = lhs, rhs
    nc.tensor.matmul(out, lh, rh, start=first, stop=False)
    nc.tensor.matmul(out, lh, rl, start=False, stop=False)
    return nc.tensor.matmul(out, ll, rh, start=False, stop=last)


def projection(nc, dram, consts, kind, x_src, g_dram, w_dram, dst, out):
    even, fox = kind == "even", kind == "c"
    width = w_dram.shape[1]
    ng = 4 if fox else 3
    gw = [494, 494, 492] if even else [386] * 4 if fox else [512] * 3
    go = [sum(gw[:g]) for g in range(ng)]
    nw = 1 if even else 2
    ww = width // nw
    ident = consts["ident"]
    with Phase(nc, f"proj_{kind}") as ph:
        sb, sem = ph.sb, ph.sem
        whi = sb("whi", [P, KD, width], F32R)
        wlo = sb("wlo", [P, KD, width], F32R)
        wraw = sb("wraw", [P, 2, ww])
        x = sb("x", [P, D])
        hhi = [sb(f"hhi{s}", [P, KD, P], F32R) for s in range(2)]
        hlo = [sb(f"hlo{s}", [P, KD, P], F32R) for s in range(2)]
        proj = sb("proj", [P, width])
        trig = sb("trig", [P, TILES, ROPE_COLS]) if even else None
        norm = Norm(ph, nc, consts, x[:], g_dram)
        mm = [ph.ps(f"mm{g}") for g in range(ng)]
        tq = [ph.ps(f"tq{g}") for g in range(6 - ng)]
        w_in = [sem("w_in0"), sem("w_in1")]
        w_hi, w_lo = sem("w_hi"), sem("w_lo")
        x_in, trig_in = sem("x_in"), sem("trig_in")
        mm_ready, proj_act = sem("mm_ready"), sem("proj_act")
        tq_ready, tq_act, qb_tp = sem("tq_ready"), sem("tq_act"), sem("qb_tp")
        stored, cache_in, cache_tp, cache_cp = sem("stored"), sem("cache_in"), sem("cache_tp"), sem("cache_cp")
        post, dve_step, passed, kept = sem("post"), sem("dve_step"), sem("passed"), sem("kept")
        dve_rope, zeroed, rr_done = sem("dve_rope"), sem("zeroed"), sem("rr_done")
        if even:
            gq = sb("gq", [P, QR])
            gkv = sb("gkv", [P, KVR])
            wuq = sb("wuq", [P, 2, 768])
            qbT = sb("qbT", [96, 8, P])
            nst = sb("nst", [P, 6])
            free, at = wraw[:].rearrange("p s n -> p (s n)"), [0]

            def take(n):
                at[0] += n
                return free[:, at[0] - n:at[0]]

            qb = take(8 * 96).rearrange("p (h d) -> p h d", h=8)
            rot = take(4 * 10 * 16).rearrange("p (j n) -> p j n", j=4)
            cqT = take(2 * P).rearrange("p (c t) -> p c t", c=2)
            aq, cqn, lat = take(4 * P), take(QR), take(KVR)
            stage = take(P + 96)
            sq_done, rt_done = sem("sq_done"), sem("rt_done")
            cqT_ready, qb_mm, qb_cp, qbT_ready, gq_in, qbT_stored = (
                sem("cqT_ready"), sem("qb_mm"), sem("qb_cp"), sem("qbT_ready"), sem("gq_in"),
                sem("qbT_stored"))
        rows4 = norm.hn[:].rearrange("p (b c n) -> p b c n", b=2, c=4)
        if even:
            ck, ci, cl, cr = rows4[:, :, 0], rows4[:, :, 1], rows4[:, :, 2], rows4[:, :, 3, 0:96]

        nstore = 5 if even else 2
        ntq = 3 if even else 2

        def steps(eng):
            yield 0, 0
            with eng.Fori(0, (NT - 2) // 2) as j:
                yield 2 * j + 1, 1
                yield 2 * j + 2, 0
            yield NT - 1, 1
            yield NT, 0

        def is_last(i):
            return isinstance(i, int) and i == NT

        def is_first(i):
            return isinstance(i, int) and i == 0

        def span(i):
            if is_last(i):
                return DEC, slice(SEQ, TOK), slice(OWN, KEYS), KT - 1
            q = slice(i * P, (i + 1) * P) if isinstance(i, int) else ds(i * P, P)
            return P, q, q, i

        block = ph.block()

        @block.sync
        def _(sp):
            def load_w(c):
                k, w0 = c // nw, (c % nw) * ww
                if c >= 2:
                    sp.wait_ge(w_lo, FROM + c - 1)
                sp.dma_start(wraw[:, c % 2, :], w_dram[k * P:(k + 1) * P, w0:w0 + ww]).then_inc(w_in[c % 2], 16)

            def load(i):
                if not is_first(i):
                    sp.wait_ge(norm.hn_ready, FROM + i)
                if is_last(i):
                    sp.dma_start(x[0:DEC, :], x_src[1]).then_inc(x_in, 16)
                else:
                    sp.dma_start(x[:], rows(x_src[0], i * P, P)).then_inc(x_in, 16)

            def store(i):
                n, pre, r0 = (DEC, "s", 0) if is_last(i) else (P, "p", i * P)

                def put(name, src):
                    sp.dma_start(rows(out[f"{pre}_{name}"], r0, n), src).then_inc(stored, 16)

                if not even:
                    sp.wait_ge(proj_act, FROM + ng * i + ng)
                    put(f"{kind}_k", proj[0:n, 512:1024])
                    put(f"{kind}_v", proj[0:n, 1024:1536])
                    return
                sp.wait_ge(post, FROM + i + 1)
                put("a_k", proj[0:n, 512:640])
                put("a_v", proj[0:n, 640:768])
                put("a_idx_k", proj[0:n, 1024:1056])
                put("b_latent", lat[0:n, :])
                put("b_rope", proj[0:n, 1448:1480])
                sp.wait_ge(qbT_ready, FROM + 2 * i + 2)
                sp.sem_inc(passed, 1)
                sp.dma_start(dram["qbT"][:, :, span(i)[1]].rearrange("h d t -> d h t"), qbT[:, :, 0:n]).then_inc(qbT_stored, 16)

            for c in range(2):
                load_w(c)
            for b in range(2):
                r = slice(b * P, (b + 1) * P)
                if even:
                    sp.dma_start(ck[:, b], dram["cache_a_k"][0, 0, r].rearrange("t g d -> t (g d)")).then_inc(cache_in, 16)
                    sp.dma_start(dst["v"][:, NT + b, :], dram["cache_a_v"][0, 0, r].rearrange("t g d -> t (g d)")).then_inc(cache_in, 16)
                    for c in range(4):
                        sp.dma_start(ci[:, b, c * 32:c * 32 + 32], dram["cache_a_idx_k"][0, 0, r]).then_inc(cache_in, 16)
                    sp.dma_start(cl[:, b, :], dram["cache_b_latent"][0, 0, r]).then_inc(cache_in, 16)
                    sp.dma_start(cr[:, b, 64:96], dram["cache_b_rope"][0, 0, r]).then_inc(cache_in, 16)
                else:
                    sp.dma_start(rows4[:, b].rearrange("p a n -> p (a n)"),
                                 dram[f"cache_{kind}_k"][0, 0, r].rearrange("t g d -> t (g d)")).then_inc(cache_in, 16)
                    sp.dma_start(dst["v"][:, NT + b, :],
                                 dram[f"cache_{kind}_v"][0, 0, r].rearrange("t g d -> t (g d)")).then_inc(cache_in, 16)
            load(0)
            norm.load_g(sp)
            for c in range(2, KD * nw):
                load_w(c)
            if even:
                sp.dma_start(trig[:], dram["trig"].rearrange("t p n -> p t n")).then_inc(trig_in, 16)
                sp.dma_start(gq[:], dram["g_b_q"][0:1, :].to_broadcast([P, QR])).then_inc(gq_in, 16)
                sp.dma_start(gkv[:], dram["g_b_kv"][0:1, :].to_broadcast([P, KVR])).then_inc(gq_in, 16)
                sp.dma_start(wuq[:], dram["w_b_uq"][0].rearrange("(k p) n -> p k n", p=P)).then_inc(gq_in, 16)
            load(1)
            with sp.Fori(0, NT - 2) as i:
                load(i + 2)
                store(i)
            load(NT)
            for i in (NT - 2, NT - 1, NT):
                store(i)
            sp.wait_ge(stored, FROM + TILES * 16 * nstore)
            if even:
                sp.wait_ge(qbT_stored, FROM + TILES * 16)

        @block.scalar
        def _(act):
            s = nc.scalar
            s.preload_act_table_set("sqrt_and_others")

            def split_w(c):
                k, w0 = c // nw, (c % nw) * ww
                act.wait_ge(w_in[c % 2], FROM + 16 * (c // 2 + 1))
                s.activation(whi[:, k, w0:w0 + ww], wraw[:, c % 2, :], ACT.Copy).then_inc(w_hi, 1)

            def cache():
                for b in range(2):
                    act.wait_ge(cache_tp, FROM + b + 1)
                    c0 = SEQ + b * P
                    if even:
                        s.activation(dst["kaT"][:, c0:c0 + P], mm[b][:, 0:P], ACT.Copy)
                        s.activation(dst["kiT"][:, c0:c0 + P], mm[b][:, P:2 * P], ACT.Copy)
                        s.activation(dst["latT"][:, c0:c0 + P], mm[b][:, 2 * P:3 * P], ACT.Copy)
                        s.activation(dst["krT"][64:96, c0:c0 + P], mm[b][64:96, 3 * P:4 * P], ACT.Copy).then_inc(cache_cp, 1)
                    else:
                        s.activation(dst["kT"][:, :, c0:c0 + P], mm[b][:].rearrange("p (c t) -> p c t", c=4),
                                     ACT.Copy).then_inc(cache_cp, 1)

            def mean_square(i):
                norm.act_square(act, i, x_in, i * 16 + 16)
                norm.act_root(act, i)

            def high(i, slot):
                if not is_first(i):
                    act.wait_ge(mm_ready, FROM + ng * (i - 1))
                norm.act_hi(act, i, [hhi[slot][:, 0:4, :], hhi[slot][:, 4:8, :]])

            def feature_major(i):
                n, q, kk, _ = span(i)
                act.wait_ge(tq_ready, FROM + ntq * i + 1)
                s.activation(dst["qaT" if even else "qT"][:, :, q], tq[0][:].rearrange("p (c t) -> p c t", c=4)[:, :, 0:n],
                             ACT.Copy, scale=HD ** -0.5).then_inc(tq_act, 1)
                act.wait_ge(tq_ready, FROM + ntq * i + 2)
                if even:
                    s.activation(dst["kaT"][:, kk], tq[1][:, 0:n], ACT.Copy)
                    s.activation(dst["kiT"][:, kk], tq[1][:, P:P + n], ACT.Copy)
                    s.activation(dst["latT"][:, kk], tq[1][:, 2 * P:2 * P + n], ACT.Copy)
                    s.activation(dst["krT"][64:96, kk], tq[1][64:96, 3 * P:3 * P + n], ACT.Copy).then_inc(tq_act, 1)
                else:
                    s.activation(dst["kT"][:, :, kk], tq[1][:].rearrange("p (c t) -> p c t", c=4)[:, :, 0:n],
                                 ACT.Copy).then_inc(tq_act, 1)

            def up_query(i):
                for g in range(2):
                    act.wait_ge(qb_mm, FROM + 2 * i + g + 1)
                    s.activation(qb[:, 4 * g:4 * g + 4, :].rearrange("p h d -> p (h d)"), tq[g][:, 0:384],
                                 ACT.Copy).then_inc(qb_cp, 1)

            def up_query_T(i):
                for g in range(2):
                    act.wait_ge(qb_tp, FROM + 2 * i + g + 1)
                    if g == 0:
                        act.wait_ge(qbT_stored, FROM + i * 16)
                    s.activation(qbT[:, 4 * g:4 * g + 4, :], tq[g][0:96, :].rearrange("p (h t) -> p h t", h=4),
                                 ACT.Copy, scale=96 ** -0.5).then_inc(qbT_ready, 1)

            c_mid = KD * nw // 2
            split_w(0)
            split_w(1)
            cache()
            for c in range(2, c_mid):
                split_w(c)
            mean_square(0)
            high(0, 0)
            for c in range(c_mid, KD * nw):
                split_w(c)
            for i, slot in steps(act):
                if not is_last(i):
                    mean_square(i + 1)
                if not is_first(i):
                    feature_major(i - 1)
                if not is_last(i):
                    high(i + 1, 1 - slot)
                act.wait_ge(stored, FROM + i * 16 * nstore)
                act.wait_ge(tq_ready, FROM + ntq * i)
                act.wait_ge(kept, FROM + i)
                for g in range(ng):
                    act.wait_ge(mm_ready, FROM + ng * i + g + 1)
                    s.activation(proj[:, go[g]:go[g] + gw[g]], mm[g][:, 0:gw[g]], ACT.Copy).then_inc(proj_act, 1)
                    if even and g == 0 and not is_first(i):
                        up_query(i - 1)
                if even and not is_first(i):
                    up_query_T(i - 1)
                act.wait_ge(proj_act, FROM + ng * i + ng)
                vt = span(i)[3]
                if even:
                    act.wait_ge(dve_step, FROM + i)
                    s.activation(norm.junk[:, 0:QR], proj[:, 1064:1320], ACT.Square, scale=QR ** -0.5,
                                 accum_out=nst[:, 0:1]).then_inc(sq_done, 1)
                    s.activation(norm.junk[:, QR:QR + KVR], proj[:, 1320:1448], ACT.Square, scale=KVR ** -0.5,
                                 accum_out=nst[:, 1:2]).then_inc(sq_done, 1)
                    act.wait_ge(sq_done, FROM + 2 * i + 2)
                    s.activation(nst[:, 2:4], nst[:, 0:2], ACT.Sqrt, bias=norm.eps[:]).then_inc(rt_done, 1)
                    s.activation(one(dst["wi"], i), proj[:, 1056:1064], ACT.Copy, scale=8 ** -0.5)
                if fox:
                    s.activation(one(dst["fc"], vt), proj[:, 1536:1544], ACT.Copy)
                vs = slice(640, 768) if even else slice(1024, 1536)
                s.activation(one(dst["v"], vt), proj[:, vs], ACT.Copy).then_inc(kept, 1)
            feature_major(NT)
            if even:
                up_query(NT)
                up_query_T(NT)

        def rope(v, dve, i, src, tab, nh, hd, off, half, cnt):
            x1, x2 = src[:, :, off:off + half], src[:, :, off + half:off + 2 * half]
            tr = one(trig, i)
            cos = tr[:, tab:tab + half].unsqueeze(1).to_broadcast([P, nh, half])
            sin = tr[:, tab + half:tab + 2 * half].unsqueeze(1).to_broadcast([P, nh, half])
            r = [rot[:, j, 0:nh * half].rearrange("p (h d) -> p h d", h=nh) for j in range(4)]
            v.tensor_tensor(r[0], x1, cos, ALU.mult).then_inc(dve_rope, 1)
            v.tensor_tensor(r[1], x2, sin, ALU.mult).then_inc(dve_rope, 1)
            v.tensor_tensor(r[2], x1, sin, ALU.mult).then_inc(dve_rope, 1)
            v.tensor_tensor(r[3], x2, cos, ALU.mult).then_inc(dve_rope, 1)
            dve.wait_ge(dve_rope, FROM + cnt + 4)
            v.tensor_tensor(x1, r[0], r[1], ALU.subtract).then_inc(dve_rope, 1)
            v.tensor_tensor(x2, r[2], r[3], ALU.add).then_inc(dve_rope, 1)
            dve.wait_ge(dve_rope, FROM + cnt + 6)
            return cnt + 6

        @block.vector
        def _(dve):
            v = nc.vector

            def split_w(c):
                k, w0 = c // nw, (c % nw) * ww
                dve.wait_ge(w_hi, FROM + c + 1)
                v.tensor_tensor(wlo[:, k, w0:w0 + ww], wraw[:, c % 2, :], whi[:, k, w0:w0 + ww].bitcast(F32),
                                ALU.subtract).then_inc(w_lo, 1)

            def low(i, slot):
                if not is_first(i):
                    dve.wait_ge(mm_ready, FROM + ng * (i - 1))
                h, l = hhi[slot], hlo[slot]
                norm.dve_lo(dve, i, [h[:, 0:4, :], h[:, 4:8, :]], [l[:, 0:4, :], l[:, 4:8, :]])

            def rotate(i):
                dve.wait_ge(proj_act, FROM + ng * i + ng)
                c = 24 * i
                c = rope(v, dve, i, proj[:, 0:640].rearrange("p (h d) -> p h d", d=64), RA, 10, 64, 0, 8, c)
                c = rope(v, dve, i, proj[:, 768:1056].rearrange("p (h d) -> p h d", d=32), RI, 9, 32, 0, 4, c)
                rope(v, dve, i, proj[:, 1448:1480].rearrange("p (h d) -> p h d", d=32), RB, 1, 32, 0, 16, c)

            def latents(i):
                dve.wait_ge(rt_done, FROM + i + 1)
                v.reciprocal(nst[:, 4:6], nst[:, 2:4]).then_inc(rr_done, 1)
                dve.wait_ge(rr_done, FROM + i + 1)
                v.scalar_tensor_tensor(cqn, proj[:, 1064:1320], nst[:, 4:5], gq[:], ALU.mult, ALU.mult)
                v.scalar_tensor_tensor(lat, proj[:, 1320:1448], nst[:, 5:6], gkv[:], ALU.mult, ALU.mult).then_inc(dve_step, 1)
                v.tensor_copy(stage[:, 0:P].rearrange("p (c d) -> p c d", c=4),
                              proj[:, 1024:1056].unsqueeze(1).to_broadcast([P, 4, 32]))
                v.tensor_copy(aq.rearrange("p (c g d) -> p c g d", c=4, g=2),
                              proj[:, 0:512].rearrange("p (g c d) -> p c g d", g=2, d=HD))
                v.tensor_copy(stage[:, P + 64:P + 96], proj[:, 1448:1480]).then_inc(post, 1)

            def feature_major(i):
                n, q, _, _ = span(i)
                dve.wait_ge(tq_ready, FROM + 3 * i + 3)
                v.tensor_copy(cqT, tq[2][:, 2 * P:4 * P].rearrange("p (c t) -> p c t", c=2)).then_inc(cqT_ready, 1)
                v.tensor_scalar(dst["qiT"][:, :, q], tq[2][:, 0:2 * P].rearrange("p (c t) -> p c t", c=2)[:, :, 0:n],
                                32 ** -0.5, None, ALU.mult).then_inc(cqT_ready, 1)

            def rotate_up(i):
                dve.wait_ge(qb_cp, FROM + 2 * i + 2)
                rope(v, dve, i, qb, RB, 8, 96, 64, 16, 24 * i + 18)

            c_mid = KD * nw // 2
            if even:
                v.memset(cr[:, :, 0:64], 0.0).then_inc(zeroed, 1)
            if fox:
                v.memset(dst["fc"][:, NT:KT - 1, :], 0.0)
            for c in range(c_mid):
                split_w(c)
            dve.wait_ge(norm.g_in, FROM + 16)
            dve.wait_ge(cache_tp, FROM + 2)
            norm.dve_norm(dve, 0)
            norm.dve_scale_g(dve, 0)
            low(0, 0)
            for c in range(c_mid, KD * nw):
                split_w(c)
            if even:
                dve.wait_ge(w_lo, FROM + KD)
                v.memset(stage, 0.0).then_inc(zeroed, 1)
                dve.wait_ge(zeroed, FROM + 2)
                dve.wait_ge(gq_in, FROM + 48)
                dve.wait_ge(trig_in, FROM + 16)
            for i, slot in steps(dve):
                if even and not is_first(i):
                    rotate(i - 1)
                if not is_last(i):
                    norm.dve_norm(dve, i + 1)
                if even and not is_first(i):
                    latents(i - 1)
                    feature_major(i - 1)
                if not is_last(i):
                    norm.dve_scale_g(dve, i + 1)
                    low(i + 1, 1 - slot)
                if even and not is_first(i):
                    rotate_up(i - 1)
            if even:
                rotate(NT)
                latents(NT)
                feature_major(NT)
                rotate_up(NT)

        @block.tensor
        def _(pe):
            t = nc.tensor

            def multiply(i, slot, g):
                if not is_first(i):
                    pe.wait_ge(proj_act, FROM + ng * (i - 1) + g + 1)
                cols = slice(go[g], go[g] + gw[g])
                for k in range(KD):
                    if is_first(i) and g == 0:
                        pe.wait_ge(w_lo, FROM + nw * (k + 1))
                    last = three_passes(nc, mm[g][:, 0:gw[g]], (hhi[slot][:, k, :], hlo[slot][:, k, :]),
                                        (whi[:, k, cols], wlo[:, k, cols]), k == 0, k == KD - 1)
                last.then_inc(mm_ready, 1)

            def transposes(i):
                if not even:
                    pe.wait_ge(proj_act, FROM + ng * i + ng)
                    pe.wait_ge(tq_act, FROM + 2 * i)
                    for g in range(2):
                        for c in range(4):
                            last = t.transpose(tq[g][:, c * P:(c + 1) * P],
                                               proj[:, 512 * g + c * P:512 * g + (c + 1) * P], ident[:])
                        last.then_inc(tq_ready, 1)
                    return
                pe.wait_ge(post, FROM + i + 1)
                pe.wait_ge(qbT_ready, FROM + 2 * i)
                for c in range(4):
                    last = t.transpose(tq[0][:, c * P:(c + 1) * P], aq[:, c * P:(c + 1) * P], ident[:])
                last.then_inc(tq_ready, 1)
                t.transpose(tq[1][:, 0:P], proj[:, 512:640], ident[:])
                t.transpose(tq[1][:, P:2 * P], stage[:, 0:P], ident[:])
                t.transpose(tq[1][:, 2 * P:3 * P], lat, ident[:])
                t.transpose(tq[1][0:96, 3 * P:4 * P], stage[:, P:P + 96], ident[:]).then_inc(tq_ready, 1)
                pe.wait_ge(cqT_ready, FROM + 2 * i)
                for c in range(2):
                    t.transpose(tq[2][:, c * P:(c + 1) * P], proj[:, 768 + c * P:768 + (c + 1) * P], ident[:])
                for c in range(2):
                    last = t.transpose(tq[2][:, (2 + c) * P:(3 + c) * P], cqn[:, c * P:(c + 1) * P], ident[:])
                last.then_inc(tq_ready, 1)

            def up_query(i):
                pe.wait_ge(cqT_ready, FROM + 2 * i + 1)
                for g in range(2):
                    pe.wait_ge(tq_act, FROM + 2 * i + g + 1)
                    for c in range(2):
                        last = t.matmul(tq[g][:, 0:384], cqT[:, c, :], wuq[:, c, 384 * g:384 * (g + 1)],
                                        start=(c == 0), stop=(c == 1))
                    last.then_inc(qb_mm, 1)

            def up_query_T(i):
                pe.wait_ge(dve_rope, FROM + 24 * i + 24)
                for g in range(2):
                    for h in range(4):
                        last = t.transpose(tq[g][0:96, h * P:(h + 1) * P], qb[:, 4 * g + h, :], ident[:])
                    last.then_inc(qb_tp, 1)

            pe.wait_ge(cache_in, FROM + 16 * (16 if even else 4))
            if even:
                pe.wait_ge(zeroed, FROM + 1)
            for b in range(2):
                if even:
                    t.transpose(mm[b][:, 0:P], ck[:, b], ident[:])
                    t.transpose(mm[b][:, P:2 * P], ci[:, b], ident[:])
                    t.transpose(mm[b][:, 2 * P:3 * P], cl[:, b, :], ident[:])
                    last = t.transpose(mm[b][0:96, 3 * P:4 * P], cr[:, b, :], ident[:])
                else:
                    for c in range(4):
                        last = t.transpose(mm[b][:, c * P:(c + 1) * P], rows4[:, b, c, :], ident[:])
                last.then_inc(cache_tp, 1)
            norm.pe_transposes(pe, 0)
            pe.wait_ge(cache_cp, FROM + 2)
            if even:
                pe.wait_ge(gq_in, FROM + 48)
            for i, slot in steps(pe):
                pe.wait_ge(norm.lo_ready, FROM + 2 * i + 2)
                multiply(i, slot, 0)
                if not is_first(i):
                    transposes(i - 1)
                if not is_last(i):
                    norm.pe_transposes(pe, i + 1)
                multiply(i, slot, 1)
                if even and not is_first(i):
                    up_query(i - 1)
                for g in range(2, ng):
                    multiply(i, slot, g)
                if even and not is_first(i):
                    up_query_T(i - 1)
            transposes(NT)
            if even:
                up_query(NT)
                up_query_T(NT)


TILES = NT + 1
UNITS = 2 * TILES
UNIT = [(t, h) for t in range(TILES) for h in range(2)]


def queries(t):
    return DEC if t == NT else P


def blocks(t, g):
    w = key_tile(t)[0]
    return [(b, min(P, w - b * P)) for b in range(4 * g, min(4 * g + 4, (w + P - 1) // P))]


WIDE = [u for u, (t, h) in enumerate(UNIT) if blocks(t, 1)]
O_USES = [[t for t in range(TILES) if t % 2 == s] for s in range(2)]
TOPK_TILES = [(t, NT + 1 - t) for t in range(2, NT // 2 + 1)]
TOPK_TURN = TOPK_P // 8 // 4


def group_count(p, u, g):
    return p * UNITS + u if g == 0 else p * len(WIDE) + WIDE.index(u)


def o_count(p, t):
    return p * len(O_USES[t % 2]) + O_USES[t % 2].index(t)


def attention(nc, dram, consts, kind, src):
    ident, ident_bf = consts["ident"], consts["ident_bf"]
    stick, mla, fox, dsa = kind == "d", kind == "b", kind == "c", kind == "a"
    mask = None if dsa else consts[{"b": "mask_chunk", "c": "mask_causal", "d": "mask_strict"}[kind]]
    with Phase(nc, f"att_{kind}") as ph:
        sb, sem = ph.sb, ph.sem
        q = sb("q", [96, 2, TOK]) if mla else sb("q", [P, 2, TILES * P])
        if mla:
            k, v = [src["krT"], sb("k1", [96, KEYS])], sb("v", [P, KT, P])
            wkv = sb("wkv", [P, 2 * P])
            best = sb("best", [P, 2, 8])
        if fox:
            fk = sb("fk", [P, 2, KEYS], F32R)
        prob = [sb(f"prob{s}", [P, SEQ]) for s in range(2)]
        if stick:
            ez = [sb(f"ez{s}", [P, SEQ]) for s in range(2)]
            sp = sb("sp", [P, SEQ])
        pt = [sb(f"pt{s}", [P, 8, P]) for s in range(2)]
        ot = [sb(f"ot{s}", [P, P]) for s in range(2)]
        nm = sb("nm", [P, 8])
        rs = sb("rs", [P, 8])
        rr = sb("rr", [P, 8])
        S = [ph.ps(f"s{s}", (P, SEQ)) for s in range(2)]
        TP = [ph.ps(f"tp{g}") for g in range(2)]
        O = [ph.ps(f"o{g}") for g in range(2)]
        q_in, staged, passed, cleared = sem("q_in"), sem("staged"), sem("passed"), sem("cleared")
        s_ready, prob_ready, pv_done = sem("s_ready"), sem("prob_ready"), sem("pv_done")
        max_done, rcp_done = sem("max_done"), sem("rcp_done")
        tp_ready = [sem(f"tp_ready{g}") for g in range(2)]
        pt_ready = [sem(f"pt_ready{g}") for g in range(2)]
        o_out = [sem(f"o_out{s}") for s in range(2)]
        ot_stored = [sem(f"ot_stored{s}") for s in range(2)]
        if mla:
            w_in, kv_ready = sem("w_in"), sem("kv_ready")
            kv_out = [sem(f"kv_out{s}") for s in range(2)]
            top_found, top_gone = sem("top_found"), sem("top_gone")
        if stick:
            abs_done, ez_done, ln_done, sp_done, scan_done, arg_done = (
                sem("abs_done"), sem("ez_done"), sem("ln_done"), sem("sp_done"), sem("scan_done"), sem("arg_done"))
        block = ph.block()

        def keys(p, h, c0, c1):
            if mla:
                return k[h][:, c0:c1]
            if dsa:
                return src["kaT"][:, c0:c1]
            return src["kT"][:, ds(p, 1), c0:c1].rearrange("d a n -> d (a n)")

        def values(p, h, b):
            if mla or dsa:
                return (v if mla else src["v"])[:, b, h * HD:(h + 1) * HD]
            return src["v"][:, b, ds(p * P + h * HD, HD)]

        @block.sync
        def _(eng):
            def load_w(p):
                eng.dma_start(wkv[:], dram["w_b_ukv"][0, :, ds(p * 2 * P, 2 * P)] if not isinstance(p, int) else
                              dram["w_b_ukv"][0, :, p * 2 * P:(p + 1) * 2 * P]).then_inc(w_in, 16)

            def load_q(p):
                if mla:
                    eng.dma_start(q[:], rows(dram["qbT"], 2 * p, 2).rearrange("h d t -> d h t")).then_inc(q_in, 16)
                    return
                for h in range(2):
                    hp = slice(h * HD, (h + 1) * HD)
                    qT = (src["qaT"] if dsa else src["qT"])[hp]
                    eng.dma_start(q[hp, h, 0:TOK], one(qT, p)).then_inc(q_in, 16)

            def store(p, t):
                s, n = t % 2, queries(t)
                eng.wait_ge(o_out[s], FROM + o_count(p, t) + 1)
                r = slice(t * P, t * P + n)
                if dsa:
                    to = dram["att"][r, 0:8 * HD].rearrange("t (g c d) -> t g c d", g=2, d=HD)
                    to = to[:, :, p:p + 1, :] if isinstance(p, int) else to[:, :, ds(p, 1), :]
                    to = to.rearrange("t g a d -> t g (a d)")
                    eng.dma_start(to, ot[s][0:n, :].rearrange("t (g d) -> t g d", g=2)).then_inc(ot_stored[s], 16)
                else:
                    c0 = (0 if fox else 8 * HD) + p * P
                    to = dram["att"][r, c0:c0 + P] if isinstance(p, int) else dram["att"][r, ds(c0, P)]
                    eng.dma_start(to, ot[s][0:n, :]).then_inc(ot_stored[s], 16)

            if mla:
                load_w(0)
            load_q(0)
            with eng.Fori(0, 3) as p:
                for t in range(TILES):
                    if t == 2 and mla:
                        eng.wait_ge(kv_ready, FROM + 9 * p + 9)
                        eng.sem_inc(passed, 1)
                        load_w(p + 1)
                    if t == NT - 1:
                        eng.wait_ge(s_ready, FROM + (p + 1) * UNITS)
                        eng.sem_inc(passed, 1)
                        load_q(p + 1)
                    store(p, t)
            for t in range(TILES):
                store(3, t)
            for s in range(2):
                eng.wait_ge(ot_stored[s], FROM + 16 * 4 * len(O_USES[s]))

        @block.gpsimd
        def _(pool):
            g = nc.gpsimd
            g.memset((v if mla else src["v"])[DEC:P, KT - 1, :], 0.0).then_inc(cleared, 1)
            if mla:
                pool.wait_ge(cleared, FROM + 1)
                g.tensor_copy(k[1][64:96, :], src["krT"][64:96, :]).then_inc(staged, 1)
                return
            pool.wait_ge(cleared, FROM + 1)
            g.memset(q[:, :, TOK:], 0.0).then_inc(cleared, 1)
            for h in range(2):
                pool.wait_ge(cleared, FROM + 2 + h)
                g.memset(q[(1 - h) * HD:(2 - h) * HD, h, 0:TOK], 0.0).then_inc(cleared, 1)

        @block.tensor
        def _(pe):
            tt = nc.tensor

            def scores(p, u):
                t, h = UNIT[u]
                s, w = u % 2, key_tile(t)[0]
                n = queries(t) if mla else P
                k0 = key_tile(t)[1]
                for c0 in range(0, w, 512):
                    cw = min(512, w - c0)
                    o = S[s][0:n, c0:c0 + cw]
                    parts = [(o, q[:, h, t * P:t * P + n], keys(p, h, k0 + c0, k0 + c0 + cw))]
                    if fox:
                        parts.append((o, src["fq"][:, t * P:t * P + n], fk[:, h, k0 + c0:k0 + c0 + cw]))
                    if dsa:
                        b0 = src["bias_at"][t] + c0
                        parts.append((o, ident_bf[:, 0:n], src["bias"][:, b0:b0 + cw]))
                    elif c0 + cw == w and not (mla and t == NT):
                        m = queries(t)
                        parts.append((S[s][0:n, w - m:w], ident_bf[:, 0:n], mask[:, 0:m]))
                    for j, (o, a, b) in enumerate(parts):
                        last = tt.matmul(o, a, b, start=(j == 0), stop=(j == len(parts) - 1))
                last.then_inc(s_ready, 1)

            def transposes(p, u):
                t, h = UNIT[u]
                n, s = queries(t), u % 2
                pe.wait_ge(prob_ready, FROM + p * UNITS + u + 1)
                for g in range(2):
                    if not blocks(t, g):
                        continue
                    pe.wait_ge(pt_ready[g], FROM + group_count(p, u, g))
                    if n < P:
                        pe.sem_inc(passed, 1)
                    for b, r in blocks(t, g):
                        last = tt.transpose(TP[g][0:r, (b % 4) * P:(b % 4) * P + n],
                                            prob[s][0:n, b * P:b * P + r], ident[0:n, 0:n])
                    last.then_inc(tp_ready[g], 1)

            def products(p, u):
                t, h = UNIT[u]
                n, s, w = queries(t), u % 2, key_tile(t)[0]
                if h == 0:
                    pe.wait_ge(o_out[t % 2], FROM + o_count(p, t))
                for g in range(2):
                    if not blocks(t, g):
                        continue
                    pe.wait_ge(pt_ready[g], FROM + group_count(p, u, g) + 1)
                    for b, r in blocks(t, g):
                        last = tt.matmul(O[t % 2][0:n, h * HD:(h + 1) * HD], pt[s][:, b, 0:n],
                                         values(p, h, b if t < NT else NT + b), start=(b == 0), stop=(b * P + r == w))
                last.then_inc(pv_done, 1)

            def expand(p):
                pe.wait_ge(w_in, FROM + 16 * p + 16)
                wv = wkv[:].rearrange("p (h x) -> p h x", h=2)[:, :, HD:P]
                for j in range(9):
                    o = S[j % 2][:, 512 * (j // 2 % 2):512 * (j // 2 % 2) + 512]
                    if j >= 4:
                        pe.wait_ge(kv_out[j % 2], FROM + (5, 4)[j % 2] * p + (j - 4) // 2 + 1)
                    if j < 6:
                        h, c = j // 3, j % 3
                        last = tt.matmul(o[0:HD, 0:448], wkv[:, h * P:h * P + HD],
                                         src["latT"][:, c * 448:(c + 1) * 448], start=True, stop=True)
                    else:
                        for b in range(4 * (j - 6), min(4 * (j - 5), KT)):
                            r = DEC if b == KT - 1 else P
                            last = tt.matmul(o[0:r, (b % 4) * P:(b % 4 + 1) * P],
                                             src["latT"][:, b * P:b * P + r], wv, start=True, stop=True)
                    last.then_inc(kv_ready, 1)
                pe.wait_ge(kv_out[0], FROM + 5 * p + 5)
                pe.wait_ge(kv_out[1], FROM + 4 * p + 4)

            if mla:
                pe.wait_ge(staged, FROM + 1)
            pe.wait_ge(cleared, FROM + (1 if mla else 4))
            with pe.Fori(0, 4) as p:
                if mla:
                    expand(p)
                if fox:
                    pe.wait_ge(staged, FROM + 2 * p + 2)
                n_in = 16 if mla else 32
                pe.wait_ge(q_in, FROM + n_in * p + n_in)
                pe.sem_inc(passed, 1)
                scores(p, 0)
                scores(p, 1)
                for u in range(UNITS):
                    if stick and u + 2 < UNITS:
                        pe.wait_ge(arg_done, FROM + p * UNITS + u + 1)
                        pe.sem_inc(passed, 1)
                        scores(p, u + 2)
                    transposes(p, u)
                    if not stick and u + 2 < UNITS:
                        scores(p, u + 2)
                    if u:
                        products(p, u - 1)
                products(p, UNITS - 1)

        def copy_group(eng, p, u, g, scalar):
            t, h = UNIT[u]
            bl = blocks(t, g)
            if not bl:
                return
            n, s = queries(t), u % 2
            eng.wait_ge(tp_ready[g], FROM + group_count(p, u, g) + 1)
            full = [b for b, r in bl if r == P]
            jobs = [(full[0], full[-1] + 1, P)] if full else []
            jobs += [(b, b + 1, r) for b, r in bl if r != P]
            for b0, b1, r in jobs:
                i = TP[g][:].rearrange("p (b t) -> p b t", b=4)[0:r, b0 - 4 * g:b1 - 4 * g, 0:n]
                o = pt[s][0:r, b0:b1, 0:n]
                last = nc.scalar.activation(o, i, ACT.Copy) if scalar else nc.vector.tensor_copy(o, i)
            last.then_inc(pt_ready[g], 1)

        def transposed(eng, p, u):
            g = 1 if blocks(UNIT[u][0], 1) else 0
            eng.wait_ge(tp_ready[g], FROM + group_count(p, u, g) + 1)

        def expanded(eng, p, j):
            o = S[j % 2][:, 512 * (j // 2 % 2):512 * (j // 2 % 2) + 512]
            copy = (lambda a, b: nc.scalar.activation(a, b, ACT.Copy)) if j % 2 == 0 else nc.vector.tensor_copy
            eng.wait_ge(kv_ready, FROM + 9 * p + j + 1)
            if j < 6:
                last = copy(k[j // 3][0:HD, (j % 3) * 448:(j % 3 + 1) * 448], o[0:HD, 0:448])
            else:
                b0 = 4 * (j - 6)
                b1 = min(b0 + 4, KT - 1)
                last = copy(v[:, b0:b1, :].rearrange("p b d -> p (b d)"), o[:, 0:(b1 - b0) * P])
                if j == 8:
                    last = copy(v[0:DEC, KT - 1, :], o[0:DEC, (b1 - b0) * P:(b1 - b0 + 1) * P])
            last.then_inc(kv_out[j % 2], 1)

        @block.scalar
        def _(act):
            s_ = nc.scalar

            def logarithm(p, u):
                n, s, w, m = queries(UNIT[u][0]), u % 2, key_tile(UNIT[u][0])[0], p * UNITS + u
                act.wait_ge(s_ready, FROM + m + 1)
                if u >= 2:
                    act.wait_ge(sp_done, FROM + m - 1)
                s_.activation(ez[s][0:n, 0:w], S[s][0:n, 0:w], ACT.Abs).then_inc(abs_done, 1)
                act.wait_ge(abs_done, FROM + m + 1)
                s_.activation(ez[s][0:n, 0:w], ez[s][0:n, 0:w], ACT.Exp, scale=-1.0).then_inc(ez_done, 1)
                act.wait_ge(ez_done, FROM + m + 1)
                s_.activation(ez[s][0:n, 0:w], ez[s][0:n, 0:w], ACT.Ln, bias=1.0).then_inc(ln_done, 1)

            def exponential(p, u):
                n, s, w, m = queries(UNIT[u][0]), u % 2, key_tile(UNIT[u][0])[0], p * UNITS + u
                if stick:
                    act.wait_ge(arg_done, FROM + m + 1)
                    s_.activation(prob[s][0:n, 0:w], prob[s][0:n, 0:w], ACT.Exp).then_inc(prob_ready, 1)
                else:
                    act.wait_ge(max_done, FROM + m + 1)
                    if u >= 2:
                        transposed(act, p, u - 2)
                    c = slice(u % 8, u % 8 + 1)
                    s_.activation(prob[s][0:n, 0:w], S[s][0:n, 0:w], ACT.Exp, bias=nm[0:n, c],
                                  accum_out=rs[0:n, c]).then_inc(prob_ready, 1)

            def output(p, u):
                t, h = UNIT[u]
                if h == 0:
                    return
                n, s = queries(t), t % 2
                act.wait_ge(pv_done, FROM + p * UNITS + u + 1)
                act.wait_ge(ot_stored[s], FROM + 16 * o_count(p, t))
                if stick:
                    last = s_.activation(ot[s][0:n, :], O[s][0:n, 0:P], ACT.Copy)
                else:
                    act.wait_ge(rcp_done, FROM + p * UNITS + u + 1)
                    for j in range(2):
                        hd, c = slice(j * HD, (j + 1) * HD), (u - 1 + j) % 8
                        last = s_.activation(ot[s][0:n, hd], O[s][0:n, hd], ACT.Copy, scale=rr[0:n, c:c + 1])
                last.then_inc(o_out[s], 1)

            if stick:
                s_.preload_act_table_set("natural_log_exp_and_others")
            with act.Fori(0, 4) as p:
                if mla:
                    for j in range(0, 9, 2):
                        expanded(act, p, j)
                if stick:
                    logarithm(p, 0)
                    logarithm(p, 1)
                exponential(p, 0)
                for u in range(UNITS):
                    if stick:
                        if u + 2 < UNITS:
                            logarithm(p, u + 2)
                        copy_group(act, p, u, 0, True)
                        if u + 1 < UNITS:
                            exponential(p, u + 1)
                    else:
                        if u + 1 < UNITS:
                            exponential(p, u + 1)
                        copy_group(act, p, u, 0, True)
                        if mla:
                            copy_group(act, p, u, 1, True)
                    if u >= 2:
                        output(p, u - 2)
                output(p, UNITS - 2)
                output(p, UNITS - 1)

        @block.vector
        def _(dve):
            v_ = nc.vector

            def top(p, u):
                n, s, w, m = queries(UNIT[u][0]), u % 2, key_tile(UNIT[u][0])[0], p * UNITS + u
                dve.wait_ge(s_ready, FROM + m + 1)
                v_.tensor_reduce(nm[0:n, u % 8:u % 8 + 1], S[s][0:n, 0:w], AX_X, ALU.max, negate=True).then_inc(max_done, 1)

            def over_sum(p, u):
                n, c, m = queries(UNIT[u][0]), slice(u % 8, u % 8 + 1), p * UNITS + u
                dve.wait_ge(prob_ready, FROM + m + 1)
                v_.reciprocal(rr[0:n, c], rs[0:n, c]).then_inc(rcp_done, 1)

            def exponent(p, u):
                n, s, w, m = queries(UNIT[u][0]), u % 2, key_tile(UNIT[u][0])[0], p * UNITS + u
                dve.wait_ge(ln_done, FROM + m + 1)
                v_.scalar_tensor_tensor(sp[0:n, 0:w], S[s][0:n, 0:w], 0.0, ez[s][0:n, 0:w], ALU.max, ALU.add).then_inc(sp_done, 1)
                dve.wait_ge(sp_done, FROM + m + 1)
                if u >= 2:
                    transposed(dve, p, u - 2)
                v_.tensor_tensor_scan(prob[s][0:n, 0:w][:, ::-1], sp[0:n, 0:w][:, ::-1], sp[0:n, 0:w][:, ::-1],
                                      0.0, ALU.add, ALU.bypass).then_inc(scan_done, 1)
                dve.wait_ge(scan_done, FROM + m + 1)
                v_.tensor_tensor(prob[s][0:n, 0:w], S[s][0:n, 0:w], prob[s][0:n, 0:w], ALU.subtract).then_inc(arg_done, 1)

            def top_round(p, j):
                m = (TOPK_TURN * len(TOPK_TILES)) * p + j
                pair = TOPK_TILES[j % len(TOPK_TILES)]
                for i, t in enumerate(pair):
                    dve.wait_ge(top_gone, FROM + 2 * m + i - 1)
                    dve.sem_inc(passed, 1)
                    v_.max(best[:, i, :], src["work"][t][:]).then_inc(top_found, 1)
                for i, t in enumerate(pair):
                    dve.wait_ge(top_found, FROM + 2 * m + i + 1)
                    dve.sem_inc(passed, 1)
                    v_.match_replace(src["work"][t][:], best[:, i, :], src["work"][t][:], GONE).then_inc(top_gone, 1)

            turn = TOPK_TURN * len(TOPK_TILES)
            with dve.Fori(0, 4) as p:
                if fox:
                    dve.wait_ge(s_ready, FROM + p * UNITS)
                    for h in range(2):
                        v_.tensor_scalar(fk[:, h, :], src["fk_all"][:], src["onehot"][:, ds(2 * p + h, 1)], None,
                                         ALU.mult).then_inc(staged, 1)
                if mla:
                    for j in range(1, 9, 2):
                        expanded(dve, p, j)
                if stick:
                    exponent(p, 0)
                else:
                    top(p, 0)
                    top(p, 1)
                    over_sum(p, 0)
                for u in range(UNITS):
                    if stick and u + 1 < UNITS:
                        exponent(p, u + 1)
                    if not mla:
                        copy_group(dve, p, u, 1, False)
                    if not stick:
                        if u + 2 < UNITS:
                            top(p, u + 2)
                        if u + 1 < UNITS:
                            over_sum(p, u + 1)
                    if mla:
                        for j in range(turn * u // UNITS, turn * (u + 1) // UNITS):
                            top_round(p, j)
            if mla:
                dve.wait_ge(top_gone, FROM + 4 * 2 * turn)
                for t, w in src["work"].items():
                    b0 = src["bias_at"][t]
                    v_.tensor_scalar(src["bias"][:, b0:b0 + w.shape[1]], w[:], -3.2e38, NEG, ALU.is_gt, ALU.mult)


def index_scores(nc, dram, consts, src):
    with Phase(nc, "index") as ph:
        sb, sem = ph.sb, ph.sem
        work = [src["work"][t] if t in src["work"] else sb(f"work{t}", [P, key_tile(t)[0]]) for t in range(TILES)]
        relu = [sb(f"relu{s}", [P, SEQ]) for s in range(2)]
        best = sb("best", [P, 8])
        S = [ph.ps(f"s{s}", (P, SEQ)) for s in range(2)]
        s_ready, relu_done, acc_done, step, passed = sem("s_ready"), sem("relu_done"), sem("acc_done"), sem("step"), sem("passed")
        block = ph.block()
        H = 8
        qiT, kiT, wi, bias, at = src["qiT"], src["kiT"], src["wi"], src["bias"], src["bias_at"]

        @block.tensor
        def _(pe):
            for t in range(TILES):
                w, k0 = key_tile(t)
                n = queries(t)
                for h in range(H):
                    u = t * H + h
                    if u >= 2:
                        pe.wait_ge(relu_done, FROM + u - 1)
                    hp = slice(32 * (h % 4), 32 * (h % 4) + 32)
                    for c0 in range(0, w, 512):
                        cw = min(512, w - c0)
                        last = nc.tensor.matmul(S[u % 2][0:n, c0:c0 + cw], qiT[hp, h // 4, t * P:t * P + n],
                                                kiT[hp, k0 + c0:k0 + c0 + cw], start=True, stop=True)
                    last.then_inc(s_ready, 1)

        @block.scalar
        def _(act):
            for t in range(TILES):
                w, n = key_tile(t)[0], queries(t)
                for h in range(H):
                    u = t * H + h
                    act.wait_ge(s_ready, FROM + u + 1)
                    if u >= 2:
                        act.wait_ge(acc_done, FROM + u - 1)
                    nc.scalar.activation(relu[u % 2][0:n, 0:w], S[u % 2][0:n, 0:w], ACT.Relu).then_inc(relu_done, 1)

        @block.vector
        def _(dve):
            v = nc.vector
            steps = 0
            v.memset(bias[DEC:P, at[NT]:at[NT] + key_tile(NT)[0]], 0.0)
            for t in range(TILES):
                w, n = key_tile(t)[0], queries(t)
                wk = work[t][0:n, :]
                for h in range(H):
                    u = t * H + h
                    dve.wait_ge(relu_done, FROM + u + 1)
                    r, f = relu[u % 2][0:n, 0:w], wi[0:n, t, h:h + 1]
                    if h == 0:
                        v.tensor_scalar(wk, r, f, None, ALU.mult).then_inc(acc_done, 1)
                    else:
                        dve.wait_ge(acc_done, FROM + u)
                        v.scalar_tensor_tensor(wk, r, f, wk, ALU.mult, ALU.add).then_inc(acc_done, 1)
                dve.wait_ge(acc_done, FROM + (t + 1) * H)
                if t < NT:
                    v.memset(work[t][0:P // 2, w - P // 2:w], -3.0e38).then_inc(step, 1)
                    steps += 1
                if t < 2:
                    dve.wait_ge(step, FROM + steps)
                    v.tensor_scalar(bias[0:n, at[t]:at[t] + w], wk, -2.9e38, NEG, ALU.is_lt, ALU.mult)
                if t == NT:
                    with dve.Fori(0, TOPK_S // 8) as j:
                        dve.wait_ge(step, FROM + steps + 2 * j)
                        dve.sem_inc(passed, 1)
                        v.max(best[0:n, :], wk).then_inc(step, 1)
                        dve.wait_ge(step, FROM + steps + 2 * j + 1)
                        dve.sem_inc(passed, 1)
                        v.match_replace(wk, best[0:n, :], wk, GONE).then_inc(step, 1)
                    steps += 2 * (TOPK_S // 8)
                    dve.wait_ge(step, FROM + steps)
                    v.tensor_scalar(bias[0:n, at[t]:at[t] + w], wk, -3.2e38, NEG, ALU.is_gt, ALU.mult)


GROUPS = 3 * 32 + 8


def group(g):
    return slice(32 * g, 32 * g + 8)


def forget(nc, dram, consts, fc, dst, out):
    with Phase(nc, "forget") as ph:
        sb, sem = ph.sb, ph.sem
        bf = sb("bf", [P, 8])
        u = sb("u", [P, KT, 8])
        e = sb("e", [P, KT, 8])
        lf = sb("lf", [P, KT, GROUPS])
        lfT = sb("lfT", [GROUPS, KEYS])
        cum = sb("cum", [GROUPS, KEYS])
        high = sb("high", [GROUPS, KEYS], F32R)
        tp = [ph.ps(f"tp{b}") for b in range(3)]
        b_in, c_in, dstep, astep, tp_ready, tp_out, stored = (sem("b_in"), sem("c_in"), sem("dstep"), sem("astep"),
                                                              sem("tp_ready"), sem("tp_out"), sem("stored"))
        ident = consts["ident"]
        block = ph.block()

        @block.sync
        def _(sp):
            sp.dma_start(bf[:], dram["b_forget"][0:1, :].to_broadcast([P, 8])).then_inc(b_in, 16)
            sp.wait_ge(dstep, FROM + 7)
            for b in range(2):
                for g in range(4):
                    sp.dma_start(lf[:, NT + b, group(g)], dram["cache_c_logf"][0, 0, b * P:(b + 1) * P]).then_inc(c_in, 16)
            sp.dma_start(out["p_c_logf"].rearrange("(t p) h -> p t h", p=P), lf[:, 0:NT, 0:8]).then_inc(stored, 16)
            sp.dma_start(out["s_c_logf"], lf[0:DEC, KT - 1, 0:8]).then_inc(stored, 16)
            sp.wait_ge(stored, FROM + 32)

        @block.vector
        def _(dve):
            v = nc.vector
            v.memset(lf[:], 0.0).then_inc(dstep, 1)
            v.memset(dst["fk_all"][:], 0.0).then_inc(dstep, 1)
            v.memset(dst["fq"][:].bitcast(F32), 0.0).then_inc(dstep, 1)
            dve.wait_ge(b_in, FROM + 16)
            v.tensor_tensor(u[:], fc[:], bf[:].unsqueeze(1).to_broadcast([P, KT, 8]), ALU.add).then_inc(dstep, 1)
            dve.wait_ge(dstep, FROM + 4)
            dve.wait_ge(astep, FROM + 3)
            v.scalar_tensor_tensor(u[:], u[:], 0.0, e[:], ALU.min, ALU.subtract).then_inc(dstep, 1)
            dve.wait_ge(dstep, FROM + 5)
            for g in range(4):
                last = v.tensor_copy(lf[:, 0:NT, group(g)], u[:, 0:NT])
            last.then_inc(dstep, 1)
            for g in range(4):
                last = v.tensor_copy(lf[0:DEC, KT - 1, group(g)], u[0:DEC, KT - 1])
            last.then_inc(dstep, 1)
            dve.wait_ge(tp_out, FROM + 3)
            for c0, c1 in ((0, SEQ), (SEQ, KEYS)):
                a = lfT[:, c0:c1]
                v.tensor_tensor_scan(cum[:, c0:c1], a, a, 0.0, ALU.add, ALU.bypass).then_inc(dstep, 1)
            dve.wait_ge(dstep, FROM + 9)
            v.tensor_copy(high[:], cum[:]).then_inc(dstep, 1)
            dve.wait_ge(dstep, FROM + 10)
            fk, fq = dst["fk_all"], dst["fq"]
            v.tensor_scalar(fk[group(0), :], high[group(0), :].bitcast(F32), -1.0, None, ALU.mult)
            v.tensor_tensor(fk[group(1), :], high[group(1), :].bitcast(F32), cum[group(1), :], ALU.subtract)
            for g in (0, 1):
                v.memset(fk[group(2 + g), :], 1.0)
                v.memset(fq[group(g), :].bitcast(F32), 1.0)
            for q, c in ((slice(0, SEQ), slice(0, SEQ)), (slice(SEQ, TOK), slice(OWN, KEYS))):
                v.tensor_copy(fq[group(2), q], high[group(2), c].bitcast(F32))
                last = v.tensor_tensor(fq[group(3), q], cum[group(3), c], high[group(3), c].bitcast(F32), ALU.subtract)
            last.then_inc(dstep, 1)
            v.tensor_copy(dst["onehot"][:, :], ident[:, 0:8]).then_inc(dstep, 1)
            dve.wait_ge(dstep, FROM + 12)
            for g in (1, 2, 3):
                v.tensor_copy(dst["onehot"][group(g), :], ident[group(g), group(g)])

        @block.scalar
        def _(act):
            s = nc.scalar
            s.preload_act_table_set("natural_log_exp_and_others")
            act.wait_ge(dstep, FROM + 4)
            s.activation(e[:], u[:], ACT.Abs).then_inc(astep, 1)
            act.wait_ge(astep, FROM + 1)
            s.activation(e[:], e[:], ACT.Exp, scale=-1.0).then_inc(astep, 1)
            act.wait_ge(astep, FROM + 2)
            s.activation(e[:], e[:], ACT.Ln, bias=1.0).then_inc(astep, 1)
            for b in range(3):
                act.wait_ge(tp_ready, FROM + b + 1)
                c0, c1 = b * 512, min(b * 512 + 512, KEYS)
                s.activation(lfT[:, c0:c1], tp[b][0:GROUPS, 0:c1 - c0], ACT.Copy).then_inc(tp_out, 1)

        @block.tensor
        def _(pe):
            pe.wait_ge(c_in, FROM + 128)
            for b in range(3):
                for i in range(4 * b, min(4 * b + 4, KT)):
                    r = DEC if i == KT - 1 else P
                    last = nc.tensor.transpose(tp[b][0:GROUPS, (i % 4) * P:(i % 4) * P + r], lf[0:r, i, :], ident[0:r, 0:r])
                last.then_inc(tp_ready, 1)


def output_projection(nc, dram, consts, layer, w_dram, x_src, xres, hT):
    with Phase(nc, f"out_{layer}") as ph:
        sb, sem = ph.sb, ph.sem
        whi = sb("whi", [P, KD, D], F32R)
        wlo = sb("wlo", [P, KD, D], F32R)
        wraw = sb("wraw", [P, 2, D])
        a = sb("a", [P, D])
        ahi = sb("ahi", [P, KD, P], F32R)
        alo = sb("alo", [P, KD, P], F32R)
        x = sb("x", [P, D])
        norm = Norm(ph, nc, consts, x[:], dram["g_ffn"][layer])
        mm = [ph.ps(f"mm{g}") for g in range(2)]
        at = ph.ps("at", (P, D))
        a_tp = sem("a_tp")
        w_in = [sem("w_in0"), sem("w_in1")]
        w_hi, w_lo, a_in, x_in = sem("w_hi"), sem("w_lo"), sem("a_in"), sem("x_in")
        a_hi, a_lo, mm_ready, added, kept, padded = (sem("a_hi"), sem("a_lo"), sem("mm_ready"), sem("added"),
                                                     sem("kept"), sem("padded"))
        block = ph.block()

        def tiles(eng):
            with eng.Fori(0, NT) as i:
                yield i, False
            yield NT, True

        @block.sync
        def _(sp):
            for k in range(KD):
                if k >= 2:
                    sp.wait_ge(w_lo, FROM + k - 1)
                sp.dma_start(wraw[:, k % 2, :], w_dram[k * P:(k + 1) * P, :]).then_inc(w_in[k % 2], 16)
            norm.load_g(sp)
            for i, tail in tiles(sp):
                n = DEC if tail else P
                sp.wait_ge(a_tp, FROM + i)
                sp.dma_start(a[0:n, :], rows(dram["att"], i * P, n)).then_inc(a_in, 16)
                sp.wait_ge(norm.hn_ready, FROM + i)
                sp.wait_ge(kept, FROM + i)
                if tail:
                    sp.dma_start(x[0:n, :], x_src[1]).then_inc(x_in, 16)
                else:
                    sp.dma_start(x[:], rows(x_src[0], i * P, P)).then_inc(x_in, 16)

        @block.scalar
        def _(act):
            s = nc.scalar
            s.preload_act_table_set("sqrt_and_others")
            for k in range(KD):
                act.wait_ge(w_in[k % 2], FROM + 16 * (k // 2 + 1))
                s.activation(whi[:, k, :], wraw[:, k % 2, :], ACT.Copy).then_inc(w_hi, 1)
            for i, tail in tiles(act):
                n = DEC if tail else P
                act.wait_ge(a_tp, FROM + i + 1)
                act.wait_ge(mm_ready, FROM + 2 * i)
                s.activation(ahi[:].rearrange("p k t -> p (k t)"), at[:], ACT.Copy).then_inc(a_hi, 1)
                norm.act_square(act, i, added, 2 * i + 2)
                norm.act_root(act, i)
                s.activation(one(xres, i), x[:], ACT.Copy).then_inc(kept, 1)
                q = ds(i * P, n) if not tail else slice(SEQ, TOK)
                norm.act_hi(act, i, [hT[0][:, 0:4, q], hT[0][:, 4:8, q]], n)

        @block.vector
        def _(dve):
            v = nc.vector
            for k in range(KD):
                dve.wait_ge(w_hi, FROM + k + 1)
                v.tensor_tensor(wlo[:, k, :], wraw[:, k % 2, :], whi[:, k, :].bitcast(F32), ALU.subtract).then_inc(w_lo, 1)
            dve.wait_ge(norm.g_in, FROM + 16)
            for i, tail in tiles(dve):
                n = DEC if tail else P
                dve.wait_ge(a_hi, FROM + i + 1)
                dve.wait_ge(mm_ready, FROM + 2 * i)
                v.tensor_tensor(alo[:].rearrange("p k t -> p (k t)"), at[:], ahi[:].rearrange("p k t -> p (k t)").bitcast(F32), ALU.subtract).then_inc(a_lo, 1)
                dve.wait_ge(x_in, FROM + 16 * i + 16)
                for g in range(2):
                    dve.wait_ge(mm_ready, FROM + 2 * i + g + 1)
                    v.tensor_tensor(x[:, g * 512:(g + 1) * 512], mm[g][:], x[:, g * 512:(g + 1) * 512], ALU.add).then_inc(added, 1)
                norm.dve_norm(dve, i)
                norm.dve_scale_g(dve, i)
                q = ds(i * P, n) if not tail else slice(SEQ, TOK)
                norm.dve_lo(dve, i, [hT[0][:, 0:4, q], hT[0][:, 4:8, q]], [hT[1][:, 0:4, q], hT[1][:, 4:8, q]], n)

        @block.tensor
        def _(pe):
            pe.wait_ge(w_lo, FROM + KD)
            for i, tail in tiles(pe):
                pe.wait_ge(a_in, FROM + 16 * i + 16)
                pe.wait_ge(a_lo, FROM + i)
                for k in range(KD):
                    last = nc.tensor.transpose(at[:, k * P:(k + 1) * P], a[:, k * P:(k + 1) * P], consts["ident"][:])
                last.then_inc(a_tp, 1)
                pe.wait_ge(a_lo, FROM + i + 1)
                pe.wait_ge(added, FROM + 2 * i)
                for g in range(2):
                    c = slice(g * 512, (g + 1) * 512)
                    for k in range(KD):
                        last = three_passes(nc, mm[g][:], (ahi[:, k, :], alo[:, k, :]), (whi[:, k, c], wlo[:, k, c]),
                                            k == 0, k == KD - 1)
                    last.then_inc(mm_ready, 1)
                norm.pe_transposes(pe, i)


def one_col(m):
    return slice(m, m + 1) if isinstance(m, int) else ds(m, 1)


TB = [(0, 384), (384, 384), (768, 320)]
CW = 2 + SEQ + 2 + DEC
NG = NF // 2


def conv_ffn(nc, dram, consts, layer, xres, hT, out, x_next):
    wup, wdn = dram["w_up"][layer], dram["w_down"][layer]
    last_layer = x_next is None
    with Phase(nc, f"ffn_{layer}") as ph:
        sb, sem = ph.sb, ph.sem
        uhi = [sb(f"uhi{c}", [P, 2, KD, P], F32R) for c in range(2)]
        ulo = [sb(f"ulo{c}", [P, 2, KD, P], F32R) for c in range(2)]
        dhi = sb("dhi", [P, 2, D], F32R)
        dlo = sb("dlo", [P, 2, D], F32R)
        uraw = sb("uraw", [P, 2, KD, P])
        draw = sb("draw", [P, 2, D])
        G = sb("G", [P, CW])
        cv = sb("cv", [P, 2, 384])
        ahi = sb("ahi", [P, 2, NT * P + P], F32R)
        alo = sb("alo", [P, 2, NT * P + P], F32R)
        rowbuf = cv[:].rearrange("p a n -> p (a n)")[:, 0:2 * P]
        ctap = sb("ctap", [P, 2, 4])
        tap = sb("tap", [P, 4 * NF])
        st = sb("st", [P, 2 * NF])
        tail = sb("tail", [P, 4, NF])
        up = [ph.ps(f"up{j}") for j in range(4)]
        dn = [ph.ps(f"dn{j}") for j in range(4)]
        uraw_in, u_hi, u_lo, draw_in, d_hi, d_lo = (sem("uraw_in"), sem("u_hi"), sem("u_lo"), sem("draw_in"),
                                                   sem("d_hi"), sem("d_lo"))
        tap_in, tap_tp, tap_ready, tail_ready, tail_tp, tail_out, state_out = (
            sem("tap_in"), sem("tap_tp"), sem("tap_ready"), sem("tail_ready"), sem("tail_tp"), sem("tail_out"), sem("state_out"))
        up_ready, g_out = sem("up_ready"), sem("g_out")
        c0_done, c1_done, c2_done, silu_done, a_done, ahi_done, alo_done = (
            sem("c0"), sem("c1"), sem("c2"), sem("silu"), sem("a_done"), sem("ahi_done"), sem("alo_done"))
        ctap_set = sem("ctap_set")
        dn_ready, dn_added, started, seam = sem("dn_ready"), sem("dn_added"), sem("started"), sem("seam")
        block = ph.block()
        wupv = wup.rearrange("(k p) (s f) -> p s k f", p=P, s=2)
        SEAM = 2 + SEQ

        def gcols(b):
            t0, n = TB[b]
            if t0 + n <= SEQ:
                return [(2 + t0, t0, n)]
            return [(2 + t0, t0, SEQ - t0), (SEAM + 2, SEQ, DEC)]

        @block.sync
        def _(sp):
            for j in range(3):
                sp.dma_start(rowbuf[j * NF:(j + 1) * NF, 0:P],
                             dram["w_conv"][layer, j].rearrange("(c p) -> c p", p=P)).then_inc(tap_in, 16)
            sp.dma_start(rowbuf[3 * NF:4 * NF, 0:P], dram["b_conv"][layer].rearrange("(c p) -> c p", p=P)).then_inc(tap_in, 16)
            for j in range(2):
                sp.dma_start(rowbuf[j * NF:(j + 1) * NF, P:2 * P],
                             dram["state_ffn_conv"][layer, 0, j].rearrange("(c p) -> c p", p=P)).then_inc(tap_in, 16)
            with sp.Fori(0, NG) as i:
                for c in range(2):
                    f = (2 * i + c) * P
                    sp.wait_ge(u_lo, FROM + 2 * i + c)
                    for s in range(2):
                        sp.dma_start(uraw[:, s], wupv[:, s, :, ds(f, P)]).then_inc(uraw_in, 16)
                    if c == 0:
                        sp.wait_ge(d_lo, FROM + i)
                        sp.dma_start(draw[:], wdn[ds(f, 2 * P), :].rearrange("(c p) n -> p c n", p=P)).then_inc(draw_in, 16)
            sp.wait_ge(tail_out, FROM + 1)
            for g, name in ((0, "p_conv"), (1, "s_conv")):
                for j in range(2):
                    r0 = (2 * g + j) * NF
                    sp.dma_start(out[name][layer, j].rearrange("(c p) -> c p", p=P), rowbuf[r0:r0 + NF, 0:P]).then_inc(state_out, 16)
            sp.wait_ge(state_out, FROM + 64)

        def upbank(c, b, s):
            return up[2 * ((3 * c + b) % 2) + s]

        def turns(eng):
            with eng.Fori(0, NG - 1) as i:
                yield i, True
            yield NG - 1, False

        @block.scalar
        def _(act):
            s = nc.scalar

            def split_up(m, c):
                act.wait_ge(uraw_in, FROM + 32 * m + 32)
                s.activation(uhi[c][:], uraw[:], ACT.Copy).then_inc(u_hi, 1)

            def split_down(i):
                act.wait_ge(draw_in, FROM + 16 * i + 16)
                act.wait_ge(dn_ready, FROM + 18 * i)
                s.activation(dhi[:], draw[:], ACT.Copy).then_inc(d_hi, 1)

            def chunk(i, c):
                for b in range(3):
                    m = 6 * i + 3 * c + b
                    n = TB[b][1]
                    if b == 0:
                        act.wait_ge(c2_done, FROM + m)
                        act.wait_ge(tail_ready, FROM + 2 * (2 * i + c))
                        act.wait_ge(seam, FROM + 2 * i + c + 1)
                    act.wait_ge(up_ready, FROM + m + 1)
                    for g0, t0, w in gcols(b):
                        j = t0 - TB[b][0]
                        s.activation(G[:, g0:g0 + w], upbank(c, b, 0)[:, j:j + w], ACT.Copy).then_inc(g_out, 1)
                    act.wait_ge(g_out, FROM + 8 * i + 4 * c + (b + 1 if b < 2 else 4))
                    act.wait_ge(silu_done, FROM + m)
                    for g0, t0, w in gcols(b):
                        j = t0 - TB[b][0]
                        last = s.activation(cv[:, 0, j:j + w], G[:, g0 - 2:g0 - 2 + w], ACT.Identity,
                                            scale=ctap[:, c, 0:1], bias=ctap[:, c, 3:4])
                    last.then_inc(c0_done, 1)
                    act.wait_ge(c2_done, FROM + m + 1)
                    act.wait_ge(alo_done, FROM + m)
                    s.activation(cv[:, 1, 0:n], cv[:, 0, 0:n], ACT.Silu).then_inc(silu_done, 1)
                    act.wait_ge(a_done, FROM + m + 1)
                    act.wait_ge(dn_ready, FROM + 18 * i)
                    t0 = TB[b][0]
                    s.activation(ahi[:, c, t0:t0 + n], cv[:, 1, 0:n], ACT.Copy).then_inc(ahi_done, 1)

            s.preload_act_table_set("silu_and_others")
            split_up(0, 0)
            split_up(1, 1)
            split_down(0)
            act.wait_ge(tap_ready, FROM + 2)
            for i, more in turns(act):
                for c in range(2):
                    chunk(i, c)
                    if more:
                        split_up(2 * i + 2 + c, c)
                if more:
                    split_down(i + 1)

        @block.vector
        def _(dve):
            v = nc.vector

            def split_up(m, c):
                dve.wait_ge(u_hi, FROM + m + 1)
                v.tensor_tensor(ulo[c][:].rearrange("p s k f -> p (s k f)"), uraw[:].rearrange("p s k f -> p (s k f)"),
                                uhi[c][:].rearrange("p s k f -> p (s k f)").bitcast(F32), ALU.subtract).then_inc(u_lo, 1)

            def split_down(i):
                dve.wait_ge(d_hi, FROM + i + 1)
                v.tensor_tensor(dlo[:], draw[:], dhi[:].bitcast(F32), ALU.subtract).then_inc(d_lo, 1)

            def chunk(i, c):
                dve.wait_ge(c2_done, FROM + 6 * i + 3 * c)
                m = 2 * i + c
                v.tensor_copy(ctap[:, c, :], tap[:].rearrange("p (j c) -> p j c", j=4)[:, :, one_col(m)]).then_inc(ctap_set, 1)
                dve.wait_ge(ctap_set, FROM + m + 1)
                v.tensor_copy(G[:, SEAM:SEAM + 2], st[:].rearrange("p (j c) -> p j c", j=2)[:, :, one_col(m)]).then_inc(seam, 1)
                for b in range(3):
                    m = 6 * i + 3 * c + b
                    t0, n0 = TB[b]
                    dve.wait_ge(c0_done, FROM + m + 1)
                    for tapno, done in ((1, c1_done), (2, c2_done)):
                        if tapno == 2:
                            dve.wait_ge(c1_done, FROM + m + 1)
                        for g0, t1, w in gcols(b):
                            j = t1 - t0
                            last = v.scalar_tensor_tensor(cv[:, 0, j:j + w], G[:, g0 - 2 + tapno:g0 - 2 + tapno + w],
                                                          ctap[:, c, tapno:tapno + 1], cv[:, 0, j:j + w], ALU.mult, ALU.add)
                        last.then_inc(done, 1)
                    if b == 2:
                        for g, col in ((0, SEAM - 2), (1, CW - 2)):
                            v.tensor_copy(tail[:, 2 * g:2 * g + 2, one_col(2 * i + c)], G[:, col:col + 2]).then_inc(tail_ready, 1)
                    dve.wait_ge(silu_done, FROM + m + 1)
                    v.tensor_tensor(cv[:, 1, 0:n0], upbank(c, b, 1)[:, 0:n0], cv[:, 1, 0:n0], ALU.mult).then_inc(a_done, 1)
                    dve.wait_ge(ahi_done, FROM + m + 1)
                    v.tensor_tensor(alo[:, c, t0:t0 + n0], cv[:, 1, 0:n0], ahi[:, c, t0:t0 + n0].bitcast(F32),
                                    ALU.subtract).then_inc(alo_done, 1)

            v.memset(G[:, 0:2], 0.0).then_inc(started, 1)
            v.memset(ahi[:, :, TOK:].bitcast(F32), 0.0).then_inc(started, 1)
            v.memset(alo[:, :, TOK:].bitcast(F32), 0.0).then_inc(started, 1)
            dve.wait_ge(started, FROM + 3)
            split_up(0, 0)
            split_up(1, 1)
            split_down(0)
            for b, (dst, n) in enumerate(((tap, 4 * NF), (st, 2 * NF))):
                dve.wait_ge(tap_tp, FROM + b + 1)
                v.tensor_copy(dst[:], dn[b][:, 0:n]).then_inc(tap_ready, 1)
            dve.wait_ge(tap_ready, FROM + 2)
            for i, more in turns(dve):
                for c in range(2):
                    chunk(i, c)
                    if more and c == 0:
                        split_up(2 * i + 2, 0)
                for t in range(TILES):
                    if more and t == NT // 2:
                        split_up(2 * i + 3, 1)
                    for g in range(2):
                        j, n = 2 * t + g, queries(t)
                        dve.wait_ge(dn_ready, FROM + 18 * i + j + 1)
                        xs = xres[0:n, t, g * 512:(g + 1) * 512]
                        v.tensor_tensor(xs, dn[j % 4][0:n, :], xs, ALU.add).then_inc(dn_added, 1)
                if more:
                    split_down(i + 1)
            dve.wait_ge(tail_tp, FROM + 1)
            v.tensor_copy(rowbuf[0:4 * NF, 0:P], up[0][0:4 * NF, 0:P]).then_inc(tail_out, 1)

        @block.tensor
        def _(pe):
            pe.wait_ge(tap_in, FROM + 96)
            for b, n in enumerate((4 * NF, 2 * NF)):
                nc.tensor.transpose(dn[b][:, 0:n], rowbuf[0:n, b * P:(b + 1) * P], consts["ident"][0:n, 0:n]).then_inc(tap_tp, 1)
            pe.wait_ge(tap_ready, FROM + 2)
            with pe.Fori(0, NG) as i:
                for c in range(2):
                    pe.wait_ge(u_lo, FROM + 2 * i + c + 1)
                    for b, (t0, n) in enumerate(TB):
                        if 3 * c + b >= 2:
                            pe.wait_ge(a_done, FROM + 6 * i + 3 * c + b - 1)
                        for s in range(2):
                            for k in range(KD):
                                last = three_passes(nc, upbank(c, b, s)[:, 0:n],
                                                    (uhi[c][:, s, k, :], ulo[c][:, s, k, :]),
                                                    (hT[0][:, k, t0:t0 + n], hT[1][:, k, t0:t0 + n]), k == 0, k == KD - 1)
                        last.then_inc(up_ready, 1)
                pe.wait_ge(d_lo, FROM + i + 1)
                pe.wait_ge(started, FROM + 3)
                for t in range(TILES):
                    pe.wait_ge(alo_done, FROM + 6 * i + 3 + min(2, ((t + 1) * P - 1) // 384) + 1)
                    for g in range(2):
                        j = 2 * t + g
                        pe.wait_ge(dn_added, FROM + 18 * i + max(0, j - 3))
                        for c in range(2):
                            last = three_passes(nc, dn[j % 4][:], (ahi[:, c, t * P:(t + 1) * P], alo[:, c, t * P:(t + 1) * P]),
                                                (dhi[:, c, g * 512:(g + 1) * 512], dlo[:, c, g * 512:(g + 1) * 512]), c == 0, c == 1)
                        last.then_inc(dn_ready, 1)
            pe.wait_ge(tail_ready, FROM + 2 * NF)
            nc.tensor.transpose(up[0][0:4 * NF, 0:P], tail[:].rearrange("p j c -> p (j c)"), consts["ident"][:]).then_inc(tail_tp, 1)

    if not last_layer:
        with Phase(nc, f"keep_{layer}") as ph:
            done = ph.sem("done")
            block = ph.block()

            @block.sync
            def _(sp):
                sp.dma_start(x_next[0].rearrange("(t p) n -> p t n", p=P), xres[:, 0:NT, :]).then_inc(done, 16)
                sp.dma_start(x_next[1], xres[0:DEC, NT, :]).then_inc(done, 16)
                sp.wait_ge(done, FROM + 32)


def final_norm(nc, dram, consts, xres, out):
    with Phase(nc, "final") as ph:
        sb, sem = ph.sb, ph.sem
        g = sb("g", [P, D])
        junk = sb("junk", [P, D])
        y = sb("y", [P, 2, D])
        st = sb("st", [P, 3, TILES])
        g_in, sq, step, rt, y_ready, stored = sem("g_in"), sem("sq"), sem("step"), sem("rt"), sem("y_ready"), [sem("stored0"), sem("stored1")]
        block = ph.block()

        @block.sync
        def _(sp):
            sp.dma_start(g[:], dram["g_final"].unsqueeze(0).to_broadcast([P, D])).then_inc(g_in, 16)
            for t in range(TILES):
                sp.wait_ge(y_ready, FROM + t + 1)
                n = queries(t)
                dst = out["y_sample"] if t == NT else out["y_prompt"][t * P:(t + 1) * P]
                sp.dma_start(dst, y[0:n, t % 2, :]).then_inc(stored[t % 2], 16)
            sp.wait_ge(stored[0], FROM + 16 * ((TILES + 1) // 2))
            sp.wait_ge(stored[1], FROM + 16 * (TILES // 2))

        @block.scalar
        def _(act):
            for t in range(TILES):
                n = queries(t)
                if t:
                    act.wait_ge(sq, FROM + t)
                nc.scalar.activation(junk[0:n, :], xres[0:n, t, :], ACT.Square, scale=D ** -0.5,
                                     accum_out=st[0:n, 0, t:t + 1]).then_inc(sq, 1)
            act.wait_ge(step, FROM + 1)
            act.wait_ge(sq, FROM + TILES)
            nc.scalar.activation(st[:, 1, :], st[:, 0, :], ACT.Sqrt, bias=consts["eps"][:]).then_inc(rt, 1)

        @block.vector
        def _(dve):
            v = nc.vector
            v.memset(st[DEC:P, 0, NT:NT + 1], 1.0).then_inc(step, 1)
            dve.wait_ge(rt, FROM + 1)
            v.reciprocal(st[:, 2, :], st[:, 1, :]).then_inc(step, 1)
            dve.wait_ge(step, FROM + 2)
            dve.wait_ge(g_in, FROM + 16)
            for t in range(TILES):
                n = queries(t)
                if t >= 2:
                    dve.wait_ge(stored[t % 2], FROM + 16 * (t // 2))
                v.scalar_tensor_tensor(y[0:n, t % 2, :], xres[0:n, t, :], st[0:n, 2, t:t + 1], g[0:n, :], ALU.mult,
                                       ALU.mult).then_inc(y_ready, 1)


def hybrid_step(nc, dram, out):
    with ExitStack() as ctx:
        def sb(name, shape, dt=F32):
            return ctx.enter_context(nc.sbuf_tensor(name, shape, dt))

        ident, ident_bf = sb("ident", [P, P]), sb("ident_bf", [P, P], BF16)
        masks = {n: sb(n, [P, P], BF16) for n in ("mask_chunk", "mask_causal", "mask_strict")}
        eps = sb("eps", [P, 1])
        consts = {"ident": ident, "ident_bf": ident_bf, "eps": eps, **masks}

        with Phase(nc, "start") as ph:
            raw = ph.sb("raw", [P, 3, P])
            got, done = ph.sem("got"), ph.sem("done")
            block = ph.block()

            @block.sync
            def _(sp):
                sp.dma_start(ident[:], dram["patterns"][0]).then_inc(got, 16)
                for j in range(3):
                    sp.dma_start(raw[:, j, :], dram["patterns"][1 + j]).then_inc(got, 16)

            @block.vector
            def _(dve):
                dve.wait_ge(got, FROM + 64)
                nc.vector.tensor_copy(ident_bf[:], ident[:])
                nc.vector.memset(eps[:], EPS)
                for j, m in enumerate(("mask_chunk", "mask_causal", "mask_strict")):
                    nc.vector.tensor_scalar(masks[m][:], raw[:, j, :], NEG, None, ALU.mult)

        x0 = (dram["x_prompt"][0], dram["x_sample"][0])
        with ExitStack() as even:
            def esb(name, shape, dt=F32):
                return even.enter_context(nc.sbuf_tensor(name, shape, dt))

            widths = [key_tile(t)[0] for t in range(TILES)]
            src = {"qaT": esb("qaT", [P, 4, TOK]), "kaT": esb("kaT", [P, KEYS]), "v": esb("va", [P, KT, P]),
                   "qiT": esb("qiT", [P, 2, TOK]), "kiT": esb("kiT", [P, KEYS]), "wi": esb("wi", [P, TILES, 8]),
                   "latT": esb("latT", [P, KEYS]), "krT": esb("krT", [96, KEYS]),
                   "bias_at": [sum(widths[:t]) for t in range(TILES)]}
            projection(nc, dram, consts, "even", x0, dram["g_mix"][0], dram["w_in_even"][0], src, out)
            src["bias"] = esb("bias", [P, sum(widths)], BF16)
            src["work"] = {t: esb(f"scores{t}", [P, widths[t]]) for t in sorted(sum(TOPK_TILES, ()))}
            index_scores(nc, dram, consts, src)
            attention(nc, dram, consts, "b", src)
            attention(nc, dram, consts, "a", src)

        with ExitStack() as ff:
            xres = ff.enter_context(nc.sbuf_tensor("xres", [P, TILES, D], F32))
            hT = [ff.enter_context(nc.sbuf_tensor(f"hT{j}", [P, KD, TOK], F32R)) for j in range(2)]
            output_projection(nc, dram, consts, 0, dram["w_o_even"][0], x0, xres, hT)
            x1 = (dram["x1"][0:SEQ], dram["x1"][SEQ:TOK])
            conv_ffn(nc, dram, consts, 0, xres, hT, out, x1)

        for kind, c0, w in (("c", 0, C_IN), ("d", C_IN, D_IN)):
            with ExitStack() as odd:
                def osb(name, shape, dt=F32):
                    return odd.enter_context(nc.sbuf_tensor(f"{kind}_{name}", shape, dt))

                src = {"qT": osb("qT", [P, 4, TOK]), "kT": osb("kT", [P, 4, KEYS]), "v": osb("v", [P, KT, 512])}
                if kind == "c":
                    src["fc"] = osb("fc", [P, KT, 8])
                projection(nc, dram, consts, kind, x1, dram["g_mix"][1], dram["w_in_odd"][0][:, c0:c0 + w], src, out)
                if kind == "c":
                    src.update(fq=osb("fq", [P, TILES * P], F32R), fk_all=osb("fk_all", [P, KEYS]), onehot=osb("onehot", [P, 8]))
                    forget(nc, dram, consts, src["fc"], src, out)
                attention(nc, dram, consts, kind, src)

        with ExitStack() as ff:
            xres = ff.enter_context(nc.sbuf_tensor("xres_1", [P, TILES, D], F32))
            hT = [ff.enter_context(nc.sbuf_tensor(f"hT{j}_1", [P, KD, TOK], F32R)) for j in range(2)]
            output_projection(nc, dram, consts, 1, dram["w_o_odd"][0], x1, xres, hT)
            conv_ffn(nc, dram, consts, 1, xres, hT, out, None)
            final_norm(nc, dram, consts, xres, out)


_INS = ["x_prompt", "x_sample", "cache_a_k", "cache_a_v", "cache_a_idx_k", "cache_b_latent", "cache_b_rope",
        "cache_c_k", "cache_c_v", "cache_c_logf", "cache_d_k", "cache_d_v", "state_ffn_conv",
        "g_mix", "g_ffn", "g_final", "w_in_even", "g_b_q", "g_b_kv", "w_b_uq", "w_b_ukv", "w_o_even",
        "w_in_odd", "b_forget", "w_o_odd", "w_up", "w_conv", "b_conv", "w_down"]
_OUTS = [("y_prompt", (1, SEQ, D), (SEQ, D)), ("y_sample", (1, DEC, D), (DEC, D))] + [
    (f"{g}_{name}", (1, 1, n) + shape, (n, flat)) if name != "conv" else (f"{g}_conv", (2, 1, 2, FF), (2, 2, FF))
    for g, n in (("p", SEQ), ("s", DEC))
    for name, shape, flat in (("a_k", (2, 64), 128), ("a_v", (2, 64), 128), ("a_idx_k", (32,), 32),
                              ("b_latent", (KVR,), KVR), ("b_rope", (32,), 32), ("c_k", (8, 64), 512),
                              ("c_v", (8, 64), 512), ("c_logf", (8,), 8), ("d_k", (8, 64), 512),
                              ("d_v", (8, 64), 512), ("conv", (), 0))]


def _constants():
    import numpy as np

    f = np.float32
    pos = np.concatenate([np.arange(SEQ), PAST + np.arange(DEC), np.zeros(P - DEC)]).astype(f)
    tabs = []
    for n_rot in (16, 8, 32):
        half = n_rot // 2
        inv = f(500000.0) ** (-np.arange(half, dtype=f) * f(2.0) / f(n_rot))
        ang = pos[:, None] * inv.astype(f)[None, :]
        tabs += [np.cos(ang), np.sin(ang)]
    trig = np.concatenate(tabs, axis=1).astype(f).reshape(TILES, P, ROPE_COLS)
    i = np.arange(P)
    hidden = [np.eye(P), (i[:, None] < P // 2) & (i[None, :] >= P // 2), i[None, :] > i[:, None], i[None, :] >= i[:, None]]
    return {"trig": trig, "patterns": np.stack(hidden).astype(f)}


def kernel(**inputs):
    import numpy as _np
    import concourse.bacc as _bacc
    from concourse import mybir as _mybir
    from concourse.bass_utils import run_bass_kernel_spmd as _run

    nc = _bacc.Bacc("TRN2", target_bir_lowering=False, num_devices=1)
    arrays, dram, out = {}, {}, {}
    for name, a in [(n, _np.ascontiguousarray(inputs[n])) for n in _INS] + list(_constants().items()):
        arrays[f"in_{name}_dram"] = a
        dram[name] = nc.dram_tensor(f"in_{name}_dram", a.shape, _mybir.dt.from_np(a.dtype), kind="ExternalInput").ap()
    for name, shape, flat in _OUTS:
        out[name] = nc.dram_tensor(f"out_{name}_dram", flat, F32, kind="ExternalOutput").ap()
    for name, shape in (("qbT", (8, 96, TOK)), ("att", (TOK, D)), ("x1", (TOK, D))):
        dram[name] = nc.dram_tensor(f"scratch_{name}", shape, F32, kind="Internal").ap()
    hybrid_step(nc, dram, out)
    r = _run(nc, [arrays], core_ids=[0])
    return tuple(r.results[0][f"out_{name}_dram"].reshape(shape) for name, shape, flat in _OUTS)
```

```python
from contextlib import ExitStack

import concourse.bass as bass
from concourse import mybir

F32 = mybir.dt.float32
F32R = mybir.dt.float32r
BF16 = mybir.dt.bfloat16
ALU = mybir.AluOpType
ACT = mybir.ActivationFunctionType
AX_X = mybir.AxisListType.X
ds = bass.ds

P = 128
D = 1024
KD = D // P
SEQ, DEC, PAST = 1024, 64, 256
NT = SEQ // P
TOK = SEQ + DEC
KEYS = SEQ + PAST + DEC
OWN = SEQ + PAST
KT = NT + PAST // P + 1
EPS = 1e-6
HD = 64
C_IN, D_IN = 1544, 1536
TOPK_P, TOPK_S = 256, 80
QR, KVR = 256, 128
FF = 2816
NF = FF // P
NEG = -1.0e30
GONE = -3.4e38
ROPE_COLS = 2 * (8 + 4 + 16)
RA, RI, RB = 0, 16, 24


FROM = 1


class Phase:

    def __init__(self, nc, name):
        self.nc, self.name, self.ctx, self.sems = nc, name, ExitStack(), []

    def __enter__(self):
        self.ctx.__enter__()
        return self

    def __exit__(self, *a):
        return self.ctx.__exit__(*a)

    def sb(self, name, shape, dt=F32):
        return self.ctx.enter_context(self.nc.sbuf_tensor(f"{self.name}_{name}", shape, dt))

    def ps(self, name, shape=(P, 512), dt=F32):
        return self.ctx.enter_context(self.nc.psum_tensor(f"{self.name}_{name}", list(shape), dt))

    def sem(self, name):
        s = self.ctx.enter_context(self.nc.semaphore(f"{self.name}_{name}"))
        self.sems.append(s)
        return s

    def block(self):
        def reset(eng, share):
            for s in self.sems[share::4]:
                eng.sem_clear(s)
                eng.sem_inc(s, FROM)

        with self.nc.Block() as start:
            @start.sync
            def _(sp):
                reset(sp, 0)

            @start.tensor
            def _(pe):
                reset(pe, 1)

            @start.vector
            def _(dve):
                reset(dve, 2)

            @start.scalar
            def _(act):
                reset(act, 3)
        return self.ctx.enter_context(self.nc.Block())


def bc(ap, n):
    return ap.unsqueeze(2).to_broadcast([ap.shape[0], ap.shape[1], n])


def one(ap, i):
    if isinstance(i, int):
        return ap[:, i]
    return ap[:, ds(i, 1)].rearrange("p a n -> p (a n)")


def rows(ap, i, n):
    return ap[i:i + n] if isinstance(i, int) else ap[ds(i, n)]


def key_tile(t):
    return (P * (t + 1), 0) if t < NT else (PAST + DEC, SEQ)


def steps(eng):
    yield 0, 0
    with eng.Fori(0, (NT - 2) // 2) as j:
        yield 2 * j + 1, 1
        yield 2 * j + 2, 0
    yield NT - 1, 1
    yield NT, 0


def is_last(i):
    return isinstance(i, int) and i == NT


def is_first(i):
    return isinstance(i, int) and i == 0


def span(i):
    if is_last(i):
        return DEC, slice(SEQ, TOK), slice(OWN, KEYS), KT - 1
    q = slice(i * P, (i + 1) * P) if isinstance(i, int) else ds(i * P, P)
    return P, q, q, i


class Norm:

    def __init__(self, ph, nc, consts, x, g_dram, hn=None, hf=None):
        self.nc, self.x = nc, x
        self.ident = consts["ident"]
        self.g_dram = g_dram
        self.junk = ph.sb("junk", [P, D], BF16)
        self.hn = ph.sb("hn", [P, D]) if hn is None else hn
        self.hf = ph.sb("hf", [P, KD, P]) if hf is None else hf
        self.gT = ph.sb("gT", [P, KD])
        self.eps = consts["eps"]
        self.stat = ph.sb("stat", [P, 3])
        self.tp = [ph.ps("ht0"), ph.ps("ht1")]
        self.g_in = ph.sem("g_in")
        self.ssq = ph.sem("ssq")
        self.rt = ph.sem("rt")
        self.rinv = ph.sem("rinv")
        self.hn_ready = ph.sem("hn_ready")
        self.ht_ready = ph.sem("ht_ready")
        self.hf_ready = ph.sem("hf_ready")
        self.hi_ready = ph.sem("hi_ready")
        self.lo_ready = ph.sem("lo_ready")

    def load_g(self, sp):
        sp.dma_start(self.gT[:], self.g_dram.rearrange("(k p) -> p k", p=P),
                     allow_slow_non_contiguous=True).then_inc(self.g_in, 16)

    def act_square(self, act, i, x_sem, x_val):
        act.wait_ge(x_sem, FROM + x_val)
        act.wait_ge(self.hn_ready, FROM + i)
        self.nc.scalar.activation(self.junk[:], self.x, ACT.Square, scale=D ** -0.5,
                                  accum_out=self.stat[:, 0:1]).then_inc(self.ssq, 1)

    def act_root(self, act, i):
        act.wait_ge(self.ssq, FROM + i + 1)
        self.nc.scalar.activation(self.stat[:, 1:2], self.stat[:, 0:1], ACT.Sqrt, bias=self.eps[:]).then_inc(self.rt, 1)

    def dve_norm(self, dve, i):
        v = self.nc.vector
        dve.wait_ge(self.rt, FROM + i + 1)
        v.reciprocal(self.stat[:, 2:3], self.stat[:, 1:2]).then_inc(self.rinv, 1)
        dve.wait_ge(self.rinv, FROM + i + 1)
        dve.wait_ge(self.ht_ready, FROM + i * 2)
        v.tensor_scalar(self.hn[:], self.x, self.stat[:, 2:3], None, ALU.mult).then_inc(self.hn_ready, 1)

    def pe_transposes(self, pe, i):
        pe.wait_ge(self.hn_ready, FROM + i + 1)
        pe.wait_ge(self.hf_ready, FROM + i * 2)
        for b in range(2):
            for k in range(4):
                last = self.nc.tensor.transpose(self.tp[b][:, k * P:(k + 1) * P],
                                                self.hn[:, (4 * b + k) * P:(4 * b + k + 1) * P], self.ident[:])
            last.then_inc(self.ht_ready, 1)

    def dve_scale_g(self, dve, i):
        dve.wait_ge(self.hi_ready, FROM + i * 2)
        dve.wait_ge(self.lo_ready, FROM + i * 2)
        if isinstance(i, int) and i == 0:
            dve.wait_ge(self.g_in, FROM + 16)
        for b in range(2):
            dve.wait_ge(self.ht_ready, FROM + i * 2 + b + 1)
            self.nc.vector.tensor_tensor(self.hf[:, 4 * b:4 * b + 4, :],
                                         self.tp[b][:].rearrange("p (k t) -> p k t", k=4),
                                         bc(self.gT[:, 4 * b:4 * b + 4], P), ALU.mult).then_inc(self.hf_ready, 1)

    def act_hi(self, act, i, hi, n=P):
        for b in range(2):
            act.wait_ge(self.hf_ready, FROM + i * 2 + b + 1)
            self.nc.scalar.activation(hi[b], self.hf[:, 4 * b:4 * b + 4, 0:n], ACT.Copy).then_inc(self.hi_ready, 1)

    def dve_lo(self, dve, i, hi, lo, n=P):
        for b in range(2):
            dve.wait_ge(self.hf_ready, FROM + i * 2 + b + 1)
            dve.wait_ge(self.hi_ready, FROM + i * 2 + b + 1)
            self.nc.vector.tensor_tensor(lo[b], self.hf[:, 4 * b:4 * b + 4, 0:n], hi[b].bitcast(F32),
                                         ALU.subtract).then_inc(self.lo_ready, 1)


def three_passes(nc, out, lhs, rhs, first, last):
    (lh, ll), (rh, rl) = lhs, rhs
    nc.tensor.matmul(out, lh, rh, start=first, stop=False)
    nc.tensor.matmul(out, lh, rl, start=False, stop=False)
    return nc.tensor.matmul(out, ll, rh, start=False, stop=last)


def projection(nc, dram, consts, kind, x_src, g_dram, w_dram, dst, out):
    even, fox = kind == "even", kind == "c"
    width = w_dram.shape[1]
    ng = 4 if fox else 3
    gw = [494, 494, 492] if even else [386] * 4 if fox else [512] * 3
    go = [sum(gw[:g]) for g in range(ng)]
    nw = 1 if even else 2
    ww = width // nw
    ident = consts["ident"]
    with Phase(nc, f"proj_{kind}") as ph:
        sb, sem = ph.sb, ph.sem
        whi = sb("whi", [P, KD, width], F32R)
        wlo = sb("wlo", [P, KD, width], F32R)
        wraw = sb("wraw", [P, 2, ww])
        x = sb("x", [P, D])
        hhi = [sb(f"hhi{s}", [P, KD, P], F32R) for s in range(2)]
        hlo = [sb(f"hlo{s}", [P, KD, P], F32R) for s in range(2)]
        proj = sb("proj", [P, width])
        trig = sb("trig", [P, TILES, ROPE_COLS]) if even else None
        norm = Norm(ph, nc, consts, x[:], g_dram)
        mm = [ph.ps(f"mm{g}") for g in range(ng)]
        tq = [ph.ps(f"tq{g}") for g in range(6 - ng)]
        landing = [wraw[:, 0, :], wraw[:, 1, :]] + [proj[:, j * ww:(j + 1) * ww] for j in range(nw)]
        nl = len(landing)
        w_in = [sem(f"w_in{j}") for j in range(nl)]
        w_hi, w_lo = sem("w_hi"), sem("w_lo")
        x_in, trig_in = sem("x_in"), sem("trig_in")
        mm_ready, proj_act = sem("mm_ready"), sem("proj_act")
        tq_ready, tq_act, qb_tp = sem("tq_ready"), sem("tq_act"), sem("qb_tp")
        stored, cache_in, cache_tp, cache_cp = sem("stored"), sem("cache_in"), sem("cache_tp"), sem("cache_cp")
        post, dve_step, passed, kept = sem("post"), sem("dve_step"), sem("passed"), sem("kept")
        dve_rope, zeroed, rr_done = sem("dve_rope"), sem("zeroed"), sem("rr_done")
        if even:
            gq = sb("gq", [P, QR])
            gkv = sb("gkv", [P, KVR])
            wuq = sb("wuq", [P, 2, 768])
            qbT = sb("qbT", [96, 8, P])
            nst = sb("nst", [P, 6])
            free, at = wraw[:].rearrange("p s n -> p (s n)"), [0]

            def take(n):
                at[0] += n
                return free[:, at[0] - n:at[0]]

            qb = take(8 * 96).rearrange("p (h d) -> p h d", h=8)
            rot = take(4 * 10 * 16).rearrange("p (j n) -> p j n", j=4)
            cqT = take(2 * P).rearrange("p (c t) -> p c t", c=2)
            aq, cqn, lat = take(4 * P), take(QR), take(KVR)
            stage = take(P + 96)
            sq_done, rt_done = sem("sq_done"), sem("rt_done")
            cqT_ready, qb_mm, qb_cp, qbT_ready, gq_in, qbT_stored = (
                sem("cqT_ready"), sem("qb_mm"), sem("qb_cp"), sem("qbT_ready"), sem("gq_in"),
                sem("qbT_stored"))
        rows4 = norm.hn[:].rearrange("p (b c n) -> p b c n", b=2, c=4)
        if even:
            ck, ci, cl, cr = rows4[:, :, 0], rows4[:, :, 1], rows4[:, :, 2], rows4[:, :, 3, 0:96]

        nstore = 5 if even else 2
        ntq = 3 if even else 2

        block = ph.block()

        @block.sync
        def _(sp):
            def load_w(c):
                k, w0 = c // nw, (c % nw) * ww
                if c >= nl:
                    sp.wait_ge(w_lo, FROM + c - nl + 1)
                sp.dma_start(landing[c % nl], w_dram[k * P:(k + 1) * P, w0:w0 + ww]).then_inc(w_in[c % nl], 16)

            def load(i):
                if not is_first(i):
                    sp.wait_ge(norm.hn_ready, FROM + i)
                if is_last(i):
                    sp.dma_start(x[0:DEC, :], x_src[1]).then_inc(x_in, 16)
                else:
                    sp.dma_start(x[:], rows(x_src[0], i * P, P)).then_inc(x_in, 16)

            def store(i):
                n, pre, r0 = (DEC, "s", 0) if is_last(i) else (P, "p", i * P)

                def put(name, src):
                    sp.dma_start(rows(out[f"{pre}_{name}"], r0, n), src).then_inc(stored, 16)

                if not even:
                    sp.wait_ge(proj_act, FROM + ng * i + ng)
                    put(f"{kind}_k", proj[0:n, 512:1024])
                    put(f"{kind}_v", proj[0:n, 1024:1536])
                    return
                sp.wait_ge(post, FROM + i + 1)
                put("a_k", proj[0:n, 512:640])
                put("a_v", proj[0:n, 640:768])
                put("a_idx_k", proj[0:n, 1024:1056])
                put("b_latent", lat[0:n, :])
                put("b_rope", proj[0:n, 1448:1480])
                sp.wait_ge(qbT_ready, FROM + 2 * i + 2)
                sp.sem_inc(passed, 1)
                sp.dma_start(dram["qbT"][:, :, span(i)[1]].rearrange("h d t -> d h t"), qbT[:, :, 0:n]).then_inc(qbT_stored, 16)

            for c in range(2):
                load_w(c)
            for b in range(2):
                r = slice(b * P, (b + 1) * P)
                if even:
                    sp.dma_start(ck[:, b], dram["cache_a_k"][0, 0, r].rearrange("t g d -> t (g d)")).then_inc(cache_in, 16)
                    sp.dma_start(dst["v"][:, NT + b, :], dram["cache_a_v"][0, 0, r].rearrange("t g d -> t (g d)")).then_inc(cache_in, 16)
                    for c in range(4):
                        sp.dma_start(ci[:, b, c * 32:c * 32 + 32], dram["cache_a_idx_k"][0, 0, r]).then_inc(cache_in, 16)
                    sp.dma_start(cl[:, b, :], dram["cache_b_latent"][0, 0, r]).then_inc(cache_in, 16)
                    sp.dma_start(cr[:, b, 64:96], dram["cache_b_rope"][0, 0, r]).then_inc(cache_in, 16)
                else:
                    sp.dma_start(rows4[:, b].rearrange("p a n -> p (a n)"),
                                 dram[f"cache_{kind}_k"][0, 0, r].rearrange("t g d -> t (g d)")).then_inc(cache_in, 16)
                    sp.dma_start(dst["v"][:, NT + b, :],
                                 dram[f"cache_{kind}_v"][0, 0, r].rearrange("t g d -> t (g d)")).then_inc(cache_in, 16)
            load(0)
            norm.load_g(sp)
            for c in range(2, KD * nw):
                load_w(c)
            if even:
                sp.dma_start(trig[:], dram["trig"].rearrange("t p n -> p t n")).then_inc(trig_in, 16)
                sp.dma_start(gq[:], dram["g_b_q"][0:1, :].to_broadcast([P, QR])).then_inc(gq_in, 16)
                sp.dma_start(gkv[:], dram["g_b_kv"][0:1, :].to_broadcast([P, KVR])).then_inc(gq_in, 16)
                sp.dma_start(wuq[:], dram["w_b_uq"][0].rearrange("(k p) n -> p k n", p=P)).then_inc(gq_in, 16)
            load(1)
            with sp.Fori(0, NT - 2) as i:
                load(i + 2)
                store(i)
            load(NT)
            for i in (NT - 2, NT - 1, NT):
                store(i)
            sp.wait_ge(stored, FROM + TILES * 16 * nstore)
            if even:
                sp.wait_ge(qbT_stored, FROM + TILES * 16)

        @block.scalar
        def _(act):
            s = nc.scalar
            s.preload_act_table_set("sqrt_and_others")

            def split_w(c):
                k, w0 = c // nw, (c % nw) * ww
                act.wait_ge(w_in[c % nl], FROM + 16 * (c // nl + 1))
                s.activation(whi[:, k, w0:w0 + ww], landing[c % nl], ACT.Copy).then_inc(w_hi, 1)

            def cache():
                for b in range(2):
                    act.wait_ge(cache_tp, FROM + b + 1)
                    c0 = SEQ + b * P
                    if even:
                        s.activation(dst["kaT"][:, c0:c0 + P], mm[b][:, 0:P], ACT.Copy)
                        s.activation(dst["kiT"][:, c0:c0 + P], mm[b][:, P:2 * P], ACT.Copy)
                        s.activation(dst["latT"][:, c0:c0 + P], mm[b][:, 2 * P:3 * P], ACT.Copy)
                        s.activation(dst["krT"][64:96, c0:c0 + P], mm[b][64:96, 3 * P:4 * P], ACT.Copy).then_inc(cache_cp, 1)
                    else:
                        s.activation(dst["kT"][:, :, c0:c0 + P], mm[b][:].rearrange("p (c t) -> p c t", c=4),
                                     ACT.Copy).then_inc(cache_cp, 1)

            def mean_square(i):
                norm.act_square(act, i, x_in, i * 16 + 16)
                norm.act_root(act, i)

            def high(i, slot):
                if not is_first(i):
                    act.wait_ge(mm_ready, FROM + ng * (i - 1))
                norm.act_hi(act, i, [hhi[slot][:, 0:4, :], hhi[slot][:, 4:8, :]])

            def feature_major(i):
                n, q, kk, _ = span(i)
                act.wait_ge(tq_ready, FROM + ntq * i + 1)
                s.activation(dst["qaT" if even else "qT"][:, :, q], tq[0][:].rearrange("p (c t) -> p c t", c=4)[:, :, 0:n],
                             ACT.Copy, scale=HD ** -0.5).then_inc(tq_act, 1)
                act.wait_ge(tq_ready, FROM + ntq * i + 2)
                if even:
                    s.activation(dst["kaT"][:, kk], tq[1][:, 0:n], ACT.Copy)
                    s.activation(dst["kiT"][:, kk], tq[1][:, P:P + n], ACT.Copy)
                    s.activation(dst["latT"][:, kk], tq[1][:, 2 * P:2 * P + n], ACT.Copy)
                    s.activation(dst["krT"][64:96, kk], tq[1][64:96, 3 * P:3 * P + n], ACT.Copy).then_inc(tq_act, 1)
                else:
                    s.activation(dst["kT"][:, :, kk], tq[1][:].rearrange("p (c t) -> p c t", c=4)[:, :, 0:n],
                                 ACT.Copy).then_inc(tq_act, 1)

            def up_query(i):
                for g in range(2):
                    act.wait_ge(qb_mm, FROM + 2 * i + g + 1)
                    s.activation(qb[:, 4 * g:4 * g + 4, :].rearrange("p h d -> p (h d)"), tq[g][:, 0:384],
                                 ACT.Copy).then_inc(qb_cp, 1)

            def up_query_T(i):
                for g in range(2):
                    act.wait_ge(qb_tp, FROM + 2 * i + g + 1)
                    if g == 0:
                        act.wait_ge(qbT_stored, FROM + i * 16)
                    s.activation(qbT[:, 4 * g:4 * g + 4, :], tq[g][0:96, :].rearrange("p (h t) -> p h t", h=4),
                                 ACT.Copy, scale=96 ** -0.5).then_inc(qbT_ready, 1)

            c_mid = KD * nw // 2
            split_w(0)
            split_w(1)
            cache()
            for c in range(2, c_mid):
                split_w(c)
            mean_square(0)
            high(0, 0)
            for c in range(c_mid, KD * nw):
                split_w(c)
            for i, slot in steps(act):
                if not is_last(i):
                    mean_square(i + 1)
                if not is_first(i):
                    feature_major(i - 1)
                if not is_last(i):
                    high(i + 1, 1 - slot)
                act.wait_ge(stored, FROM + i * 16 * nstore)
                act.wait_ge(tq_ready, FROM + ntq * i)
                act.wait_ge(kept, FROM + i)
                for g in range(ng):
                    act.wait_ge(mm_ready, FROM + ng * i + g + 1)
                    s.activation(proj[:, go[g]:go[g] + gw[g]], mm[g][:, 0:gw[g]], ACT.Copy).then_inc(proj_act, 1)
                    if even and g == 0 and not is_first(i):
                        up_query(i - 1)
                if even and not is_first(i):
                    up_query_T(i - 1)
                act.wait_ge(proj_act, FROM + ng * i + ng)
                vt = span(i)[3]
                if even:
                    act.wait_ge(dve_step, FROM + i)
                    s.activation(norm.junk[:, 0:QR], proj[:, 1064:1320], ACT.Square, scale=QR ** -0.5,
                                 accum_out=nst[:, 0:1]).then_inc(sq_done, 1)
                    s.activation(norm.junk[:, QR:QR + KVR], proj[:, 1320:1448], ACT.Square, scale=KVR ** -0.5,
                                 accum_out=nst[:, 1:2]).then_inc(sq_done, 1)
                    act.wait_ge(sq_done, FROM + 2 * i + 2)
                    s.activation(nst[:, 2:4], nst[:, 0:2], ACT.Sqrt, bias=norm.eps[:]).then_inc(rt_done, 1)
                    s.activation(one(dst["wi"], i), proj[:, 1056:1064], ACT.Copy, scale=8 ** -0.5)
                if fox:
                    s.activation(one(dst["fc"], vt), proj[:, 1536:1544], ACT.Copy)
                vs = slice(640, 768) if even else slice(1024, 1536)
                s.activation(one(dst["v"], vt), proj[:, vs], ACT.Copy).then_inc(kept, 1)
            feature_major(NT)
            if even:
                up_query(NT)
                up_query_T(NT)

        def rope(v, dve, i, src, tab, nh, hd, off, half, cnt):
            x1, x2 = src[:, :, off:off + half], src[:, :, off + half:off + 2 * half]
            tr = one(trig, i)
            cos = tr[:, tab:tab + half].unsqueeze(1).to_broadcast([P, nh, half])
            sin = tr[:, tab + half:tab + 2 * half].unsqueeze(1).to_broadcast([P, nh, half])
            r = [rot[:, j, 0:nh * half].rearrange("p (h d) -> p h d", h=nh) for j in range(4)]
            v.tensor_tensor(r[0], x1, cos, ALU.mult).then_inc(dve_rope, 1)
            v.tensor_tensor(r[1], x2, sin, ALU.mult).then_inc(dve_rope, 1)
            v.tensor_tensor(r[2], x1, sin, ALU.mult).then_inc(dve_rope, 1)
            v.tensor_tensor(r[3], x2, cos, ALU.mult).then_inc(dve_rope, 1)
            dve.wait_ge(dve_rope, FROM + cnt + 4)
            v.tensor_tensor(x1, r[0], r[1], ALU.subtract).then_inc(dve_rope, 1)
            v.tensor_tensor(x2, r[2], r[3], ALU.add).then_inc(dve_rope, 1)
            dve.wait_ge(dve_rope, FROM + cnt + 6)
            return cnt + 6

        @block.vector
        def _(dve):
            v = nc.vector

            def split_w(c):
                k, w0 = c // nw, (c % nw) * ww
                dve.wait_ge(w_hi, FROM + c + 1)
                v.tensor_tensor(wlo[:, k, w0:w0 + ww], landing[c % nl], whi[:, k, w0:w0 + ww].bitcast(F32),
                                ALU.subtract).then_inc(w_lo, 1)

            def low(i, slot):
                if not is_first(i):
                    dve.wait_ge(mm_ready, FROM + ng * (i - 1))
                h, l = hhi[slot], hlo[slot]
                norm.dve_lo(dve, i, [h[:, 0:4, :], h[:, 4:8, :]], [l[:, 0:4, :], l[:, 4:8, :]])

            def rotate(i):
                dve.wait_ge(proj_act, FROM + ng * i + ng)
                c = 24 * i
                c = rope(v, dve, i, proj[:, 0:640].rearrange("p (h d) -> p h d", d=64), RA, 10, 64, 0, 8, c)
                c = rope(v, dve, i, proj[:, 768:1056].rearrange("p (h d) -> p h d", d=32), RI, 9, 32, 0, 4, c)
                rope(v, dve, i, proj[:, 1448:1480].rearrange("p (h d) -> p h d", d=32), RB, 1, 32, 0, 16, c)

            def latents(i):
                dve.wait_ge(rt_done, FROM + i + 1)
                v.reciprocal(nst[:, 4:6], nst[:, 2:4]).then_inc(rr_done, 1)
                dve.wait_ge(rr_done, FROM + i + 1)
                v.scalar_tensor_tensor(cqn, proj[:, 1064:1320], nst[:, 4:5], gq[:], ALU.mult, ALU.mult)
                v.scalar_tensor_tensor(lat, proj[:, 1320:1448], nst[:, 5:6], gkv[:], ALU.mult, ALU.mult).then_inc(dve_step, 1)
                v.tensor_copy(stage[:, 0:P].rearrange("p (c d) -> p c d", c=4),
                              proj[:, 1024:1056].unsqueeze(1).to_broadcast([P, 4, 32]))
                v.tensor_copy(aq.rearrange("p (c g d) -> p c g d", c=4, g=2),
                              proj[:, 0:512].rearrange("p (g c d) -> p c g d", g=2, d=HD))
                v.tensor_copy(stage[:, P + 64:P + 96], proj[:, 1448:1480]).then_inc(post, 1)

            def feature_major(i):
                n, q, _, _ = span(i)
                dve.wait_ge(tq_ready, FROM + 3 * i + 3)
                v.tensor_copy(cqT, tq[2][:, 2 * P:4 * P].rearrange("p (c t) -> p c t", c=2)).then_inc(cqT_ready, 1)
                v.tensor_scalar(dst["qiT"][:, :, q], tq[2][:, 0:2 * P].rearrange("p (c t) -> p c t", c=2)[:, :, 0:n],
                                32 ** -0.5, None, ALU.mult).then_inc(cqT_ready, 1)

            def rotate_up(i):
                dve.wait_ge(qb_cp, FROM + 2 * i + 2)
                rope(v, dve, i, qb, RB, 8, 96, 64, 16, 24 * i + 18)

            c_mid = KD * nw // 2
            if even:
                v.memset(cr[:, :, 0:64], 0.0).then_inc(zeroed, 1)
            if fox:
                v.memset(dst["fc"][:, NT:KT - 1, :], 0.0)
            for c in range(c_mid):
                split_w(c)
            dve.wait_ge(norm.g_in, FROM + 16)
            dve.wait_ge(cache_tp, FROM + 2)
            norm.dve_norm(dve, 0)
            norm.dve_scale_g(dve, 0)
            low(0, 0)
            for c in range(c_mid, KD * nw):
                split_w(c)
            if even:
                dve.wait_ge(w_lo, FROM + KD)
                v.memset(stage, 0.0).then_inc(zeroed, 1)
                dve.wait_ge(zeroed, FROM + 2)
                dve.wait_ge(gq_in, FROM + 48)
                dve.wait_ge(trig_in, FROM + 16)
            for i, slot in steps(dve):
                if even and not is_first(i):
                    rotate(i - 1)
                if not is_last(i):
                    norm.dve_norm(dve, i + 1)
                if even and not is_first(i):
                    latents(i - 1)
                    feature_major(i - 1)
                if not is_last(i):
                    norm.dve_scale_g(dve, i + 1)
                    low(i + 1, 1 - slot)
                if even and not is_first(i):
                    rotate_up(i - 1)
            if even:
                rotate(NT)
                latents(NT)
                feature_major(NT)
                rotate_up(NT)

        @block.tensor
        def _(pe):
            t = nc.tensor

            def multiply(i, slot, g):
                if not is_first(i):
                    pe.wait_ge(proj_act, FROM + ng * (i - 1) + g + 1)
                cols = slice(go[g], go[g] + gw[g])
                for k in range(KD):
                    if is_first(i) and g == 0:
                        pe.wait_ge(w_lo, FROM + nw * (k + 1))
                    last = three_passes(nc, mm[g][:, 0:gw[g]], (hhi[slot][:, k, :], hlo[slot][:, k, :]),
                                        (whi[:, k, cols], wlo[:, k, cols]), k == 0, k == KD - 1)
                last.then_inc(mm_ready, 1)

            def transposes(i):
                if not even:
                    pe.wait_ge(proj_act, FROM + ng * i + ng)
                    pe.wait_ge(tq_act, FROM + 2 * i)
                    for g in range(2):
                        for c in range(4):
                            last = t.transpose(tq[g][:, c * P:(c + 1) * P],
                                               proj[:, 512 * g + c * P:512 * g + (c + 1) * P], ident[:])
                        last.then_inc(tq_ready, 1)
                    return
                pe.wait_ge(post, FROM + i + 1)
                pe.wait_ge(qbT_ready, FROM + 2 * i)
                for c in range(4):
                    last = t.transpose(tq[0][:, c * P:(c + 1) * P], aq[:, c * P:(c + 1) * P], ident[:])
                last.then_inc(tq_ready, 1)
                t.transpose(tq[1][:, 0:P], proj[:, 512:640], ident[:])
                t.transpose(tq[1][:, P:2 * P], stage[:, 0:P], ident[:])
                t.transpose(tq[1][:, 2 * P:3 * P], lat, ident[:])
                t.transpose(tq[1][0:96, 3 * P:4 * P], stage[:, P:P + 96], ident[:]).then_inc(tq_ready, 1)
                pe.wait_ge(cqT_ready, FROM + 2 * i)
                for c in range(2):
                    t.transpose(tq[2][:, c * P:(c + 1) * P], proj[:, 768 + c * P:768 + (c + 1) * P], ident[:])
                for c in range(2):
                    last = t.transpose(tq[2][:, (2 + c) * P:(3 + c) * P], cqn[:, c * P:(c + 1) * P], ident[:])
                last.then_inc(tq_ready, 1)

            def up_query(i):
                pe.wait_ge(cqT_ready, FROM + 2 * i + 1)
                for g in range(2):
                    pe.wait_ge(tq_act, FROM + 2 * i + g + 1)
                    for c in range(2):
                        last = t.matmul(tq[g][:, 0:384], cqT[:, c, :], wuq[:, c, 384 * g:384 * (g + 1)],
                                        start=(c == 0), stop=(c == 1))
                    last.then_inc(qb_mm, 1)

            def up_query_T(i):
                pe.wait_ge(dve_rope, FROM + 24 * i + 24)
                for g in range(2):
                    for h in range(4):
                        last = t.transpose(tq[g][0:96, h * P:(h + 1) * P], qb[:, 4 * g + h, :], ident[:])
                    last.then_inc(qb_tp, 1)

            pe.wait_ge(cache_in, FROM + 16 * (16 if even else 4))
            if even:
                pe.wait_ge(zeroed, FROM + 1)
            for b in range(2):
                if even:
                    t.transpose(mm[b][:, 0:P], ck[:, b], ident[:])
                    t.transpose(mm[b][:, P:2 * P], ci[:, b], ident[:])
                    t.transpose(mm[b][:, 2 * P:3 * P], cl[:, b, :], ident[:])
                    last = t.transpose(mm[b][0:96, 3 * P:4 * P], cr[:, b, :], ident[:])
                else:
                    for c in range(4):
                        last = t.transpose(mm[b][:, c * P:(c + 1) * P], rows4[:, b, c, :], ident[:])
                last.then_inc(cache_tp, 1)
            norm.pe_transposes(pe, 0)
            pe.wait_ge(cache_cp, FROM + 2)
            if even:
                pe.wait_ge(gq_in, FROM + 48)
            for i, slot in steps(pe):
                pe.wait_ge(norm.lo_ready, FROM + 2 * i + 2)
                multiply(i, slot, 0)
                if not is_first(i):
                    transposes(i - 1)
                if not is_last(i):
                    norm.pe_transposes(pe, i + 1)
                multiply(i, slot, 1)
                if even and not is_first(i):
                    up_query(i - 1)
                for g in range(2, ng):
                    multiply(i, slot, g)
                if even and not is_first(i):
                    up_query_T(i - 1)
            transposes(NT)
            if even:
                up_query(NT)
                up_query_T(NT)


TILES = NT + 1
UNITS = 2 * TILES
UNIT = [(t, h) for t in range(TILES) for h in range(2)]


def queries(t):
    return DEC if t == NT else P


def blocks(t, g):
    w = key_tile(t)[0]
    return [(b, min(P, w - b * P)) for b in range(4 * g, min(4 * g + 4, (w + P - 1) // P))]


WIDE = [u for u, (t, h) in enumerate(UNIT) if blocks(t, 1)]
O_USES = [[t for t in range(TILES) if t % 2 == s] for s in range(2)]
TOPK_TILES = [(t, NT + 1 - t) for t in range(2, NT // 2 + 1)]
EARLY = [16, 8, 4]
TOPK_TURN = [(TOPK_P // 8 - e) // 4 for e in EARLY]
TURN = sorted((j / n, c) for c, n in enumerate(TOPK_TURN) for j in range(n))


class TopRounds:

    def __init__(self, ph, nc, work):
        self.nc, self.work = nc, work
        self.best = ph.sb("best", [P, 2, 8])
        self.found, self.gone, self.passed = ph.sem("top_found"), ph.sem("top_gone"), ph.sem("top_passed")

    def round(self, dve, m, pair):
        v = self.nc.vector
        for i, t in enumerate(pair):
            dve.wait_ge(self.gone, FROM + 2 * m + i - 1)
            dve.sem_inc(self.passed, 1)
            v.max(self.best[:, i, :], self.work[t][:]).then_inc(self.found, 1)
        for i, t in enumerate(pair):
            dve.wait_ge(self.found, FROM + 2 * m + i + 1)
            dve.sem_inc(self.passed, 1)
            v.match_replace(self.work[t][:], self.best[:, i, :], self.work[t][:], GONE).then_inc(self.gone, 1)


def group_count(p, u, g):
    return p * UNITS + u if g == 0 else p * len(WIDE) + WIDE.index(u)


def o_count(p, t):
    return p * len(O_USES[t % 2]) + O_USES[t % 2].index(t)


def attention(nc, dram, consts, kind, src):
    ident, ident_bf = consts["ident"], consts["ident_bf"]
    stick, mla, fox, dsa = kind == "d", kind == "b", kind == "c", kind == "a"
    mask = None if dsa else consts[{"b": "mask_chunk", "c": "mask_causal", "d": "mask_strict"}[kind]]
    with Phase(nc, f"att_{kind}") as ph:
        sb, sem = ph.sb, ph.sem
        q = sb("q", [96, 2, TOK]) if mla else sb("q", [P, 2, TILES * P])
        if mla:
            k, v = [src["krT"], sb("k1", [96, KEYS])], sb("v", [P, KT, P])
            wkv = sb("wkv", [P, 2 * P])
            tops = TopRounds(ph, nc, src["work"])
        if fox:
            fk = sb("fk", [P, 2, KEYS], F32R)
        prob = [sb(f"prob{s}", [P, SEQ]) for s in range(2)]
        if stick:
            rest = [sb(f"rest{s}", [P, SEQ]) for s in range(2)]
            left = sb("left", [P, SEQ + 1])
        pt = [sb(f"pt{s}", [P, 8, P]) for s in range(2)]
        ot = [sb(f"ot{s}", [P, P]) for s in range(2)]
        nm = sb("nm", [P, 8])
        rs = sb("rs", [P, 8])
        rr = sb("rr", [P, 8])
        S = [ph.ps(f"s{s}", (P, SEQ)) for s in range(2)]
        TP = [ph.ps(f"tp{g}") for g in range(2)]
        O = [ph.ps(f"o{g}") for g in range(2)]
        q_in, staged, passed, cleared = sem("q_in"), sem("staged"), sem("passed"), sem("cleared")
        s_ready, prob_ready, pv_done = sem("s_ready"), sem("prob_ready"), sem("pv_done")
        max_done, rcp_done = sem("max_done"), sem("rcp_done")
        tp_ready = [sem(f"tp_ready{g}") for g in range(2)]
        pt_ready = [sem(f"pt_ready{g}") for g in range(2)]
        o_out = [sem(f"o_out{s}") for s in range(2)]
        ot_stored = [sem(f"ot_stored{s}") for s in range(2)]
        if mla:
            w_in, kv_ready = sem("w_in"), sem("kv_ready")
            kv_out = [sem(f"kv_out{s}") for s in range(2)]
        if stick:
            rest_done, taken_done, scan_done = sem("rest_done"), sem("taken_done"), sem("scan_done")
        block = ph.block()

        def keys(p, h, c0, c1):
            if mla:
                return k[h][:, c0:c1]
            if dsa:
                return src["kaT"][:, c0:c1]
            return src["kT"][:, ds(p, 1), c0:c1].rearrange("d a n -> d (a n)")

        def values(p, h, b):
            if mla or dsa:
                return (v if mla else src["v"])[:, b, h * HD:(h + 1) * HD]
            return src["v"][:, b, ds(p * P + h * HD, HD)]

        @block.sync
        def _(eng):
            def load_w(p):
                eng.dma_start(wkv[:], dram["w_b_ukv"][0, :, ds(p * 2 * P, 2 * P)] if not isinstance(p, int) else
                              dram["w_b_ukv"][0, :, p * 2 * P:(p + 1) * 2 * P]).then_inc(w_in, 16)

            def load_q(p):
                if mla:
                    eng.dma_start(q[:], rows(dram["qbT"], 2 * p, 2).rearrange("h d t -> d h t")).then_inc(q_in, 16)
                    return
                for h in range(2):
                    hp = slice(h * HD, (h + 1) * HD)
                    qT = (src["qaT"] if dsa else src["qT"])[hp]
                    eng.dma_start(q[hp, h, 0:TOK], one(qT, p)).then_inc(q_in, 16)

            def store(p, t):
                s, n = t % 2, queries(t)
                eng.wait_ge(o_out[s], FROM + o_count(p, t) + 1)
                r = slice(t * P, t * P + n)
                if dsa:
                    to = dram["att"][r, 0:8 * HD].rearrange("t (g c d) -> t g c d", g=2, d=HD)
                    to = to[:, :, p:p + 1, :] if isinstance(p, int) else to[:, :, ds(p, 1), :]
                    to = to.rearrange("t g a d -> t g (a d)")
                    eng.dma_start(to, ot[s][0:n, :].rearrange("t (g d) -> t g d", g=2)).then_inc(ot_stored[s], 16)
                else:
                    c0 = (0 if fox else 8 * HD) + p * P
                    to = dram["att"][r, c0:c0 + P] if isinstance(p, int) else dram["att"][r, ds(c0, P)]
                    eng.dma_start(to, ot[s][0:n, :]).then_inc(ot_stored[s], 16)

            if mla:
                load_w(0)
            load_q(0)
            with eng.Fori(0, 3) as p:
                for t in range(TILES):
                    if t == 2 and mla:
                        eng.wait_ge(kv_ready, FROM + 9 * p + 9)
                        eng.sem_inc(passed, 1)
                        load_w(p + 1)
                    if t == NT - 1:
                        eng.wait_ge(s_ready, FROM + (p + 1) * UNITS)
                        eng.sem_inc(passed, 1)
                        load_q(p + 1)
                    store(p, t)
            for t in range(TILES):
                store(3, t)
            for s in range(2):
                eng.wait_ge(ot_stored[s], FROM + 16 * 4 * len(O_USES[s]))

        @block.gpsimd
        def _(pool):
            g = nc.gpsimd
            g.memset((v if mla else src["v"])[DEC:P, KT - 1, :], 0.0).then_inc(cleared, 1)
            if mla:
                pool.wait_ge(cleared, FROM + 1)
                g.tensor_copy(k[1][64:96, :], src["krT"][64:96, :]).then_inc(staged, 1)
                return
            pool.wait_ge(cleared, FROM + 1)
            g.memset(q[:, :, TOK:], 0.0).then_inc(cleared, 1)
            for h in range(2):
                pool.wait_ge(cleared, FROM + 2 + h)
                g.memset(q[(1 - h) * HD:(2 - h) * HD, h, 0:TOK], 0.0).then_inc(cleared, 1)

        @block.tensor
        def _(pe):
            tt = nc.tensor

            def scores(p, u):
                t, h = UNIT[u]
                s, w = u % 2, key_tile(t)[0]
                n = queries(t) if mla else P
                k0 = key_tile(t)[1]
                for c0 in range(0, w, 512):
                    cw = min(512, w - c0)
                    o = S[s][0:n, c0:c0 + cw]
                    parts = [(o, q[:, h, t * P:t * P + n], keys(p, h, k0 + c0, k0 + c0 + cw))]
                    if fox:
                        parts.append((o, src["fq"][:, t * P:t * P + n], fk[:, h, k0 + c0:k0 + c0 + cw]))
                    if dsa:
                        b0 = src["bias_at"][t] + c0
                        parts.append((o, ident_bf[:, 0:n], src["bias"][:, b0:b0 + cw]))
                    elif c0 + cw == w and not (mla and t == NT):
                        m = queries(t)
                        parts.append((S[s][0:n, w - m:w], ident_bf[:, 0:n], mask[:, 0:m]))
                    for j, (o, a, b) in enumerate(parts):
                        last = tt.matmul(o, a, b, start=(j == 0), stop=(j == len(parts) - 1))
                last.then_inc(s_ready, 1)

            def transposes(p, u):
                t, h = UNIT[u]
                n, s = queries(t), u % 2
                pe.wait_ge(prob_ready, FROM + p * UNITS + u + 1)
                for g in range(2):
                    if not blocks(t, g):
                        continue
                    pe.wait_ge(pt_ready[g], FROM + group_count(p, u, g))
                    if n < P:
                        pe.sem_inc(passed, 1)
                    for b, r in blocks(t, g):
                        last = tt.transpose(TP[g][0:r, (b % 4) * P:(b % 4) * P + n],
                                            prob[s][0:n, b * P:b * P + r], ident[0:n, 0:n])
                    last.then_inc(tp_ready[g], 1)

            def products(p, u):
                t, h = UNIT[u]
                n, s, w = queries(t), u % 2, key_tile(t)[0]
                if h == 0:
                    pe.wait_ge(o_out[t % 2], FROM + o_count(p, t))
                for g in range(2):
                    if not blocks(t, g):
                        continue
                    pe.wait_ge(pt_ready[g], FROM + group_count(p, u, g) + 1)
                    for b, r in blocks(t, g):
                        last = tt.matmul(O[t % 2][0:n, h * HD:(h + 1) * HD], pt[s][:, b, 0:n],
                                         values(p, h, b if t < NT else NT + b), start=(b == 0), stop=(b * P + r == w))
                last.then_inc(pv_done, 1)

            def expand(p):
                pe.wait_ge(w_in, FROM + 16 * p + 16)
                wv = wkv[:].rearrange("p (h x) -> p h x", h=2)[:, :, HD:P]
                for j in range(9):
                    o = S[j % 2][:, 512 * (j // 2 % 2):512 * (j // 2 % 2) + 512]
                    if j >= 4:
                        pe.wait_ge(kv_out[j % 2], FROM + (5, 4)[j % 2] * p + (j - 4) // 2 + 1)
                    if j < 6:
                        h, c = j // 3, j % 3
                        last = tt.matmul(o[0:HD, 0:448], wkv[:, h * P:h * P + HD],
                                         src["latT"][:, c * 448:(c + 1) * 448], start=True, stop=True)
                    else:
                        for b in range(4 * (j - 6), min(4 * (j - 5), KT)):
                            r = DEC if b == KT - 1 else P
                            last = tt.matmul(o[0:r, (b % 4) * P:(b % 4 + 1) * P],
                                             src["latT"][:, b * P:b * P + r], wv, start=True, stop=True)
                    last.then_inc(kv_ready, 1)
                pe.wait_ge(kv_out[0], FROM + 5 * p + 5)
                pe.wait_ge(kv_out[1], FROM + 4 * p + 4)

            if mla:
                pe.wait_ge(staged, FROM + 1)
            pe.wait_ge(cleared, FROM + (1 if mla else 4))
            with pe.Fori(0, 4) as p:
                if mla:
                    expand(p)
                if fox:
                    pe.wait_ge(staged, FROM + 2 * p + 2)
                n_in = 16 if mla else 32
                pe.wait_ge(q_in, FROM + n_in * p + n_in)
                pe.sem_inc(passed, 1)
                scores(p, 0)
                scores(p, 1)
                for u in range(UNITS):
                    transposes(p, u)
                    if u + 2 < UNITS:
                        scores(p, u + 2)
                    if u:
                        products(p, u - 1)
                products(p, UNITS - 1)

        def copy_group(eng, p, u, g, scalar):
            t, h = UNIT[u]
            bl = blocks(t, g)
            if not bl:
                return
            n, s = queries(t), u % 2
            eng.wait_ge(tp_ready[g], FROM + group_count(p, u, g) + 1)
            full = [b for b, r in bl if r == P]
            jobs = [(full[0], full[-1] + 1, P)] if full else []
            jobs += [(b, b + 1, r) for b, r in bl if r != P]
            for b0, b1, r in jobs:
                i = TP[g][:].rearrange("p (b t) -> p b t", b=4)[0:r, b0 - 4 * g:b1 - 4 * g, 0:n]
                o = pt[s][0:r, b0:b1, 0:n]
                last = nc.scalar.activation(o, i, ACT.Copy) if scalar else nc.vector.tensor_copy(o, i)
            last.then_inc(pt_ready[g], 1)

        def transposed(eng, p, u):
            g = 1 if blocks(UNIT[u][0], 1) else 0
            eng.wait_ge(tp_ready[g], FROM + group_count(p, u, g) + 1)

        def expanded(eng, p, j):
            o = S[j % 2][:, 512 * (j // 2 % 2):512 * (j // 2 % 2) + 512]
            copy = (lambda a, b: nc.scalar.activation(a, b, ACT.Copy)) if j % 2 == 0 else nc.vector.tensor_copy
            eng.wait_ge(kv_ready, FROM + 9 * p + j + 1)
            if j < 6:
                last = copy(k[j // 3][0:HD, (j % 3) * 448:(j % 3 + 1) * 448], o[0:HD, 0:448])
            else:
                b0 = 4 * (j - 6)
                b1 = min(b0 + 4, KT - 1)
                last = copy(v[:, b0:b1, :].rearrange("p b d -> p (b d)"), o[:, 0:(b1 - b0) * P])
                if j == 8:
                    last = copy(v[0:DEC, KT - 1, :], o[0:DEC, (b1 - b0) * P:(b1 - b0 + 1) * P])
            last.then_inc(kv_out[j % 2], 1)

        @block.scalar
        def _(act):
            s_ = nc.scalar

            def exponential(p, u):
                n, s, w, m = queries(UNIT[u][0]), u % 2, key_tile(UNIT[u][0])[0], p * UNITS + u
                act.wait_ge(s_ready if stick else max_done, FROM + m + 1)
                if u >= 2:
                    transposed(act, p, u - 2)
                if stick:
                    s_.activation(rest[s][0:n, 0:w], S[s][0:n, 0:w], ACT.Sigmoid, scale=-1.0).then_inc(rest_done, 1)
                    s_.activation(prob[s][0:n, 0:w], S[s][0:n, 0:w], ACT.Sigmoid).then_inc(taken_done, 1)
                else:
                    c = slice(u % 8, u % 8 + 1)
                    s_.activation(prob[s][0:n, 0:w], S[s][0:n, 0:w], ACT.Exp, bias=nm[0:n, c],
                                  accum_out=rs[0:n, c]).then_inc(prob_ready, 1)

            def output(p, u):
                t, h = UNIT[u]
                if h == 0:
                    return
                n, s = queries(t), t % 2
                act.wait_ge(pv_done, FROM + p * UNITS + u + 1)
                act.wait_ge(ot_stored[s], FROM + 16 * o_count(p, t))
                if stick:
                    last = s_.activation(ot[s][0:n, :], O[s][0:n, 0:P], ACT.Copy)
                else:
                    act.wait_ge(rcp_done, FROM + p * UNITS + u + 1)
                    for j in range(2):
                        hd, c = slice(j * HD, (j + 1) * HD), (u - 1 + j) % 8
                        last = s_.activation(ot[s][0:n, hd], O[s][0:n, hd], ACT.Copy, scale=rr[0:n, c:c + 1])
                last.then_inc(o_out[s], 1)

            with act.Fori(0, 4) as p:
                if mla:
                    for j in range(0, 9, 2):
                        expanded(act, p, j)
                exponential(p, 0)
                for u in range(UNITS):
                    if u + 1 < UNITS:
                        exponential(p, u + 1)
                    copy_group(act, p, u, 0, True)
                    if mla:
                        copy_group(act, p, u, 1, True)
                    if u >= 2:
                        output(p, u - 2)
                output(p, UNITS - 2)
                output(p, UNITS - 1)

        @block.vector
        def _(dve):
            v_ = nc.vector

            def top(p, u):
                n, s, w, m = queries(UNIT[u][0]), u % 2, key_tile(UNIT[u][0])[0], p * UNITS + u
                dve.wait_ge(s_ready, FROM + m + 1)
                v_.tensor_reduce(nm[0:n, u % 8:u % 8 + 1], S[s][0:n, 0:w], AX_X, ALU.max, negate=True).then_inc(max_done, 1)

            def over_sum(p, u):
                n, c, m = queries(UNIT[u][0]), slice(u % 8, u % 8 + 1), p * UNITS + u
                dve.wait_ge(prob_ready, FROM + m + 1)
                v_.reciprocal(rr[0:n, c], rs[0:n, c]).then_inc(rcp_done, 1)

            def broken(p, u):
                n, s, w, m = queries(UNIT[u][0]), u % 2, key_tile(UNIT[u][0])[0], p * UNITS + u
                dve.wait_ge(rest_done, FROM + m + 1)
                dve.wait_ge(prob_ready, FROM + m)
                r = rest[s][0:n, 0:w][:, ::-1]
                v_.tensor_tensor_scan(left[0:n, SEQ - w:SEQ][:, ::-1], r, r, 1.0, ALU.mult, ALU.bypass).then_inc(scan_done, 1)
                dve.wait_ge(scan_done, FROM + m + 1)
                dve.wait_ge(taken_done, FROM + m + 1)
                v_.tensor_tensor(prob[s][0:n, 0:w], prob[s][0:n, 0:w], left[0:n, SEQ - w + 1:SEQ + 1],
                                 ALU.mult).then_inc(prob_ready, 1)

            if stick:
                v_.memset(left[:, SEQ:SEQ + 1], 1.0).then_inc(staged, 1)
                dve.wait_ge(staged, FROM + 1)
            with dve.Fori(0, 4) as p:
                if fox:
                    dve.wait_ge(s_ready, FROM + p * UNITS)
                    for h in range(2):
                        v_.tensor_scalar(fk[:, h, :], src["fk_all"][:], src["onehot"][:, ds(2 * p + h, 1)], None,
                                         ALU.mult).then_inc(staged, 1)
                if mla:
                    for j in range(1, 9, 2):
                        expanded(dve, p, j)
                if stick:
                    broken(p, 0)
                else:
                    top(p, 0)
                    top(p, 1)
                    over_sum(p, 0)
                for u in range(UNITS):
                    if stick and u + 1 < UNITS:
                        broken(p, u + 1)
                    if not mla:
                        copy_group(dve, p, u, 1, False)
                    if not stick:
                        if u + 2 < UNITS:
                            top(p, u + 2)
                        if u + 1 < UNITS:
                            over_sum(p, u + 1)
                    if mla:
                        for j in range(len(TURN) * u // UNITS, len(TURN) * (u + 1) // UNITS):
                            tops.round(dve, len(TURN) * p + j, TOPK_TILES[TURN[j][1]])
            if mla:
                dve.wait_ge(tops.gone, FROM + 4 * 2 * len(TURN))
                for t, w in src["work"].items():
                    b0 = src["bias_at"][t]
                    v_.tensor_scalar(src["bias"][:, b0:b0 + w.shape[1]], w[:], -3.2e38, NEG, ALU.is_gt, ALU.mult)


def index_scores(nc, dram, consts, src):
    with Phase(nc, "index") as ph:
        sb, sem = ph.sb, ph.sem
        work = [src["work"][t] if t in src["work"] else sb(f"work{t}", [P, key_tile(t)[0]]) for t in range(TILES)]
        relu = [sb(f"relu{s}", [P, SEQ]) for s in range(2)]
        best = sb("sample_best", [P, 8])
        qz = [sb(f"qz{s}", [P, 2, 4, P]) for s in range(2)]
        zeroed, q_ready = sem("zeroed"), sem("q_ready")
        tops = TopRounds(ph, nc, src["work"])
        order = [t for pair in TOPK_TILES for t in pair[::-1]] + [1, 0, NT]
        S = [ph.ps(f"s{s}", (P, SEQ)) for s in range(2)]
        s_ready, relu_done, acc_done, step, passed = sem("s_ready"), sem("relu_done"), sem("acc_done"), sem("step"), sem("passed")
        block = ph.block()
        H = 8
        qiT, kiT, wi, bias, at = src["qiT"], src["kiT"], src["wi"], src["bias"], src["bias_at"]

        @block.tensor
        def _(pe):
            for i, t in enumerate(order):
                w, k0 = key_tile(t)
                n = queries(t)
                for h in range(H):
                    u = i * H + h
                    if u >= 2:
                        pe.wait_ge(relu_done, FROM + u - 1)
                    if h == 0:
                        pe.wait_ge(q_ready, FROM + i + 1)
                    for c0 in range(0, w, 512):
                        cw = min(512, w - c0)
                        last = nc.tensor.matmul(S[u % 2][0:n, c0:c0 + cw], qz[i % 2][:, h // 4, h % 4, 0:n],
                                                kiT[:, k0 + c0:k0 + c0 + cw], start=True, stop=True)
                    last.then_inc(s_ready, 1)

        @block.gpsimd
        def _(pool):
            for s in range(2):
                if s:
                    pool.wait_ge(zeroed, FROM + 1)
                nc.gpsimd.memset(qz[s][:], 0.0).then_inc(zeroed, 1)

        @block.scalar
        def _(act):
            def spread(i):
                t = order[i]
                n = queries(t)
                if i >= 2:
                    act.wait_ge(s_ready, FROM + (i - 1) * H)
                for r in range(4):
                    hp = slice(32 * r, 32 * r + 32)
                    last = nc.scalar.activation(qz[i % 2][hp, :, r, 0:n], qiT[hp, :, t * P:t * P + n], ACT.Copy)
                last.then_inc(q_ready, 1)

            act.wait_ge(zeroed, FROM + 2)
            spread(0)
            for i, t in enumerate(order):
                w, n = key_tile(t)[0], queries(t)
                if i + 1 < TILES:
                    spread(i + 1)
                for h in range(H):
                    u = i * H + h
                    act.wait_ge(s_ready, FROM + u + 1)
                    if u >= 2:
                        act.wait_ge(acc_done, FROM + u - 1)
                    nc.scalar.activation(relu[u % 2][0:n, 0:w], S[u % 2][0:n, 0:w], ACT.Relu).then_inc(relu_done, 1)

        @block.vector
        def _(dve):
            v = nc.vector
            steps = 0
            v.memset(bias[DEC:P, at[NT]:at[NT] + key_tile(NT)[0]], 0.0)
            left, m = list(EARLY), 0
            for i, t in enumerate(order):
                w, n = key_tile(t)[0], queries(t)
                wk = work[t][0:n, :]
                for h in range(H):
                    u = i * H + h
                    dve.wait_ge(relu_done, FROM + u + 1)
                    r, f = relu[u % 2][0:n, 0:w], wi[0:n, t, h:h + 1]
                    if h == 0:
                        v.tensor_scalar(wk, r, f, None, ALU.mult).then_inc(acc_done, 1)
                    else:
                        dve.wait_ge(acc_done, FROM + u)
                        v.scalar_tensor_tensor(wk, r, f, wk, ALU.mult, ALU.add).then_inc(acc_done, 1)
                    c = max(range(min(i // 2, len(left))), key=lambda j: left[j], default=None)
                    if h % 2 and c is not None and left[c]:
                        tops.round(dve, m, TOPK_TILES[c])
                        left[c] -= 1
                        m += 1
                dve.wait_ge(acc_done, FROM + (i + 1) * H)
                if t < NT:
                    v.memset(work[t][0:P // 2, w - P // 2:w], -3.0e38).then_inc(step, 1)
                    steps += 1
                    dve.wait_ge(step, FROM + steps)
                if t < 2:
                    v.tensor_scalar(bias[0:n, at[t]:at[t] + w], wk, -2.9e38, NEG, ALU.is_lt, ALU.mult)
                if t == NT:
                    assert not any(left)
                    with dve.Fori(0, TOPK_S // 8) as j:
                        dve.wait_ge(step, FROM + steps + 2 * j)
                        dve.sem_inc(passed, 1)
                        v.max(best[0:n, :], wk).then_inc(step, 1)
                        dve.wait_ge(step, FROM + steps + 2 * j + 1)
                        dve.sem_inc(passed, 1)
                        v.match_replace(wk, best[0:n, :], wk, GONE).then_inc(step, 1)
                    steps += 2 * (TOPK_S // 8)
                    dve.wait_ge(step, FROM + steps)
                    v.tensor_scalar(bias[0:n, at[t]:at[t] + w], wk, -3.2e38, NEG, ALU.is_gt, ALU.mult)


GROUPS = 3 * 32 + 8


def group(g):
    return slice(32 * g, 32 * g + 8)


def forget(nc, dram, consts, fc, dst, out):
    with Phase(nc, "forget") as ph:
        sb, sem = ph.sb, ph.sem
        bf = sb("bf", [P, 8])
        u = sb("u", [P, KT, 8])
        e = sb("e", [P, KT, 8])
        lf = sb("lf", [P, KT, GROUPS])
        lfT = sb("lfT", [GROUPS, KEYS])
        cum = sb("cum", [GROUPS, KEYS])
        high = sb("high", [GROUPS, KEYS], F32R)
        tp = [ph.ps(f"tp{b}") for b in range(3)]
        b_in, c_in, dstep, astep, tp_ready, tp_out, stored = (sem("b_in"), sem("c_in"), sem("dstep"), sem("astep"),
                                                              sem("tp_ready"), sem("tp_out"), sem("stored"))
        ident = consts["ident"]
        block = ph.block()

        @block.sync
        def _(sp):
            sp.dma_start(bf[:], dram["b_forget"][0:1, :].to_broadcast([P, 8])).then_inc(b_in, 16)
            sp.wait_ge(dstep, FROM + 7)
            for b in range(2):
                for g in range(4):
                    sp.dma_start(lf[:, NT + b, group(g)], dram["cache_c_logf"][0, 0, b * P:(b + 1) * P]).then_inc(c_in, 16)
            sp.dma_start(out["p_c_logf"].rearrange("(t p) h -> p t h", p=P), lf[:, 0:NT, 0:8]).then_inc(stored, 16)
            sp.dma_start(out["s_c_logf"], lf[0:DEC, KT - 1, 0:8]).then_inc(stored, 16)
            sp.wait_ge(stored, FROM + 32)

        @block.vector
        def _(dve):
            v = nc.vector
            v.memset(lf[:], 0.0).then_inc(dstep, 1)
            v.memset(dst["fk_all"][:], 0.0).then_inc(dstep, 1)
            v.memset(dst["fq"][:].bitcast(F32), 0.0).then_inc(dstep, 1)
            dve.wait_ge(b_in, FROM + 16)
            v.tensor_tensor(u[:], fc[:], bf[:].unsqueeze(1).to_broadcast([P, KT, 8]), ALU.add).then_inc(dstep, 1)
            dve.wait_ge(dstep, FROM + 4)
            dve.wait_ge(astep, FROM + 3)
            v.scalar_tensor_tensor(u[:], u[:], 0.0, e[:], ALU.min, ALU.subtract).then_inc(dstep, 1)
            dve.wait_ge(dstep, FROM + 5)
            for g in range(4):
                last = v.tensor_copy(lf[:, 0:NT, group(g)], u[:, 0:NT])
            last.then_inc(dstep, 1)
            for g in range(4):
                last = v.tensor_copy(lf[0:DEC, KT - 1, group(g)], u[0:DEC, KT - 1])
            last.then_inc(dstep, 1)
            dve.wait_ge(tp_out, FROM + 3)
            for c0, c1 in ((0, SEQ), (SEQ, KEYS)):
                a = lfT[:, c0:c1]
                v.tensor_tensor_scan(cum[:, c0:c1], a, a, 0.0, ALU.add, ALU.bypass).then_inc(dstep, 1)
            dve.wait_ge(dstep, FROM + 9)
            v.tensor_copy(high[:], cum[:]).then_inc(dstep, 1)
            dve.wait_ge(dstep, FROM + 10)
            fk, fq = dst["fk_all"], dst["fq"]
            v.tensor_scalar(fk[group(0), :], high[group(0), :].bitcast(F32), -1.0, None, ALU.mult)
            v.tensor_tensor(fk[group(1), :], high[group(1), :].bitcast(F32), cum[group(1), :], ALU.subtract)
            for g in (0, 1):
                v.memset(fk[group(2 + g), :], 1.0)
                v.memset(fq[group(g), :].bitcast(F32), 1.0)
            for q, c in ((slice(0, SEQ), slice(0, SEQ)), (slice(SEQ, TOK), slice(OWN, KEYS))):
                v.tensor_copy(fq[group(2), q], high[group(2), c].bitcast(F32))
                last = v.tensor_tensor(fq[group(3), q], cum[group(3), c], high[group(3), c].bitcast(F32), ALU.subtract)
            last.then_inc(dstep, 1)
            v.tensor_copy(dst["onehot"][:, :], ident[:, 0:8]).then_inc(dstep, 1)
            dve.wait_ge(dstep, FROM + 12)
            for g in (1, 2, 3):
                v.tensor_copy(dst["onehot"][group(g), :], ident[group(g), group(g)])

        @block.scalar
        def _(act):
            s = nc.scalar
            s.preload_act_table_set("natural_log_exp_and_others")
            act.wait_ge(dstep, FROM + 4)
            s.activation(e[:], u[:], ACT.Abs).then_inc(astep, 1)
            act.wait_ge(astep, FROM + 1)
            s.activation(e[:], e[:], ACT.Exp, scale=-1.0).then_inc(astep, 1)
            act.wait_ge(astep, FROM + 2)
            s.activation(e[:], e[:], ACT.Ln, bias=1.0).then_inc(astep, 1)
            for b in range(3):
                act.wait_ge(tp_ready, FROM + b + 1)
                c0, c1 = b * 512, min(b * 512 + 512, KEYS)
                s.activation(lfT[:, c0:c1], tp[b][0:GROUPS, 0:c1 - c0], ACT.Copy).then_inc(tp_out, 1)

        @block.tensor
        def _(pe):
            pe.wait_ge(c_in, FROM + 128)
            for b in range(3):
                for i in range(4 * b, min(4 * b + 4, KT)):
                    r = DEC if i == KT - 1 else P
                    last = nc.tensor.transpose(tp[b][0:GROUPS, (i % 4) * P:(i % 4) * P + r], lf[0:r, i, :], ident[0:r, 0:r])
                last.then_inc(tp_ready, 1)


def output_projection(nc, dram, consts, layer, w_dram, x_src, xres, hT):
    with Phase(nc, f"out_{layer}") as ph:
        sb, sem = ph.sb, ph.sem
        whi = sb("whi", [P, KD, D], F32R)
        wlo = sb("wlo", [P, KD, D], F32R)
        wraw = sb("wraw", [P, 2, D])
        a = sb("a", [P, D])
        ahi = [sb(f"ahi{s}", [P, KD * P], F32R) for s in range(2)]
        alo = [sb(f"alo{s}", [P, KD * P], F32R) for s in range(2)]
        x = sb("x", [P, D])
        norm = Norm(ph, nc, consts, x[:], dram["g_ffn"][layer],
                    hn=wraw[:, 0, :], hf=wraw[:, 1, :].rearrange("p (k t) -> p k t", k=KD))
        mm = [ph.ps(f"mm{g}") for g in range(2)]
        at = ph.ps("at", (P, D))
        w_in = [sem("w_in0"), sem("w_in1")]
        w_hi, w_lo, a_in, x_in, a_tp = sem("w_hi"), sem("w_lo"), sem("a_in"), sem("x_in"), sem("a_tp")
        a_hi, a_lo, mm_ready, added, kept = sem("a_hi"), sem("a_lo"), sem("mm_ready"), sem("added"), sem("kept")
        block = ph.block()

        @block.sync
        def _(sp):
            def load_w(k):
                if k >= 2:
                    sp.wait_ge(w_lo, FROM + k - 1)
                sp.dma_start(wraw[:, k % 2, :], w_dram[k * P:(k + 1) * P, :]).then_inc(w_in[k % 2], 16)

            def load_a(i):
                n = span(i)[0]
                if not is_first(i):
                    sp.wait_ge(a_tp, FROM + i)
                sp.dma_start(a[0:n, :], rows(dram["att"], i * P, n)).then_inc(a_in, 16)

            def load_x(i):
                if not is_first(i):
                    sp.wait_ge(norm.hn_ready, FROM + i)
                    sp.wait_ge(kept, FROM + i)
                if is_last(i):
                    sp.dma_start(x[0:DEC, :], x_src[1]).then_inc(x_in, 16)
                else:
                    sp.dma_start(x[:], rows(x_src[0], i * P, P)).then_inc(x_in, 16)

            load_a(0)
            for k in range(KD):
                load_w(k)
                if k == 2:
                    load_x(0)
                    load_a(1)
            norm.load_g(sp)
            with sp.Fori(0, NT - 2) as i:
                load_a(i + 2)
                load_x(i + 1)
            load_a(NT)
            load_x(NT - 1)
            load_x(NT)

        @block.scalar
        def _(act):
            s = nc.scalar
            s.preload_act_table_set("sqrt_and_others")

            def split_w(k):
                act.wait_ge(w_in[k % 2], FROM + 16 * (k // 2 + 1))
                s.activation(whi[:, k, :], wraw[:, k % 2, :], ACT.Copy).then_inc(w_hi, 1)

            def high(i, slot):
                act.wait_ge(a_tp, FROM + i + 1)
                if not is_first(i):
                    act.wait_ge(mm_ready, FROM + 2 * (i - 1))
                s.activation(ahi[slot][:], at[:], ACT.Copy).then_inc(a_hi, 1)

            def keep(i):
                norm.act_square(act, i, added, 2 * i + 2)
                norm.act_root(act, i)
                s.activation(one(xres, i), x[:], ACT.Copy).then_inc(kept, 1)

            def normed(i):
                n, q, _, _ = span(i)
                norm.act_hi(act, i, [hT[0][:, 0:4, q], hT[0][:, 4:8, q]], n)

            for k in range(KD):
                split_w(k)
                if k == 2:
                    high(0, 0)
            for i, slot in steps(act):
                if not is_first(i):
                    keep(i - 1)
                if not is_last(i):
                    high(i + 1, 1 - slot)
                if not is_first(i):
                    normed(i - 1)
            keep(NT)
            normed(NT)

        @block.vector
        def _(dve):
            v = nc.vector

            def split_w(k):
                dve.wait_ge(w_hi, FROM + k + 1)
                v.tensor_tensor(wlo[:, k, :], wraw[:, k % 2, :], whi[:, k, :].bitcast(F32), ALU.subtract).then_inc(w_lo, 1)

            def low(i, slot):
                dve.wait_ge(a_hi, FROM + i + 1)
                v.tensor_tensor(alo[slot][:], at[:], ahi[slot][:].bitcast(F32), ALU.subtract).then_inc(a_lo, 1)

            def add(i):
                dve.wait_ge(x_in, FROM + 16 * i + 16)
                for g in range(2):
                    dve.wait_ge(mm_ready, FROM + 2 * i + g + 1)
                    c = slice(g * 512, (g + 1) * 512)
                    v.tensor_tensor(x[:, c], mm[g][:], x[:, c], ALU.add).then_inc(added, 1)

            def normed(i):
                n, q, _, _ = span(i)
                norm.dve_scale_g(dve, i)
                norm.dve_lo(dve, i, [hT[0][:, 0:4, q], hT[0][:, 4:8, q]], [hT[1][:, 0:4, q], hT[1][:, 4:8, q]], n)

            for k in range(KD):
                split_w(k)
                if k == 2:
                    low(0, 0)
            dve.wait_ge(norm.g_in, FROM + 16)
            dve.wait_ge(w_lo, FROM + KD)
            for i, slot in steps(dve):
                if not is_first(i):
                    norm.dve_norm(dve, i - 1)
                if not is_last(i):
                    low(i + 1, 1 - slot)
                if not is_first(i):
                    normed(i - 1)
                add(i)
            norm.dve_norm(dve, NT)
            normed(NT)

        @block.tensor
        def _(pe):
            def attention_T(i):
                pe.wait_ge(a_in, FROM + 16 * i + 16)
                if not is_first(i):
                    pe.wait_ge(a_lo, FROM + i)
                for k in range(KD):
                    c = slice(k * P, (k + 1) * P)
                    last = nc.tensor.transpose(at[:, c], a[:, c], consts["ident"][:])
                last.then_inc(a_tp, 1)

            def multiply(i, slot, g):
                if not is_first(i):
                    pe.wait_ge(added, FROM + 2 * (i - 1) + g + 1)
                c = slice(g * 512, (g + 1) * 512)
                for k in range(KD):
                    if is_first(i) and g == 0:
                        pe.wait_ge(w_lo, FROM + k + 1)
                    kk = slice(k * P, (k + 1) * P)
                    last = three_passes(nc, mm[g][:], (ahi[slot][:, kk], alo[slot][:, kk]), (whi[:, k, c], wlo[:, k, c]),
                                        k == 0, k == KD - 1)
                last.then_inc(mm_ready, 1)

            attention_T(0)
            for i, slot in steps(pe):
                pe.wait_ge(a_lo, FROM + i + 1)
                multiply(i, slot, 0)
                if not is_last(i):
                    attention_T(i + 1)
                if not is_first(i):
                    norm.pe_transposes(pe, i - 1)
                multiply(i, slot, 1)
            norm.pe_transposes(pe, NT)


def one_col(m):
    return slice(m, m + 1) if isinstance(m, int) else ds(m, 1)


TB = [(0, 384), (384, 384), (768, 320)]
CW = 2 + SEQ + 2 + DEC
NG = NF // 2


def conv_ffn(nc, dram, consts, layer, xres, hT, out, x_next):
    wup, wdn = dram["w_up"][layer], dram["w_down"][layer]
    last_layer = x_next is None
    with Phase(nc, f"ffn_{layer}") as ph:
        sb, sem = ph.sb, ph.sem
        uhi = [sb(f"uhi{c}", [P, 2, KD, P], F32R) for c in range(2)]
        ulo = [sb(f"ulo{c}", [P, 2, KD, P], F32R) for c in range(2)]
        dhi = sb("dhi", [P, 2, D], F32R)
        dlo = sb("dlo", [P, 2, D], F32R)
        uraw = sb("uraw", [P, 2, KD, P])
        draw = sb("draw", [P, 2, D])
        G = sb("G", [P, CW])
        cv = sb("cv", [P, 2, 384])
        ahi = sb("ahi", [P, 2, NT * P + P], F32R)
        alo = sb("alo", [P, 2, NT * P + P], F32R)
        rowbuf = cv[:].rearrange("p a n -> p (a n)")[:, 0:2 * P]
        ctap = sb("ctap", [P, 2, 4])
        tap = sb("tap", [P, 4 * NF])
        st = sb("st", [P, 2 * NF])
        tail = sb("tail", [P, 4, NF])
        up = [ph.ps(f"up{j}") for j in range(4)]
        dn = [ph.ps(f"dn{j}") for j in range(4)]
        uraw_in, u_hi, u_lo, draw_in, d_hi, d_lo = (sem("uraw_in"), sem("u_hi"), sem("u_lo"), sem("draw_in"),
                                                   sem("d_hi"), sem("d_lo"))
        tap_in, tap_tp, tap_ready, tail_ready, tail_tp, tail_out, state_out = (
            sem("tap_in"), sem("tap_tp"), sem("tap_ready"), sem("tail_ready"), sem("tail_tp"), sem("tail_out"), sem("state_out"))
        up_ready, g_out = sem("up_ready"), sem("g_out")
        c0_done, c1_done, c2_done, silu_done, a_done, ahi_done, alo_done = (
            sem("c0"), sem("c1"), sem("c2"), sem("silu"), sem("a_done"), sem("ahi_done"), sem("alo_done"))
        ctap_set = sem("ctap_set")
        dn_ready, dn_added, started, seam = sem("dn_ready"), sem("dn_added"), sem("started"), sem("seam")
        x_out = [sem("x_out0"), sem("x_out1")]
        if last_layer:
            g_final, junk = [uraw[:, s].rearrange("p k f -> p (k f)") for s in range(2)]
            y = draw
            stat = sb("stat", [P, 3, TILES])
            g_in, ssq, rt, rinv, y_ready = sem("g_in"), sem("ssq"), sem("rt"), sem("rinv"), sem("y_ready")
        whole = 18 * (NG - 1)
        block = ph.block()
        wupv = wup.rearrange("(k p) (s f) -> p s k f", p=P, s=2)
        SEAM = 2 + SEQ

        def gcols(b):
            t0, n = TB[b]
            if t0 + n <= SEQ:
                return [(2 + t0, t0, n)]
            return [(2 + t0, t0, SEQ - t0), (SEAM + 2, SEQ, DEC)]

        @block.sync
        def _(sp):
            def load_up(m):
                for s in range(2):
                    f = slice(m * P, (m + 1) * P) if isinstance(m, int) else ds(m * P, P)
                    sp.dma_start(uraw[:, s], wupv[:, s, :, f]).then_inc(uraw_in, 16)

            def load_down(i):
                sp.dma_start(draw[:], rows(wdn, i * 2 * P, 2 * P).rearrange("(c p) n -> p c n", p=P)).then_inc(draw_in, 16)

            load_up(0)
            for j in range(3):
                sp.dma_start(rowbuf[j * NF:(j + 1) * NF, 0:P],
                             dram["w_conv"][layer, j].rearrange("(c p) -> c p", p=P)).then_inc(tap_in, 16)
            sp.dma_start(rowbuf[3 * NF:4 * NF, 0:P], dram["b_conv"][layer].rearrange("(c p) -> c p", p=P)).then_inc(tap_in, 16)
            for j in range(2):
                sp.dma_start(rowbuf[j * NF:(j + 1) * NF, P:2 * P],
                             dram["state_ffn_conv"][layer, 0, j].rearrange("(c p) -> c p", p=P)).then_inc(tap_in, 16)
            load_down(0)
            sp.wait_ge(u_lo, FROM + 1)
            load_up(1)
            with sp.Fori(1, NG) as i:
                for c in range(2):
                    sp.wait_ge(u_lo, FROM + 2 * i + c)
                    load_up(2 * i + c)
                    if c == 0:
                        sp.wait_ge(d_lo, FROM + i)
                        load_down(i)
            if last_layer:
                sp.wait_ge(u_lo, FROM + NF)
                sp.dma_start(g_final, dram["g_final"].unsqueeze(0).to_broadcast([P, D])).then_inc(g_in, 16)
            for t in range(TILES):
                n = queries(t)
                if last_layer:
                    sp.wait_ge(y_ready, FROM + t + 1)
                    to = out["y_sample"] if t == NT else out["y_prompt"][t * P:(t + 1) * P]
                    sp.dma_start(to, y[0:n, t % 2, :]).then_inc(x_out[t % 2], 16)
                else:
                    sp.wait_ge(dn_added, FROM + whole + 2 * t + 2)
                    to = x_next[1] if t == NT else x_next[0][t * P:(t + 1) * P]
                    sp.dma_start(to, xres[0:n, t, :]).then_inc(x_out[t % 2], 16)
            for s in range(2):
                sp.wait_ge(x_out[s], FROM + 16 * ((TILES + 1 - s) // 2))
            sp.wait_ge(tail_out, FROM + 1)
            for g, name in ((0, "p_conv"), (1, "s_conv")):
                for j in range(2):
                    r0 = (2 * g + j) * NF
                    sp.dma_start(out[name][layer, j].rearrange("(c p) -> c p", p=P), rowbuf[r0:r0 + NF, 0:P]).then_inc(state_out, 16)
            sp.wait_ge(state_out, FROM + 64)

        def upbank(c, b, s):
            return up[2 * ((3 * c + b) % 2) + s]

        def turns(eng):
            with eng.Fori(0, NG - 1) as i:
                yield i, True
            yield NG - 1, False

        @block.scalar
        def _(act):
            s = nc.scalar

            def split_up(m, c):
                act.wait_ge(uraw_in, FROM + 32 * m + 32)
                s.activation(uhi[c][:], uraw[:], ACT.Copy).then_inc(u_hi, 1)

            def split_down(i):
                act.wait_ge(draw_in, FROM + 16 * i + 16)
                act.wait_ge(dn_ready, FROM + 18 * i)
                s.activation(dhi[:], draw[:], ACT.Copy).then_inc(d_hi, 1)

            def chunk(i, c):
                for b in range(3):
                    m = 6 * i + 3 * c + b
                    n = TB[b][1]
                    if b == 0:
                        act.wait_ge(c2_done, FROM + m)
                        act.wait_ge(tail_ready, FROM + 2 * (2 * i + c))
                        act.wait_ge(seam, FROM + 2 * i + c + 1)
                    act.wait_ge(up_ready, FROM + m + 1)
                    for g0, t0, w in gcols(b):
                        j = t0 - TB[b][0]
                        s.activation(G[:, g0:g0 + w], upbank(c, b, 0)[:, j:j + w], ACT.Copy).then_inc(g_out, 1)
                    act.wait_ge(g_out, FROM + 8 * i + 4 * c + (b + 1 if b < 2 else 4))
                    act.wait_ge(silu_done, FROM + m)
                    for g0, t0, w in gcols(b):
                        j = t0 - TB[b][0]
                        last = s.activation(cv[:, 0, j:j + w], G[:, g0 - 2:g0 - 2 + w], ACT.Identity,
                                            scale=ctap[:, c, 0:1], bias=ctap[:, c, 3:4])
                    last.then_inc(c0_done, 1)
                    act.wait_ge(c2_done, FROM + m + 1)
                    act.wait_ge(alo_done, FROM + m)
                    s.activation(cv[:, 1, 0:n], cv[:, 0, 0:n], ACT.Silu).then_inc(silu_done, 1)
                    act.wait_ge(a_done, FROM + m + 1)
                    act.wait_ge(dn_ready, FROM + 18 * i)
                    t0 = TB[b][0]
                    s.activation(ahi[:, c, t0:t0 + n], cv[:, 1, 0:n], ACT.Copy).then_inc(ahi_done, 1)

            s.preload_act_table_set("silu_and_others")
            split_up(0, 0)
            split_up(1, 1)
            split_down(0)
            act.wait_ge(tap_ready, FROM + 2)
            for i, more in turns(act):
                for c in range(2):
                    chunk(i, c)
                    if more:
                        split_up(2 * i + 2 + c, c)
                if more:
                    split_down(i + 1)
            if last_layer:
                for t in range(TILES):
                    n = queries(t)
                    act.wait_ge(dn_added, FROM + whole + 2 * t + 2)
                    s.activation(junk[0:n, :], xres[0:n, t, :], ACT.Square, scale=D ** -0.5,
                                 accum_out=stat[0:n, 0, t:t + 1]).then_inc(ssq, 1)
                    act.wait_ge(ssq, FROM + t + 1)
                    s.activation(stat[0:n, 1, t:t + 1], stat[0:n, 0, t:t + 1], ACT.Sqrt,
                                 bias=consts["eps"][0:n]).then_inc(rt, 1)

        @block.vector
        def _(dve):
            v = nc.vector

            def final(t):
                n = queries(t)
                dve.wait_ge(rt, FROM + t + 1)
                v.reciprocal(stat[0:n, 2, t:t + 1], stat[0:n, 1, t:t + 1]).then_inc(rinv, 1)
                dve.wait_ge(rinv, FROM + t + 1)
                if t >= 2:
                    dve.wait_ge(x_out[t % 2], FROM + 16 * (t // 2))
                v.scalar_tensor_tensor(y[0:n, t % 2, :], xres[0:n, t, :], stat[0:n, 2, t:t + 1], g_final[0:n, :], ALU.mult,
                                       ALU.mult).then_inc(y_ready, 1)

            def split_up(m, c):
                dve.wait_ge(u_hi, FROM + m + 1)
                v.tensor_tensor(ulo[c][:].rearrange("p s k f -> p (s k f)"), uraw[:].rearrange("p s k f -> p (s k f)"),
                                uhi[c][:].rearrange("p s k f -> p (s k f)").bitcast(F32), ALU.subtract).then_inc(u_lo, 1)

            def split_down(i):
                dve.wait_ge(d_hi, FROM + i + 1)
                v.tensor_tensor(dlo[:], draw[:], dhi[:].bitcast(F32), ALU.subtract).then_inc(d_lo, 1)

            def chunk(i, c):
                dve.wait_ge(c2_done, FROM + 6 * i + 3 * c)
                m = 2 * i + c
                v.tensor_copy(ctap[:, c, :], tap[:].rearrange("p (j c) -> p j c", j=4)[:, :, one_col(m)]).then_inc(ctap_set, 1)
                dve.wait_ge(ctap_set, FROM + m + 1)
                v.tensor_copy(G[:, SEAM:SEAM + 2], st[:].rearrange("p (j c) -> p j c", j=2)[:, :, one_col(m)]).then_inc(seam, 1)
                for b in range(3):
                    m = 6 * i + 3 * c + b
                    t0, n0 = TB[b]
                    dve.wait_ge(c0_done, FROM + m + 1)
                    for tapno, done in ((1, c1_done), (2, c2_done)):
                        if tapno == 2:
                            dve.wait_ge(c1_done, FROM + m + 1)
                        for g0, t1, w in gcols(b):
                            j = t1 - t0
                            last = v.scalar_tensor_tensor(cv[:, 0, j:j + w], G[:, g0 - 2 + tapno:g0 - 2 + tapno + w],
                                                          ctap[:, c, tapno:tapno + 1], cv[:, 0, j:j + w], ALU.mult, ALU.add)
                        last.then_inc(done, 1)
                    if b == 2:
                        for g, col in ((0, SEAM - 2), (1, CW - 2)):
                            v.tensor_copy(tail[:, 2 * g:2 * g + 2, one_col(2 * i + c)], G[:, col:col + 2]).then_inc(tail_ready, 1)
                    dve.wait_ge(silu_done, FROM + m + 1)
                    v.tensor_tensor(cv[:, 1, 0:n0], upbank(c, b, 1)[:, 0:n0], cv[:, 1, 0:n0], ALU.mult).then_inc(a_done, 1)
                    dve.wait_ge(ahi_done, FROM + m + 1)
                    v.tensor_tensor(alo[:, c, t0:t0 + n0], cv[:, 1, 0:n0], ahi[:, c, t0:t0 + n0].bitcast(F32),
                                    ALU.subtract).then_inc(alo_done, 1)

            v.memset(G[:, 0:2], 0.0).then_inc(started, 1)
            v.memset(ahi[:, :, TOK:].bitcast(F32), 0.0).then_inc(started, 1)
            v.memset(alo[:, :, TOK:].bitcast(F32), 0.0).then_inc(started, 1)
            dve.wait_ge(started, FROM + 3)
            split_up(0, 0)
            split_up(1, 1)
            split_down(0)
            for b, (dst, n) in enumerate(((tap, 4 * NF), (st, 2 * NF))):
                dve.wait_ge(tap_tp, FROM + b + 1)
                v.tensor_copy(dst[:], dn[b][:, 0:n]).then_inc(tap_ready, 1)
            dve.wait_ge(tap_ready, FROM + 2)
            for i, more in turns(dve):
                for c in range(2):
                    chunk(i, c)
                    if more and c == 0:
                        split_up(2 * i + 2, 0)
                for t in range(TILES):
                    if more and t == NT // 2:
                        split_up(2 * i + 3, 1)
                    for g in range(2):
                        j, n = 2 * t + g, queries(t)
                        dve.wait_ge(dn_ready, FROM + 18 * i + j + 1)
                        xs = xres[0:n, t, g * 512:(g + 1) * 512]
                        v.tensor_tensor(xs, dn[j % 4][0:n, :], xs, ALU.add).then_inc(dn_added, 1)
                    if last_layer and not more and t:
                        if t == 1:
                            dve.wait_ge(g_in, FROM + 16)
                        final(t - 1)
                if more:
                    split_down(i + 1)
            if last_layer:
                final(NT)
            dve.wait_ge(tail_tp, FROM + 1)
            v.tensor_copy(rowbuf[0:4 * NF, 0:P], up[0][0:4 * NF, 0:P]).then_inc(tail_out, 1)

        @block.tensor
        def _(pe):
            pe.wait_ge(tap_in, FROM + 96)
            for b, n in enumerate((4 * NF, 2 * NF)):
                nc.tensor.transpose(dn[b][:, 0:n], rowbuf[0:n, b * P:(b + 1) * P], consts["ident"][0:n, 0:n]).then_inc(tap_tp, 1)
            pe.wait_ge(tap_ready, FROM + 2)
            with pe.Fori(0, NG) as i:
                for c in range(2):
                    pe.wait_ge(u_lo, FROM + 2 * i + c + 1)
                    for b, (t0, n) in enumerate(TB):
                        if 3 * c + b >= 2:
                            pe.wait_ge(a_done, FROM + 6 * i + 3 * c + b - 1)
                        for s in range(2):
                            for k in range(KD):
                                last = three_passes(nc, upbank(c, b, s)[:, 0:n],
                                                    (uhi[c][:, s, k, :], ulo[c][:, s, k, :]),
                                                    (hT[0][:, k, t0:t0 + n], hT[1][:, k, t0:t0 + n]), k == 0, k == KD - 1)
                        last.then_inc(up_ready, 1)
                pe.wait_ge(d_lo, FROM + i + 1)
                pe.wait_ge(started, FROM + 3)
                for t in range(TILES):
                    pe.wait_ge(alo_done, FROM + 6 * i + 3 + min(2, ((t + 1) * P - 1) // 384) + 1)
                    for g in range(2):
                        j = 2 * t + g
                        pe.wait_ge(dn_added, FROM + 18 * i + max(0, j - 3))
                        for c in range(2):
                            last = three_passes(nc, dn[j % 4][:], (ahi[:, c, t * P:(t + 1) * P], alo[:, c, t * P:(t + 1) * P]),
                                                (dhi[:, c, g * 512:(g + 1) * 512], dlo[:, c, g * 512:(g + 1) * 512]), c == 0, c == 1)
                        last.then_inc(dn_ready, 1)
            pe.wait_ge(tail_ready, FROM + 2 * NF)
            nc.tensor.transpose(up[0][0:4 * NF, 0:P], tail[:].rearrange("p j c -> p (j c)"), consts["ident"][:]).then_inc(tail_tp, 1)


def hybrid_step(nc, dram, out):
    with ExitStack() as ctx:
        def sb(name, shape, dt=F32):
            return ctx.enter_context(nc.sbuf_tensor(name, shape, dt))

        ident, ident_bf = sb("ident", [P, P]), sb("ident_bf", [P, P], BF16)
        masks = {n: sb(n, [P, P], BF16) for n in ("mask_chunk", "mask_causal", "mask_strict")}
        eps = sb("eps", [P, 1])
        consts = {"ident": ident, "ident_bf": ident_bf, "eps": eps, **masks}

        with Phase(nc, "start") as ph:
            raw = ph.sb("raw", [P, 3, P])
            got, done = ph.sem("got"), ph.sem("done")
            block = ph.block()

            @block.sync
            def _(sp):
                sp.dma_start(ident[:], dram["patterns"][0]).then_inc(got, 16)
                for j in range(3):
                    sp.dma_start(raw[:, j, :], dram["patterns"][1 + j]).then_inc(got, 16)

            @block.vector
            def _(dve):
                dve.wait_ge(got, FROM + 64)
                nc.vector.tensor_copy(ident_bf[:], ident[:])
                nc.vector.memset(eps[:], EPS)
                for j, m in enumerate(("mask_chunk", "mask_causal", "mask_strict")):
                    nc.vector.tensor_scalar(masks[m][:], raw[:, j, :], NEG, None, ALU.mult)

        x0 = (dram["x_prompt"][0], dram["x_sample"][0])
        with ExitStack() as even:
            def esb(name, shape, dt=F32):
                return even.enter_context(nc.sbuf_tensor(name, shape, dt))

            widths = [key_tile(t)[0] for t in range(TILES)]
            src = {"qaT": esb("qaT", [P, 4, TOK]), "kaT": esb("kaT", [P, KEYS]), "v": esb("va", [P, KT, P]),
                   "qiT": esb("qiT", [P, 2, TOK]), "kiT": esb("kiT", [P, KEYS]), "wi": esb("wi", [P, TILES, 8]),
                   "latT": esb("latT", [P, KEYS]), "krT": esb("krT", [96, KEYS]),
                   "bias_at": [sum(widths[:t]) for t in range(TILES)]}
            projection(nc, dram, consts, "even", x0, dram["g_mix"][0], dram["w_in_even"][0], src, out)
            src["bias"] = esb("bias", [P, sum(widths)], BF16)
            src["work"] = {t: esb(f"scores{t}", [P, widths[t]]) for t in sorted(sum(TOPK_TILES, ()))}
            index_scores(nc, dram, consts, src)
            attention(nc, dram, consts, "b", src)
            attention(nc, dram, consts, "a", src)

        with ExitStack() as ff:
            xres = ff.enter_context(nc.sbuf_tensor("xres", [P, TILES, D], F32))
            hT = [ff.enter_context(nc.sbuf_tensor(f"hT{j}", [P, KD, TOK], F32R)) for j in range(2)]
            output_projection(nc, dram, consts, 0, dram["w_o_even"][0], x0, xres, hT)
            x1 = (dram["x1"][0:SEQ], dram["x1"][SEQ:TOK])
            conv_ffn(nc, dram, consts, 0, xres, hT, out, x1)

        for kind, c0, w in (("c", 0, C_IN), ("d", C_IN, D_IN)):
            with ExitStack() as odd:
                def osb(name, shape, dt=F32):
                    return odd.enter_context(nc.sbuf_tensor(f"{kind}_{name}", shape, dt))

                src = {"qT": osb("qT", [P, 4, TOK]), "kT": osb("kT", [P, 4, KEYS]), "v": osb("v", [P, KT, 512])}
                if kind == "c":
                    src["fc"] = osb("fc", [P, KT, 8])
                projection(nc, dram, consts, kind, x1, dram["g_mix"][1], dram["w_in_odd"][0][:, c0:c0 + w], src, out)
                if kind == "c":
                    src.update(fq=osb("fq", [P, TILES * P], F32R), fk_all=osb("fk_all", [P, KEYS]), onehot=osb("onehot", [P, 8]))
                    forget(nc, dram, consts, src["fc"], src, out)
                attention(nc, dram, consts, kind, src)

        with ExitStack() as ff:
            xres = ff.enter_context(nc.sbuf_tensor("xres_1", [P, TILES, D], F32))
            hT = [ff.enter_context(nc.sbuf_tensor(f"hT{j}_1", [P, KD, TOK], F32R)) for j in range(2)]
            output_projection(nc, dram, consts, 1, dram["w_o_odd"][0], x1, xres, hT)
            conv_ffn(nc, dram, consts, 1, xres, hT, out, None)


_INS = ["x_prompt", "x_sample", "cache_a_k", "cache_a_v", "cache_a_idx_k", "cache_b_latent", "cache_b_rope",
        "cache_c_k", "cache_c_v", "cache_c_logf", "cache_d_k", "cache_d_v", "state_ffn_conv",
        "g_mix", "g_ffn", "g_final", "w_in_even", "g_b_q", "g_b_kv", "w_b_uq", "w_b_ukv", "w_o_even",
        "w_in_odd", "b_forget", "w_o_odd", "w_up", "w_conv", "b_conv", "w_down"]
_OUTS = [("y_prompt", (1, SEQ, D), (SEQ, D)), ("y_sample", (1, DEC, D), (DEC, D))] + [
    (f"{g}_{name}", (1, 1, n) + shape, (n, flat)) if name != "conv" else (f"{g}_conv", (2, 1, 2, FF), (2, 2, FF))
    for g, n in (("p", SEQ), ("s", DEC))
    for name, shape, flat in (("a_k", (2, 64), 128), ("a_v", (2, 64), 128), ("a_idx_k", (32,), 32),
                              ("b_latent", (KVR,), KVR), ("b_rope", (32,), 32), ("c_k", (8, 64), 512),
                              ("c_v", (8, 64), 512), ("c_logf", (8,), 8), ("d_k", (8, 64), 512),
                              ("d_v", (8, 64), 512), ("conv", (), 0))]


def _constants():
    import numpy as np

    f = np.float32
    pos = np.concatenate([np.arange(SEQ), PAST + np.arange(DEC), np.zeros(P - DEC)]).astype(f)
    tabs = []
    for n_rot in (16, 8, 32):
        half = n_rot // 2
        inv = f(500000.0) ** (-np.arange(half, dtype=f) * f(2.0) / f(n_rot))
        ang = pos[:, None] * inv.astype(f)[None, :]
        tabs += [np.cos(ang), np.sin(ang)]
    trig = np.concatenate(tabs, axis=1).astype(f).reshape(TILES, P, ROPE_COLS)
    i = np.arange(P)
    hidden = [np.eye(P), (i[:, None] < P // 2) & (i[None, :] >= P // 2), i[None, :] > i[:, None], i[None, :] >= i[:, None]]
    return {"trig": trig, "patterns": np.stack(hidden).astype(f)}


def kernel(**inputs):
    import numpy as _np
    import concourse.bacc as _bacc
    from concourse import mybir as _mybir
    from concourse.bass_utils import run_bass_kernel_spmd as _run

    nc = _bacc.Bacc("TRN2", target_bir_lowering=False, num_devices=1)
    arrays, dram, out = {}, {}, {}
    for name, a in [(n, _np.ascontiguousarray(inputs[n])) for n in _INS] + list(_constants().items()):
        arrays[f"in_{name}_dram"] = a
        dram[name] = nc.dram_tensor(f"in_{name}_dram", a.shape, _mybir.dt.from_np(a.dtype), kind="ExternalInput").ap()
    for name, shape, flat in _OUTS:
        out[name] = nc.dram_tensor(f"out_{name}_dram", flat, F32, kind="ExternalOutput").ap()
    for name, shape in (("qbT", (8, 96, TOK)), ("att", (TOK, D)), ("x1", (TOK, D))):
        dram[name] = nc.dram_tensor(f"scratch_{name}", shape, F32, kind="Internal").ap()
    hybrid_step(nc, dram, out)
    r = _run(nc, [arrays], core_ids=[0])
    return tuple(r.results[0][f"out_{name}_dram"].reshape(shape) for name, shape, flat in _OUTS)
```
